# Optimizing a Trainium2 kernel written in Bass

```python
import math
import jax, jax.numpy as jnp
from jax import lax
import numpy as np

D_MODEL = 1024
BATCH = 1
SEQ = 128
DEPTH = 2
DEC_BATCH = 1
DEC_SEQ = 512
PAST_LEN = 128

GRID_W = 64
N_EVEN = (DEPTH + 1) // 2
N_ODD = DEPTH // 2
ADA_CHUNKS = 6
EPS = 1e-6
HY_WIDTH = D_MODEL // 2
HY_ORDER = 2
HY_BANDS = 16
HY_EMB = 1 + 2 * HY_BANDS
HY_FFN = 64
S5_WIDTH = D_MODEL // 2
S5_CH = 16
S5_GROUPS = S5_WIDTH // S5_CH
S5_P = 64
ML_WIDTH = D_MODEL
ML_HEADS = 8
ML_DH = ML_WIDTH // ML_HEADS
ML_CHUNK = 128
PK_HEADS = 8
PK_DQ = 256
PK_HALF = PK_DQ // 2
N_KEYS = 128
N_EXPERTS = N_KEYS * N_KEYS
PK_TOPK = 16
PEER_BLOCK = 128

kernel_name = 'hyena_s5_mlstm_peer_diffusion_step'

def _f(a):
    return a.astype(jnp.float32)

def rmsnorm(x, g):
    x32 = _f(x)
    y = x32 * lax.rsqrt(jnp.mean(x32 * x32, axis=-1, keepdims=True) + EPS)
    return (y * _f(g)).astype(x.dtype)

def short_conv(x, w, b):
    xp = jnp.pad(x, ((0, 0), (1, 1), (0, 0)))
    return xp[:, :-2] * w[0] + xp[:, 1:-1] * w[1] + xp[:, 2:] * w[2] + b

def grid_pos_embed(n_tok, dtype):
    rows = n_tok // GRID_W
    quarter = D_MODEL // 4
    omega = 1.0 / (10000.0 ** (jnp.arange(quarter, dtype=jnp.float32) / quarter))
    def emb1d(pos):
        ang = pos.astype(jnp.float32)[:, None] * omega[None]
        return jnp.concatenate([jnp.sin(ang), jnp.cos(ang)], axis=-1)
    er = emb1d(jnp.arange(rows))
    ec = emb1d(jnp.arange(GRID_W))
    half = D_MODEL // 2
    pe = jnp.concatenate([jnp.broadcast_to(er[:, None], (rows, GRID_W, half)),
                          jnp.broadcast_to(ec[None], (rows, GRID_W, half))], axis=-1)
    return pe.reshape(rows * GRID_W, D_MODEL).astype(dtype)

def hyena_filters(n_tok, w1, b1, w2, b2, w3, freq, decay):
    pos = jnp.arange(n_tok, dtype=jnp.float32)
    t = pos / n_tok
    bands = jnp.linspace(1e-4, HY_BANDS - 1, HY_BANDS, dtype=jnp.float32)
    ang = 2.0 * math.pi * t[:, None] * bands[None]
    z = jnp.concatenate([t[:, None], jnp.cos(ang), jnp.sin(ang)], axis=-1)
    fr = _f(freq)
    h = jnp.sin(fr * (z @ _f(w1) + _f(b1)))
    h = jnp.sin(fr * (h @ _f(w2) + _f(b2)))
    h = (h @ _f(w3)) * jnp.exp(-t[:, None] * jnp.abs(_f(decay)))
    h = h.reshape(n_tok, HY_ORDER, 2, HY_WIDTH)
    fwd, bwd = h[:, :, 0], h[:, :, 1]
    kern = jnp.concatenate([fwd, jnp.zeros_like(fwd[:1]), bwd[1:][::-1]], axis=0)
    kern = kern * lax.rsqrt(jnp.sum(kern * kern, axis=0, keepdims=True) + EPS)
    return jnp.fft.rfft(kern, axis=0)

def hyena_mix(u, kf, bias):
    n_tok = u.shape[1]
    v, g1, g2 = jnp.split(_f(u), 3, axis=-1)
    gates = (g1, g2)
    z = v
    for o in range(HY_ORDER):
        zf = jnp.fft.rfft(z, n=2 * n_tok, axis=1)
        conv = jnp.fft.irfft(zf * kf[None, :, o], n=2 * n_tok, axis=1)[:, :n_tok]
        z = gates[o] * (conv + bias[o] * z)
    return z

def _lin_rec(e1, e2):
    a1, b1 = e1
    a2, b2 = e2
    return a1 * a2, a2 * b1 + b2

def s5_scan(u, lam_bar, b_bar, c_mat, h0):
    bu = jnp.einsum('gpj,blgj->blgp', b_bar, u.astype(jnp.complex64))
    bu = bu.at[:, 0].add(lam_bar[None] * h0)
    a = jnp.broadcast_to(lam_bar, bu.shape)
    _, hs = lax.associative_scan(_lin_rec, (a, bu), axis=1)
    y = jnp.einsum('gjp,blgp->blgj', c_mat, hs).real
    return y, hs[:, -1]

def s5_mix(u, h0_re, h0_im, a_re, a_im, b_re, b_im, c_re, c_im, log_step, d_skip, glu_w, glu_b):
    bsz, n_tok, _ = u.shape
    u = _f(u).reshape(bsz, n_tok, S5_GROUPS, S5_CH)
    lam = lax.complex(_f(a_re), _f(a_im))
    lam_bar = jnp.exp(lam * jnp.exp(_f(log_step))[..., None])
    b_bar = ((lam_bar - 1.0) / lam)[..., None] * lax.complex(_f(b_re), _f(b_im))
    c_mat = lax.complex(_f(c_re), _f(c_im))
    h0 = lax.complex(_f(h0_re), _f(h0_im))
    y_f, hf = s5_scan(u, lam_bar[0], b_bar[0], c_mat[0], h0[:, 0])
    y_b, hb = s5_scan(u[:, ::-1], lam_bar[1], b_bar[1], c_mat[1], h0[:, 1])
    u_flat = u.reshape(bsz, n_tok, S5_WIDTH)
    y = (y_f + y_b[:, ::-1]).reshape(bsz, n_tok, S5_WIDTH) + _f(d_skip) * u_flat
    y = jax.nn.gelu(y)
    y = y * jax.nn.sigmoid(y @ _f(glu_w) + _f(glu_b))
    h_fin = jnp.stack([hf, hb], axis=1)
    return y, h_fin.real, h_fin.imag

def mlstm_scan(q, k, v, ig, lf, c0, n0, m0):
    bsz, nh, n_tok, dh = q.shape
    nc = n_tok // ML_CHUNK
    def chunks(a):
        return jnp.moveaxis(a.reshape(bsz, nh, nc, ML_CHUNK, *a.shape[3:]), 2, 0)
    causal = jnp.tril(jnp.ones((ML_CHUNK, ML_CHUNK), dtype=bool))
    def step(carry, xs):
        cm, nv, m = carry
        qc, kc, vc, ic, fc = xs
        b = jnp.cumsum(fc, axis=-1)
        a = b + m[..., None]
        dmat = jnp.where(causal, b[..., :, None] - b[..., None, :] + ic[..., None, :], -jnp.inf)
        mq = jnp.maximum(a, jnp.max(dmat, axis=-1))
        w_intra = jnp.exp(dmat - mq[..., None])
        w_inter = jnp.exp(a - mq)
        s = jnp.einsum('bhtd,bhsd->bhts', qc, kc) * w_intra
        num = jnp.einsum('bhts,bhsv->bhtv', s, vc) + w_inter[..., None] * jnp.einsum('bhtk,bhkv->bhtv', qc, cm)
        den = jnp.sum(s, axis=-1) + w_inter * jnp.einsum('bhtk,bhk->bht', qc, nv)
        h = num / jnp.maximum(jnp.abs(den), jnp.exp(-mq))[..., None]
        b_last = b[..., -1]
        g = b_last[..., None] - b + ic
        m_new = jnp.maximum(b_last + m, jnp.max(g, axis=-1))
        w_s = jnp.exp(g - m_new[..., None])
        keep = jnp.exp(b_last + m - m_new)
        cm_new = keep[..., None, None] * cm + jnp.einsum('bhs,bhsk,bhsv->bhkv', w_s, kc, vc)
        nv_new = keep[..., None] * nv + jnp.einsum('bhs,bhsk->bhk', w_s, kc)
        return (cm_new, nv_new, m_new), h
    (cm, nv, m), hs = lax.scan(step, (c0, n0, m0), (chunks(q), chunks(k), chunks(v), chunks(ig), chunks(lf)))
    h = jnp.moveaxis(hs, 0, 2).reshape(bsz, nh, n_tok, dh)
    return h, cm, nv, m

def mlstm_mix(hn, c0, n0, m0, w_in, gate_b, conv_w, conv_b, norm_g, w_out):
    bsz, n_tok, _ = hn.shape
    proj = _f(hn @ w_in)
    qk_raw, v, o, gates = jnp.split(proj, [2 * ML_WIDTH, 3 * ML_WIDTH, 4 * ML_WIDTH], axis=-1)
    qk = jax.nn.silu(short_conv(qk_raw, _f(conv_w), _f(conv_b)))
    q, k = jnp.split(qk, 2, axis=-1)
    def heads(a):
        return a.reshape(bsz, n_tok, ML_HEADS, ML_DH).transpose(0, 2, 1, 3)
    q = heads(q) * (ML_DH ** -0.5)
    k = heads(k)
    vh = heads(v)
    gates = (gates.reshape(bsz, n_tok, 4, ML_HEADS) + _f(gate_b)).transpose(2, 0, 3, 1)
    ig_f, ig_b = gates[0], gates[1]
    lf_f, lf_b = jax.nn.log_sigmoid(gates[2]), jax.nn.log_sigmoid(gates[3])
    c0, n0, m0 = _f(c0), _f(n0), _f(m0)
    h_f, cf, nf, mf = mlstm_scan(q, k, vh, ig_f, lf_f, c0[:, 0], n0[:, 0], m0[:, 0])
    def rev(a):
        return jnp.flip(a, axis=2)
    h_b, cb, nb, mb = mlstm_scan(rev(q), rev(k), rev(vh), rev(ig_b), rev(lf_b), c0[:, 1], n0[:, 1], m0[:, 1])
    h = h_f + rev(h_b)
    h = h * lax.rsqrt(jnp.mean(h * h, axis=-1, keepdims=True) + EPS)
    h = h.transpose(0, 2, 1, 3).reshape(bsz, n_tok, ML_WIDTH) * _f(norm_g)
    out = (h * jax.nn.silu(o)).astype(hn.dtype) @ w_out
    return out, jnp.stack([cf, cb], 1), jnp.stack([nf, nb], 1), jnp.stack([mf, mb], 1)

def peer(x, w_q, keys, u_tab, v_tab):
    bsz, n_tok, _ = x.shape
    n = bsz * n_tok
    xt = x.reshape(n, D_MODEL)
    q = _f(xt @ w_q).reshape(n, PK_HEADS, 2, PK_HALF)
    s = jnp.einsum('thcd,hcnd->thcn', q, _f(keys))
    sv, si = lax.top_k(s, PK_TOPK)
    cand = (sv[:, :, 0, :, None] + sv[:, :, 1, None, :]).reshape(n, PK_HEADS, PK_TOPK * PK_TOPK)
    best, bi = lax.top_k(cand, PK_TOPK)
    i1 = jnp.take_along_axis(si[:, :, 0], bi // PK_TOPK, axis=-1)
    i2 = jnp.take_along_axis(si[:, :, 1], bi % PK_TOPK, axis=-1)
    nblk = n // PEER_BLOCK
    eidx = (i1 * N_KEYS + i2).reshape(nblk, PEER_BLOCK, PK_HEADS * PK_TOPK)
    gate = jax.nn.softmax(best, axis=-1).reshape(nblk, PEER_BLOCK, PK_HEADS * PK_TOPK)
    xb = xt.reshape(nblk, PEER_BLOCK, D_MODEL)
    def block(args):
        xi, ei, gi = args
        act = jax.nn.gelu(_f(jnp.einsum('td,ted->te', xi, u_tab[ei]))) * gi
        return jnp.einsum('te,ted->td', act.astype(xi.dtype), v_tab[ei])
    out = lax.map(block, (xb, eidx, gate))
    return out.reshape(bsz, n_tok, D_MODEL).astype(x.dtype)

def even_mixer(h, s5_re0, s5_im0, p, i):
    n_tok = h.shape[1]
    proj = h @ p['ev_w_in'][i]
    hy_in = short_conv(proj[..., :3 * HY_WIDTH], p['hy_conv_w'][i], p['hy_conv_b'][i])
    kf = hyena_filters(n_tok, p['hy_w1'][i], p['hy_b1'][i], p['hy_w2'][i], p['hy_b2'][i],
                       p['hy_w3'][i], p['hy_freq'][i], p['hy_decay'][i])
    hy_out = hyena_mix(hy_in, kf, _f(p['hy_bias'][i]))
    s5_out, s_re, s_im = s5_mix(proj[..., 3 * HY_WIDTH:], s5_re0, s5_im0,
                                p['s5_a_re'][i], p['s5_a_im'][i], p['s5_b_re'][i], p['s5_b_im'][i],
                                p['s5_c_re'][i], p['s5_c_im'][i], p['s5_log_step'][i], p['s5_d'][i],
                                p['s5_glu_w'][i], p['s5_glu_b'][i])
    out = jnp.concatenate([hy_out, s5_out], axis=-1).astype(h.dtype) @ p['ev_w_out'][i]
    return out, s_re, s_im

def odd_mixer(h, c0, n0, m0, p, i):
    return mlstm_mix(h, c0, n0, m0, p['od_w_in'][i], p['od_gate_b'][i], p['ml_conv_w'][i],
                     p['ml_conv_b'][i], p['ml_norm_g'][i], p['od_w_out'][i])

def trunk(x, cond, s5_re0, s5_im0, ml_c0, ml_n0, ml_m0, p):
    s5_re, s5_im, ml_c, ml_n, ml_m = [], [], [], [], []
    for l in range(DEPTH):
        mod = jax.nn.silu(_f(cond)) @ _f(p['ada_w'][l]) + _f(p['ada_b'][l])
        sh1, sc1, g1, sh2, sc2, g2 = jnp.split(mod[:, None, :].astype(x.dtype), ADA_CHUNKS, axis=-1)
        h = rmsnorm(x, p['norm_g'][l, 0]) * (1 + sc1) + sh1
        i = l // 2
        if l % 2 == 0:
            y, sr, si = even_mixer(h, s5_re0[:, i], s5_im0[:, i], p, i)
            s5_re.append(sr)
            s5_im.append(si)
        else:
            y, cm, nv, m = odd_mixer(h, ml_c0[:, i], ml_n0[:, i], ml_m0[:, i], p, i)
            ml_c.append(cm)
            ml_n.append(nv)
            ml_m.append(m)
        x = x + g1 * y
        h = rmsnorm(x, p['norm_g'][l, 1]) * (1 + sc2) + sh2
        x = x + g2 * peer(h, p['pk_w_q'][l], p['pk_keys'][l], p['pk_u'][l], p['pk_v'][l])
    y = rmsnorm(x, p['final_g'])
    return (y, jnp.stack(s5_re, 1), jnp.stack(s5_im, 1), jnp.stack(ml_c, 1), jnp.stack(ml_n, 1), jnp.stack(ml_m, 1))

def setup_inputs(seed: int = 0) -> dict:
    key = jax.random.key(seed)
    ks = iter(list(jax.random.split(key, 64)))
    f32 = jnp.float32
    def nrm(shape, scale):
        return jax.random.normal(next(ks), shape, f32) * scale
    def unif(shape, lo, hi):
        return jax.random.uniform(next(ks), shape, f32, lo, hi)
    d = D_MODEL
    ne, no = N_EVEN, N_ODD
    hy_decay0 = jnp.linspace(math.log(100.0) / 1.5, math.log(100.0) / 0.3, 4 * HY_WIDTH, dtype=f32)
    fgate0 = jnp.linspace(3.0, 6.0, ML_HEADS, dtype=f32)
    return {
        'x_prompt': nrm((BATCH, SEQ, d), 1.0),
        'x_sample': nrm((DEC_BATCH, DEC_SEQ, d), 1.0),
        'state_s5_re': nrm((DEC_BATCH, ne, 2, S5_GROUPS, S5_P), 0.1),
        'state_s5_im': nrm((DEC_BATCH, ne, 2, S5_GROUPS, S5_P), 0.1),
        'state_mlstm_C': nrm((DEC_BATCH, no, 2, ML_HEADS, ML_DH, ML_DH), 0.3),
        'state_mlstm_n': nrm((DEC_BATCH, no, 2, ML_HEADS, ML_DH), 0.3),
        'state_mlstm_m': unif((DEC_BATCH, no, 2, ML_HEADS), 0.0, 3.0),
        'c': nrm((DEC_BATCH, d), 1.0),
        'c_ctx': nrm((d,), 1.0),
        'norm_g': 1.0 + nrm((DEPTH, 2, d), 0.02),
        'ada_w': nrm((DEPTH, d, ADA_CHUNKS * d), 0.5 * d ** -0.5),
        'ada_b': nrm((DEPTH, ADA_CHUNKS * d), 0.02),
        'final_g': 1.0 + nrm((d,), 0.02),
        'ev_w_in': nrm((ne, d, 3 * HY_WIDTH + S5_WIDTH), d ** -0.5),
        'hy_conv_w': nrm((ne, 3, 3 * HY_WIDTH), 3 ** -0.5),
        'hy_conv_b': nrm((ne, 3 * HY_WIDTH), 0.02),
        'hy_w1': nrm((ne, HY_EMB, HY_FFN), HY_EMB ** -0.5),
        'hy_b1': nrm((ne, HY_FFN), 0.1),
        'hy_w2': nrm((ne, HY_FFN, HY_FFN), HY_FFN ** -0.5),
        'hy_b2': nrm((ne, HY_FFN), 0.1),
        'hy_w3': nrm((ne, HY_FFN, 4 * HY_WIDTH), HY_FFN ** -0.5),
        'hy_freq': 1.0 + nrm((ne, HY_FFN), 0.1),
        'hy_decay': hy_decay0[None] + nrm((ne, 4 * HY_WIDTH), 0.1),
        'hy_bias': nrm((ne, HY_ORDER, HY_WIDTH), 0.1),
        's5_a_re': -0.5 + nrm((ne, 2, S5_GROUPS, S5_P), 0.01),
        's5_a_im': math.pi * jnp.arange(S5_P, dtype=f32) + nrm((ne, 2, S5_GROUPS, S5_P), 0.01),
        's5_b_re': nrm((ne, 2, S5_GROUPS, S5_P, S5_CH), (2 * S5_CH) ** -0.5),
        's5_b_im': nrm((ne, 2, S5_GROUPS, S5_P, S5_CH), (2 * S5_CH) ** -0.5),
        's5_c_re': nrm((ne, 2, S5_GROUPS, S5_CH, S5_P), S5_P ** -0.5),
        's5_c_im': nrm((ne, 2, S5_GROUPS, S5_CH, S5_P), S5_P ** -0.5),
        's5_log_step': unif((ne, 2, S5_GROUPS), math.log(1e-3), math.log(1e-1)),
        's5_d': nrm((ne, S5_WIDTH), 1.0),
        's5_glu_w': nrm((ne, S5_WIDTH, S5_WIDTH), S5_WIDTH ** -0.5),
        's5_glu_b': nrm((ne, S5_WIDTH), 0.02),
        'ev_w_out': nrm((ne, HY_WIDTH + S5_WIDTH, d), (HY_WIDTH + S5_WIDTH) ** -0.5),
        'od_w_in': nrm((no, d, 4 * ML_WIDTH + 4 * ML_HEADS), d ** -0.5),
        'od_gate_b': jnp.concatenate([nrm((no, 2, ML_HEADS), 0.1),
                                      fgate0[None, None] + nrm((no, 2, ML_HEADS), 0.1)], axis=1),
        'ml_conv_w': nrm((no, 3, 2 * ML_WIDTH), 3 ** -0.5),
        'ml_conv_b': nrm((no, 2 * ML_WIDTH), 0.02),
        'ml_norm_g': 1.0 + nrm((no, ML_WIDTH), 0.02),
        'od_w_out': nrm((no, ML_WIDTH, d), ML_WIDTH ** -0.5),
        'pk_w_q': nrm((DEPTH, d, PK_HEADS * PK_DQ), d ** -0.5),
        'pk_keys': nrm((DEPTH, PK_HEADS, 2, N_KEYS, PK_HALF), PK_HALF ** -0.5),
        'pk_u': nrm((DEPTH, N_EXPERTS, d), d ** -0.5),
        'pk_v': nrm((DEPTH, N_EXPERTS, d), PK_HEADS ** -0.5),
    }

def reference(x_prompt, x_sample, state_s5_re, state_s5_im, state_mlstm_C, state_mlstm_n, state_mlstm_m,
              c, c_ctx, norm_g, ada_w, ada_b, final_g, ev_w_in, hy_conv_w, hy_conv_b, hy_w1, hy_b1, hy_w2,
              hy_b2, hy_w3, hy_freq, hy_decay, hy_bias, s5_a_re, s5_a_im, s5_b_re, s5_b_im, s5_c_re, s5_c_im,
              s5_log_step, s5_d, s5_glu_w, s5_glu_b, ev_w_out, od_w_in, od_gate_b, ml_conv_w, ml_conv_b,
              ml_norm_g, od_w_out, pk_w_q, pk_keys, pk_u, pk_v):
    p = dict(norm_g=norm_g, ada_w=ada_w, ada_b=ada_b, final_g=final_g, ev_w_in=ev_w_in,
             hy_conv_w=hy_conv_w, hy_conv_b=hy_conv_b, hy_w1=hy_w1, hy_b1=hy_b1, hy_w2=hy_w2, hy_b2=hy_b2,
             hy_w3=hy_w3, hy_freq=hy_freq, hy_decay=hy_decay, hy_bias=hy_bias, s5_a_re=s5_a_re,
             s5_a_im=s5_a_im, s5_b_re=s5_b_re, s5_b_im=s5_b_im, s5_c_re=s5_c_re, s5_c_im=s5_c_im,
             s5_log_step=s5_log_step, s5_d=s5_d, s5_glu_w=s5_glu_w, s5_glu_b=s5_glu_b, ev_w_out=ev_w_out,
             od_w_in=od_w_in, od_gate_b=od_gate_b, ml_conv_w=ml_conv_w, ml_conv_b=ml_conv_b,
             ml_norm_g=ml_norm_g, od_w_out=od_w_out, pk_w_q=pk_w_q, pk_keys=pk_keys, pk_u=pk_u, pk_v=pk_v)
    f32 = jnp.float32
    nb = x_prompt.shape[0]
    z_s5 = jnp.zeros((nb, N_EVEN, 2, S5_GROUPS, S5_P), f32)
    z_c = jnp.zeros((nb, N_ODD, 2, ML_HEADS, ML_DH, ML_DH), f32)
    z_n = jnp.zeros((nb, N_ODD, 2, ML_HEADS, ML_DH), f32)
    z_m = jnp.zeros((nb, N_ODD, 2, ML_HEADS), f32)
    y_prompt, new_s5_re, new_s5_im, new_mlstm_C, new_mlstm_n, new_mlstm_m = trunk(
        x_prompt, c_ctx[None], z_s5, z_s5, z_c, z_n, z_m, p)
    x_lat = x_sample + grid_pos_embed(x_sample.shape[1], x_sample.dtype)
    y_sample = trunk(x_lat, c, state_s5_re, state_s5_im, state_mlstm_C, state_mlstm_n, state_mlstm_m, p)[0]
    return (y_prompt, y_sample, new_s5_re, new_s5_im, new_mlstm_C, new_mlstm_n, new_mlstm_m)


_drawn_inputs = setup_inputs


def setup_inputs(seed=0):
    import zlib

    import numpy as np

    out = dict(_drawn_inputs(seed))
    spreads = {}
    factors = {'state_s5_re': 8.0,
     'state_s5_im': 8.0,
     'state_mlstm_C': 4.411,
     'state_mlstm_n': 8.0,
     'state_mlstm_m': 8.0,
     'final_g': 22.452,
     's5_a_re': 81.612,
     's5_c_re': 4.569,
     's5_c_im': 5.115,
     's5_glu_b': 30.853,
     'ml_norm_g': 68.346}
    for name, (base, spread) in spreads.items():
        noise = np.random.default_rng([zlib.crc32(name.encode()), seed]).standard_normal(out[name].shape)
        drawn = base * np.exp(spread * noise) if base else spread * noise
        out[name] = __import__('jax').numpy.asarray(drawn.astype(out[name].dtype))
    for name, factor in factors.items():
        out[name] = (out[name] * factor).astype(out[name].dtype)
    return out
```

```python
import math
from contextlib import ExitStack, contextmanager

import numpy as np

import concourse.bass as bass
from concourse import mybir

F32 = mybir.dt.float32
U32 = mybir.dt.uint32
I32 = mybir.dt.int32
ALU = mybir.AluOpType
ACT = mybir.ActivationFunctionType
AX = mybir.AxisListType

P = 128
D = 1024
KD = D // P
CTX = 128
LAT = 512
TOK = CTX + LAT
NT = TOK // P
GROUPS = ((0, CTX), (CTX, TOK))
EPS = 1e-6
HALF = 512
TWO_PI = 2.0 * math.pi
PI_BELOW = 3.1415925
ROUND = 1.5 * 2.0 ** 23


def group_of(tile):
    return 0 if tile == 0 else 1


def wait_apart(eng, sem, count, mark):
    eng.wait_ge(sem, count)
    eng.sem_inc(mark, 1)


class Line:

    def __init__(self, eng, sem):
        self.eng, self.sem, self.n, self.at = eng, sem, 0, 0

    def then(self, ins, mark=None):
        self.n += 1
        ins.then_inc(self.sem, 1)
        if mark is None:
            self.eng.wait_ge(self.sem, self.at + self.n)
        else:
            wait_apart(self.eng, self.sem, self.at + self.n, mark)

    @contextmanager
    def loop(self, start, stop, per):
        before, was = self.n, self.at
        assert isinstance(was, int)
        with self.eng.Fori(start, stop) as i:
            self.at, self.n = was + before + (i - start) * per, 0
            yield i
            assert self.n == per, (self.n, per)
        self.at, self.n = was + before + (stop - start) * per, 0


USED = {}


def numbered(name):
    USED[name] = USED.get(name, -1) + 1
    return f"{name}_{USED[name]}"


@contextmanager
def stage(nc, *names):
    sems = [nc.alloc_semaphore(numbered(n)) for n in names]
    with ExitStack() as ctx:
        yield ctx, sems
    nc.clear_and_free_semaphores(sems)
    nc.all_engine_barrier()


def buf(ctx, nc, name, shape, dt=F32):
    return ctx.enter_context(nc.sbuf_tensor(numbered(name), shape, dt))


def load_and_modulate(nc, T, ps, X, ident, mod):
    blocks = 2 * 6 * D // HALF
    with stage(nc, "cond_in", "x_in", "w_in0", "w_in1", "cond_ready", "w_used", "rows_added",
               "mod_out", "dve_line", "ident0") as (
            ctx, (cond_in, x_in, w_in0, w_in1, cond_ready, w_used, rows_added, mod_out, dve_line,
                  ident0)):
        w_in = (w_in0, w_in1)
        cond = buf(ctx, nc, "cond", [P, KD, 2])
        cond_s = buf(ctx, nc, "cond_s", [P, KD, 2])
        w = buf(ctx, nc, "ada_block", [P, 2, KD * HALF])
        rows = buf(ctx, nc, "mod_rows", [2, blocks * HALF])
        pos = buf(ctx, nc, "pos", [P, NT - 1, D])
        block = ctx.enter_context(nc.Block())

        @block.sync
        def _(sp):
            sp.dma_start(cond[:], T["cond"]).then_inc(cond_in, 16)
            for b in range(2):
                sp.dma_start(w[:, b, :], T["ada_w"][b]).then_inc(w_in[b], 16)
            with sp.Fori(1, blocks // 2) as i:
                for b in range(2):
                    sp.wait_ge(w_used, 2 * i + (b - 1))
                    sp.dma_start(w[:, b, :], T["ada_w"][2 * i + b]).then_inc(w_in[b], 16)
            sp.wait_ge(rows_added, blocks)
            sp.dma_start(mod.rearrange("l g n -> g l n"),
                         rows[:, :].rearrange("g (l n) -> g l n", l=2)).then_inc(mod_out, 16)
            sp.wait_ge(mod_out, 16)

        @block.gpsimd
        def _(pool):
            pool.memset(ident[:], 0.0).then_inc(ident0, 1)
            pool.wait_ge(ident0, 1)
            pool.affine_select(out=ident[:], in_=ident[:], compare_op=ALU.not_equal, fill=1.0,
                               base=0, pattern=[[-1, P]], channel_multiplier=1).then_inc(ident0, 1)
            pool.wait_ge(ident0, 2)

        @block.scalar
        def _(act):
            for g in range(2):
                act.dma_start(rows[g:g + 1, :], T["ada_b"]).then_inc(x_in, 16)
            act.dma_start(X[:], T["x"]).then_inc(x_in, 16)
            act.dma_start(pos[:], T["pos"]).then_inc(x_in, 16)
            act.wait_ge(cond_in, 16)
            act.activation(cond_s[:], cond[:], ACT.Silu).then_inc(cond_ready, 1)

        @block.tensor
        def _(pe):
            pe.wait_ge(cond_ready, 1)

            def products(b):
                for k in range(KD):
                    mm = pe.matmul(ps[0:2, b * HALF:(b + 1) * HALF], cond_s[:, k, :], w[:, b, k * HALF:(k + 1) * HALF],
                                   start=(k == 0), stop=(k == KD - 1))
                mm.then_inc(w_used, 1)

            for b in range(2):
                pe.wait_ge(w_in[b], 16)
                products(b)
            with pe.Fori(1, blocks // 2) as i:
                for b in range(2):
                    pe.wait_ge(w_in[b], 16 * i + 16)
                    pe.wait_ge(rows_added, 2 * i + (b - 1))
                    products(b)

        @block.vector
        def _(dve):
            dve.wait_ge(x_in, 64)
            with dve.Fori(0, blocks // 2) as i:
                for b in range(2):
                    dve.wait_ge(w_used, 2 * i + (b + 1))
                    r = rows[:, bass.ds(i * (2 * HALF) + b * HALF, HALF)]
                    dve.tensor_tensor(r, r, ps[0:2, b * HALF:(b + 1) * HALF], ALU.add).then_inc(rows_added, 1)
            line = Line(dve, dve_line)
            line.then(dve.tensor_tensor(X[:, 1:NT, :], X[:, 1:NT, :], pos[:], ALU.add))


def norm_modulate(nc, ps, X, H, HT, ident, mod, gain, layer, shift, scale):
    with stage(nc, "rows_in", "squared", "rooted", "dve_line", "h_ready", "turned",
               "copied") as (ctx, (rows_in, squared, rooted, dve_line, h_ready, turned, copied)):
        g_row = buf(ctx, nc, "g_row", [P, D])
        sc = buf(ctx, nc, "sc_row", [P, 2, D])
        sh = buf(ctx, nc, "sh_row", [P, 2, D])
        junk = buf(ctx, nc, "squares", [P, D])
        ss = buf(ctx, nc, "mean_square", [P, NT])
        rs = buf(ctx, nc, "root", [P, NT])
        block = ctx.enter_context(nc.Block())

        @block.sync
        def _(sp):
            sp.dma_start(g_row[:], gain.partition_broadcast(P)).then_inc(rows_in, 16)
            for g in range(2):
                for dst, c in ((sc, scale), (sh, shift)):
                    sp.dma_start(dst[:, g, :], mod[layer, g, c * D:(c + 1) * D]
                                 .partition_broadcast(P)).then_inc(rows_in, 16)

        @block.scalar
        def _(act):
            for t in range(NT):
                act.activation(junk[:], X[:, t, :], ACT.Square,
                               accum_out=ss[:, t:t + 1]).then_inc(squared, 1)
                act.wait_ge(squared, t + 1)
            act.wait_ge(dve_line, 2)
            act.activation(rs[:], ss[:], ACT.Sqrt).then_inc(rooted, 1)
            for n in range(2 * NT):
                act.wait_ge(turned, n + 1)
                t, q = n // 2, n % 2
                act.activation(HT[:, 4 * q:4 * q + 4, t * P:(t + 1) * P],
                               ps[:, (n % 4) * HALF:(n % 4 + 1) * HALF].rearrange("p (k c) -> p k c", k=4),
                               ACT.Copy).then_inc(copied, 1)

        @block.vector
        def _(dve):
            line = Line(dve, dve_line)
            dve.wait_ge(squared, NT)
            line.then(dve.tensor_scalar(ss[:], ss[:], 1.0 / D, EPS, ALU.mult, ALU.add))
            line.then(dve.reciprocal(ss[:], ss[:]))
            dve.wait_ge(rows_in, 80)
            for g in range(2):
                line.then(dve.scalar_tensor_tensor(out=sc[:, g, :], in0=sc[:, g, :], scalar=1.0,
                                                   in1=g_row[:], op0=ALU.add, op1=ALU.mult))
            dve.wait_ge(rooted, 1)
            for t in range(NT):
                g = group_of(t)
                line.then(dve.scalar_tensor_tensor(out=H[:, t, :], in0=X[:, t, :],
                                                   scalar=rs[:, t:t + 1], in1=sc[:, g, :],
                                                   op0=ALU.mult, op1=ALU.mult))
                dve.tensor_tensor(H[:, t, :], H[:, t, :], sh[:, g, :], ALU.add).then_inc(h_ready, 1)
                dve.wait_ge(h_ready, t + 1)

        @block.tensor
        def _(pe):
            for n in range(2 * NT):
                t, q = n // 2, n % 2
                if q == 0:
                    pe.wait_ge(h_ready, t + 1)
                if n >= 4:
                    pe.wait_ge(copied, n - 3)
                for k in range(4):
                    mm = pe.transpose(ps[:, (n % 4) * HALF + k * P:(n % 4) * HALF + (k + 1) * P],
                                      H[:, t, (4 * q + k) * P:(4 * q + k + 1) * P], ident[:])
                mm.then_inc(turned, 1)


def project_channels(nc, ps, HT, W, OUT, blocks, width=P):
    with stage(nc, "w_in0", "w_in1", "used", "lat_out", "ctx_out") as (
            ctx, (w_in0, w_in1, used, lat_out, ctx_out)):
        w_in = (w_in0, w_in1)
        w = buf(ctx, nc, "w_block", [P, 2, KD * width])
        block = ctx.enter_context(nc.Block())

        @block.sync
        def _(sp):
            for b in range(2):
                sp.dma_start(w[:, b, :], W[b]).then_inc(w_in[b], 16)
            with sp.Fori(1, blocks // 2) as i:
                for b in range(2):
                    sp.wait_ge(used, 2 * i + (b - 1))
                    sp.dma_start(w[:, b, :], W[2 * i + b]).then_inc(w_in[b], 16)

        @block.tensor
        def _(pe):
            def products(b):
                for k in range(KD):
                    lhs = w[:, b, k * width:(k + 1) * width]
                    pe.matmul(ps[0:width, 2 * b * HALF:2 * b * HALF + LAT], lhs, HT[:, k, CTX:TOK],
                              start=(k == 0), stop=(k == KD - 1))
                    mm = pe.matmul(ps[0:width, (2 * b + 1) * HALF:(2 * b + 1) * HALF + CTX], lhs, HT[:, k, 0:CTX],
                                   start=(k == 0), stop=(k == KD - 1))
                mm.then_inc(used, 1)

            for b in range(2):
                pe.wait_ge(w_in[b], 16)
                products(b)
            with pe.Fori(1, blocks // 2) as i:
                for b in range(2):
                    pe.wait_ge(w_in[b], 16 * i + 16)
                    pe.wait_ge(lat_out, 2 * i + (b - 1))
                    pe.wait_ge(ctx_out, 2 * i + (b - 1))
                    products(b)

        @block.vector
        def _(dve):
            with dve.Fori(0, blocks // 2) as i:
                for b in range(2):
                    dve.wait_ge(used, 2 * i + (b + 1))
                    dve.tensor_copy(OUT[0:width, bass.ds(2 * i + b, 1), CTX:TOK],
                                    ps[0:width, 2 * b * HALF:2 * b * HALF + LAT].unsqueeze(1)).then_inc(lat_out, 1)

        @block.scalar
        def _(act):
            with act.Fori(0, blocks // 2) as i:
                for b in range(2):
                    act.wait_ge(used, 2 * i + (b + 1))
                    act.activation(OUT[0:width, bass.ds(2 * i + b, 1), 0:CTX],
                                   ps[0:width, (2 * b + 1) * HALF:(2 * b + 1) * HALF + CTX].unsqueeze(1),
                                   ACT.Copy).then_inc(ctx_out, 1)


HEADS = 8
TOPK = 16
SLOTS = HEADS * TOPK
CODES = 2 * HEADS
LOWEST = -3.0e38


def choose_experts(nc, T, ps, QT, idx, gate, layer):
    with stage(nc, "keys_in", "q_cur", "scored", "scores_out", "s_free", "exp_in", "exp_out",
               "dve_line", "iota_done", "waited") as (ctx, (keys_in, q_cur, scored, scores_out, s_free,
                                                  exp_in, exp_out, dve_line, iota_done, mark)):
        keys = buf(ctx, nc, "keys", [P, CODES, P])
        q = buf(ctx, nc, "q_tile", [P, CODES, P])
        s = buf(ctx, nc, "scores", [P, CODES, P])
        s2 = buf(ctx, nc, "scores_rest", [P, CODES, P])
        top = buf(ctx, nc, "top_value", [P, CODES, TOPK])
        where = buf(ctx, nc, "top_index", [P, CODES, TOPK], U32)
        where_f = buf(ctx, nc, "top_index_f", [P, CODES, TOPK])
        best = buf(ctx, nc, "best_value", [P, HEADS, TOPK])
        at = buf(ctx, nc, "best_at", [P, HEADS, TOPK], U32)
        at_part = buf(ctx, nc, "best_part", [P, 2, SLOTS], U32)
        at_f = buf(ctx, nc, "best_part_f", [P, 2, SLOTS])
        key_f = buf(ctx, nc, "key_f", [P, 2, SLOTS])
        iota = buf(ctx, nc, "iota16", [P, TOPK])
        e = buf(ctx, nc, "exp_score", [P, HEADS, TOPK])
        e_sum = buf(ctx, nc, "exp_sum", [P, HEADS])
        block = ctx.enter_context(nc.Block())
        cand = s[:, :, :].rearrange("p (h a) n -> p h (a n)", a=2)
        cand2 = s2[:, :, :].rearrange("p (h a) n -> p h (a n)", a=2)
        pick = cand.rearrange("p h (k j) -> p h k j", j=TOPK)

        @block.sync
        def _(sp):
            sp.dma_start(keys[:], T["pk_keys"][layer]).then_inc(keys_in, 16)
            sp.wait_ge(keys_in, 16)

        @block.gpsimd
        def _(pool):
            pool.iota(iota[:], pattern=[[1, TOPK]], base=0, channel_multiplier=0,
                      allow_small_or_imprecise_dtypes=True).then_inc(iota_done, 1)

        @block.scalar
        def _(act):
            with act.Fori(0, NT) as t:
                act.activation(q[:], QT[:, :, bass.ds(t * P, P)], ACT.Copy).then_inc(q_cur, 1)
                act.wait_ge(scored, t + 1)
                act.wait_ge(s_free, t + 1)
                for b in range(4):
                    act.activation(s[:, 4 * b:4 * b + 4, :],
                                   ps[:, b * HALF:(b + 1) * HALF].rearrange("p (c n) -> p c n", c=4),
                                   ACT.Copy).then_inc(scores_out, 1)
                act.wait_ge(exp_in, t + 1)
                act.activation(e[:], e[:], ACT.Exp).then_inc(exp_out, 1)

        @block.tensor
        def _(pe):
            pe.wait_ge(keys_in, 16)
            with pe.Fori(0, NT) as t:
                pe.wait_ge(q_cur, t + 1)
                for c in range(CODES):
                    mm = pe.matmul(ps[:, c * P:(c + 1) * P], q[:, c, :],
                                   keys[:, c, :], start=True, stop=True)
                mm.then_inc(scored, 1)

        @block.vector
        def _(dve):
            line = Line(dve, dve_line)
            dve.sem_inc(s_free, 1)
            dve.wait_ge(iota_done, 1)

            def top16(src, rest, values, places, rows):
                for r in range(rows):
                    ins = dve.max(values[:, r, 0:8], src[:, r, :])
                line.then(ins, mark)
                for r in range(rows):
                    dve.max_index(places[:, r, 0:8], values[:, r, 0:8], src[:, r, :])
                    ins = dve.match_replace(rest[:, r, :], values[:, r, 0:8], src[:, r, :], LOWEST)
                line.then(ins, mark)
                for r in range(rows):
                    ins = dve.max(values[:, r, 8:16], rest[:, r, :])
                line.then(ins, mark)
                for r in range(rows):
                    ins = dve.max_index(places[:, r, 8:16], values[:, r, 8:16], rest[:, r, :])
                line.then(ins)

            with line.loop(0, NT, 22) as t:
                wait_apart(dve, scores_out, t * 4 + 4, mark)
                top16(s, s2, top, where, CODES)
                pair = top[:, :, :].rearrange("p (h a) k -> p h a k", a=2)
                line.then(dve.tensor_tensor(
                    pick, pair[:, :, 0, :].unsqueeze(3).to_broadcast([P, HEADS, TOPK, TOPK]),
                    pair[:, :, 1, :].unsqueeze(2).to_broadcast([P, HEADS, TOPK, TOPK]), ALU.add),
                    mark)
                top16(cand, cand2, best, at, HEADS)
                line.then(dve.tensor_tensor(e[:], best[:], best[:, :, 0:1].to_broadcast(
                    [P, HEADS, TOPK]), ALU.subtract))
                dve.sem_inc(exp_in, 1)
                flat = at[:, :, :].rearrange("p h k -> p (h k)")
                dve.tensor_scalar(at_part[:, 0, :], flat, 4, None, ALU.logical_shift_right)
                line.then(dve.tensor_scalar(at_part[:, 1, :], flat, TOPK - 1, None, ALU.bitwise_and))
                dve.tensor_copy(where_f[:], where[:])
                line.then(dve.tensor_copy(at_f[:], at_part[:]))
                half = where_f[:, :, :].rearrange("p (h a) k -> p h a k", a=2)
                for a in range(2):
                    line.then(dve.tensor_tensor(
                        pick.rearrange("p h k j -> p (h k) j"),
                        iota[:, :].unsqueeze(1).to_broadcast([P, SLOTS, TOPK]),
                        at_f[:, a, :].unsqueeze(2).to_broadcast([P, SLOTS, TOPK]), ALU.is_equal))
                    line.then(dve.tensor_tensor(
                        pick, pick, half[:, :, a, :].unsqueeze(2)
                        .to_broadcast([P, HEADS, TOPK, TOPK]), ALU.mult))
                    line.then(dve.tensor_reduce(key_f[:, a, :], pick.rearrange(
                        "p h k j -> p (h k) j"), AX.X, ALU.add))
                dve.sem_inc(s_free, 1)
                line.then(dve.scalar_tensor_tensor(
                    out=idx[:, bass.ds(t, 1), :], in0=key_f[:, 0:1, :], scalar=float(P),
                    in1=key_f[:, 1:2, :], op0=ALU.mult, op1=ALU.add))
                dve.wait_ge(exp_out, t + 1)
                line.then(dve.tensor_reduce(e_sum[:], e[:], AX.X, ALU.add))
                line.then(dve.reciprocal(e_sum[:], e_sum[:]))
                line.then(dve.tensor_tensor(
                    gate[:, bass.ds(t, 1), :].rearrange("p o (h k) -> p (o h) k", h=HEADS), e[:],
                    e_sum[:, :].unsqueeze(2).to_broadcast([P, HEADS, TOPK]), ALU.mult))


RING = 16
FREED = 4


def apply_experts(nc, ps, H, X, mod, idx, gate, table_u, table_v, layer, g_chunk):
    names = [f"row_in{b}" for b in range(RING)]
    with stage(nc, "row_free", "idx_set", "h_set", "dots_done", "gelu_done", "weights_set",
               "v_idx_free", "g_in", "dve_line", "waited", *names) as (
            ctx, (row_free, idx_set, h_set, dots_done, gelu_done, weights_set, v_idx_free, g_in,
                  dve_line, mark, *row_in)):
        rows = buf(ctx, nc, "expert_rows", [P, RING, D])
        idx_u = buf(ctx, nc, "idx_u", [P, SLOTS], U32)
        idx_v = buf(ctx, nc, "idx_v", [P, SLOTS], U32)
        h = buf(ctx, nc, "h_tile", [P, D])
        acc = buf(ctx, nc, "acc", [P, D])
        dots = buf(ctx, nc, "dots", [P, SLOTS])
        act_w = buf(ctx, nc, "expert_weight", [P, SLOTS])
        g_row = buf(ctx, nc, "gate_row", [P, 2, D])
        block = ctx.enter_context(nc.Block())
        per_tile = 2 * SLOTS

        @block.sync
        def _(sp):
            for g in range(2):
                sp.dma_start(g_row[:, g, :], mod[layer, g, g_chunk * D:(g_chunk + 1) * D]
                             .partition_broadcast(P)).then_inc(g_in, 16)

        @block.gpsimd
        def _(pool):
            with pool.Fori(0, NT) as t:
                for table, index, first in ((table_u, idx_u, 0), (table_v, idx_v, SLOTS)):
                    wait_apart(pool, (dots_done, v_idx_free)[first // SLOTS], t + 1, mark)
                    pool.tensor_copy(index[:, :].unsqueeze(1),
                                     idx[:, bass.ds(t, 1), :]).then_inc(idx_set, 1)
                    pool.wait_ge(idx_set, t * 2 + (1 + first // SLOTS))
                    for n in range(SLOTS):
                        b = n % RING
                        if n % FREED == 0:
                            wait_apart(pool, row_free, t * per_tile + (first + n + FREED), mark)
                        pool.indirect_dma_start(
                            out=rows[:, b, :], out_offset=None, in_=table,
                            in_offset=bass.IndirectOffsetOnAxis(ap=index[:, n:n + 1], axis=0),
                        ).then_inc(row_in[b], 16)

        @block.scalar
        def _(act):
            with act.Fori(0, NT) as t:
                act.wait_ge(dots_done, t + 1)
                act.activation(h[:, :].unsqueeze(1), H[:, bass.ds(t, 1), :],
                               ACT.Copy).then_inc(h_set, 1)
                act.wait_ge(dots_done, t + 2)
                act.activation(act_w[:], dots[:], ACT.Gelu_apprx_tanh).then_inc(gelu_done, 1)

        @block.vector
        def _(dve):
            line = Line(dve, dve_line)
            dve.sem_inc(row_free, RING)
            dve.sem_inc(dots_done, 1)
            dve.sem_inc(v_idx_free, 1)
            with line.loop(0, NT, 1) as t:
                dve.wait_ge(h_set, t + 1)
                for n in range(SLOTS):
                    b = n % RING
                    dve.wait_ge(row_in[b], t * (16 * per_tile // RING) + 16 * (n // RING + 1))
                    dve.tensor_tensor_reduce(rows[:, b, :], rows[:, b, :], h[:], 1.0, 0.0,
                                             ALU.mult, ALU.add, dots[:, n:n + 1]
                                             ).then_inc(row_free, 1)
                dve.wait_ge(row_free, t * per_tile + (RING + SLOTS))
                dve.sem_inc(dots_done, 1)
                dve.wait_ge(gelu_done, t + 1)
                line.then(dve.tensor_tensor(act_w[:, :].unsqueeze(1), act_w[:, :].unsqueeze(1),
                                            gate[:, bass.ds(t, 1), :], ALU.mult))
                for n in range(SLOTS):
                    b = n % RING
                    dve.wait_ge(row_in[b], t * (16 * per_tile // RING)
                                + 16 * ((SLOTS + n) // RING + 1))
                    w = act_w[:, n:n + 1]
                    if n == 0:
                        ins = dve.tensor_scalar(acc[:], rows[:, b, :], w, None, ALU.mult)
                    elif n < SLOTS - 1:
                        ins = dve.scalar_tensor_tensor(out=acc[:], in0=rows[:, b, :], scalar=w,
                                                       in1=acc[:], op0=ALU.mult, op1=ALU.add)
                    else:
                        ins = dve.scalar_tensor_tensor(
                            out=H[:, bass.ds(t, 1), :], in0=rows[:, b, :].unsqueeze(1), scalar=w,
                            in1=acc[:, :].unsqueeze(1), op0=ALU.mult, op1=ALU.add)
                    ins.then_inc(row_free, 1)
                    dve.wait_ge(row_free, t * per_tile + (RING + SLOTS + n + 1))
                dve.sem_inc(v_idx_free, 1)
            dve.wait_ge(g_in, 32)
            for t in range(NT):
                line.then(dve.tensor_tensor(H[:, t, :], H[:, t, :], g_row[:, group_of(t), :], ALU.mult))
                line.then(dve.tensor_tensor(X[:, t, :], X[:, t, :], H[:, t, :], ALU.add))


HYW = 512
HYF = 64
EMB = 33
DFT = P + (LAT // P) * LAT


def dft_block(m, src, dst):
    if dst == 0:
        return m[:, 0:P]
    at = P + (src - 1) * LAT + (dst - 1) * P
    return m[:, at:at + P]


def sources(tile):
    return (0,) if tile == 0 else tuple(range(1, NT))


def hyena_filters(nc, T, ps, KC, KS):
    with stage(nc, "small_in", "big_in", "layer_done", "args_ready", "sines_done", "taps_raw",
               "env_done", "taps_done", "sq_done", "sums_done", "rooted", "scaled", "dft_done",
               "dve_line", "act_line") as (
            ctx, (small_in, big_in, layer_done, args_ready, sines_done, taps_raw, env_done,
                  taps_done, sq_done, sums_done, rooted, scaled, dft_done, dve_line, act_line)):
        z = buf(ctx, nc, "features", [EMB, TOK])
        w1 = buf(ctx, nc, "hy_w1", [EMB, HYF])
        w2 = buf(ctx, nc, "hy_w2", [HYF, HYF])
        w3 = buf(ctx, nc, "hy_w3", [HYF, 4 * HYW])
        col = buf(ctx, nc, "hy_cols", [HYF, 3])
        times = buf(ctx, nc, "hy_times", [P, 2, NT])
        decay = buf(ctx, nc, "decay", [P, 4 * HYW])
        arg = buf(ctx, nc, "sine_arg", [HYF, TOK])
        turn = buf(ctx, nc, "sine_turn", [HYF, TOK])
        h = buf(ctx, nc, "sine", [HYF, TOK])
        env = buf(ctx, nc, "envelope", [P, 4 * HYW])
        tmp = buf(ctx, nc, "bwd_taps", [P, 2, HYW])
        A = buf(ctx, nc, "taps_sum", [P, NT, 2, HYW])
        B = buf(ctx, nc, "taps_diff", [P, NT, 2, HYW])
        ones = buf(ctx, nc, "ones", [P, P])
        root = buf(ctx, nc, "filter_norm", [P, 2, 2 * HYW])
        cf = buf(ctx, nc, "cos_fwd", [P, DFT])
        sf = buf(ctx, nc, "sin_fwd", [P, DFT])
        block = ctx.enter_context(nc.Block())
        four = ps[:, 0:4 * HALF]
        sq = env

        @block.sync
        def _(sp):
            for dst, src in ((z, "hy_z"), (w1, "hy_w1"), (w2, "hy_w2"), (col, "hy_cols"),
                             (w3, "hy_w3"), (times, "hy_times")):
                sp.dma_start(dst[:], T[src]).then_inc(small_in, 16)
            sp.dma_start(decay[:], T["hy_decay"].partition_broadcast(P)).then_inc(small_in, 16)
            sp.dma_start(cf[:], T["cos_fwd"]).then_inc(big_in, 16)
            sp.dma_start(sf[:], T["sin_fwd"]).then_inc(big_in, 16)

        @block.tensor
        def _(pe):
            pe.wait_ge(small_in, 7 * 16)
            for layer, (w, src) in enumerate(((w1, z), (w2, h))):
                if layer:
                    pe.wait_ge(sines_done, 1)
                pe.matmul(ps[0:HYF, 0:HALF], w[:], src[:, 0:HALF], start=True, stop=True)
                pe.matmul(ps[0:HYF, HALF:TOK], w[:], src[:, HALF:TOK],
                          start=True, stop=True).then_inc(layer_done, 1)
            pe.wait_ge(sines_done, 2)
            for t in range(NT):
                if t:
                    pe.wait_ge(taps_done, t)
                for j in range(4):
                    mm = pe.matmul(ps[:, j * HALF:(j + 1) * HALF], h[:, t * P:(t + 1) * P],
                                   w3[:, j * HYW:(j + 1) * HYW], start=True, stop=True)
                mm.then_inc(taps_raw, 1)
            for t in range(NT):
                pe.wait_ge(sq_done, t + 1)
                g = group_of(t)
                for o in range(2):
                    at = (4 + 2 * g + o) * HALF
                    mm = pe.matmul(ps[:, at:at + HALF], ones[:], sq[:, o * HYW:(o + 1) * HYW],
                                   start=(t < 2), stop=(t in (0, NT - 1)))
                mm.then_inc(sums_done, 1)
            pe.wait_ge(big_in, 32)
            pe.wait_ge(scaled, 2 * NT)
            n = 0
            for t in range(NT):
                for m, taps in ((cf, A), (sf, B)):
                    for o in range(2):
                        if n >= 4:
                            pe.wait_ge(dft_done, n - 3)
                        b = (n % 4) * HALF
                        for k in sources(t):
                            mm = pe.matmul(ps[:, b:b + HALF], dft_block(m, k, t),
                                           taps[:, k, o, :], start=(k == sources(t)[0]),
                                           stop=(k == sources(t)[-1]))
                        mm.then_inc(taps_raw, 1)
                        n += 1

        @block.scalar
        def _(act):
            line = Line(act, act_line)
            act.wait_ge(small_in, 7 * 16)
            line.then(act.activation(decay[:], decay[:], ACT.Abs))
            for layer in range(2):
                act.wait_ge(args_ready, layer + 1)
                act.activation(h[:], arg[:], ACT.Sin).then_inc(sines_done, 1)
            for t in range(NT):
                if t:
                    act.wait_ge(taps_done, t)
                act.activation(env[:], decay[:], ACT.Exp,
                               scale=times[:, 0, t:t + 1]).then_inc(env_done, 1)
            act.wait_ge(rooted, 1)
            line.then(act.activation(root[:], root[:], ACT.Sqrt))
            for n in range(4 * NT):
                t, o = n // 4, n % 2
                act.wait_ge(taps_raw, NT + n + 1)
                b = (n % 4) * HALF
                act.activation((KC, KS)[n % 4 // 2][:, t, o, :], ps[:, b:b + HALF],
                               ACT.Copy).then_inc(dft_done, 1)

        @block.vector
        def _(dve):
            line = Line(dve, dve_line)
            line.then(dve.memset(ones[:], 1.0))
            dve.wait_ge(small_in, 7 * 16)
            for layer in range(2):
                dve.wait_ge(layer_done, layer + 1)
                line.then(dve.tensor_scalar(arg[:], ps[0:HYF, 0:TOK], col[:, layer:layer + 1],
                                            col[:, 2:3], ALU.add, ALU.mult))
                reduce_turns(dve, line, arg, turn)
                dve.sem_inc(args_ready, 1)
            for t in range(NT):
                dve.wait_ge(taps_raw, t + 1)
                dve.wait_ge(env_done, t + 1)
                raw = four.rearrange("p (o d c) -> p o d c", o=2, d=2)
                e = env[:, :].rearrange("p (o d c) -> p o d c", o=2, d=2)
                dve.tensor_tensor(A[:, t], raw[:, :, 0, :], e[:, :, 0, :], ALU.mult)
                line.then(dve.scalar_tensor_tensor(out=tmp[:], in0=raw[:, :, 1, :],
                                                   scalar=times[:, 1, t:t + 1],
                                                   in1=e[:, :, 1, :], op0=ALU.mult, op1=ALU.mult))
                dve.sem_inc(taps_done, 1)
                dve.tensor_tensor(B[:, t], A[:, t], tmp[:], ALU.subtract)
                line.then(dve.tensor_tensor(A[:, t], A[:, t], tmp[:], ALU.add))
            q = sq[:, 0:2 * HYW]
            q2 = sq[:, 2 * HYW:4 * HYW]
            for t in range(NT):
                if t:
                    dve.wait_ge(sums_done, t)
                dve.tensor_tensor(q, A[:, t].rearrange("p o c -> p (o c)"),
                                  A[:, t].rearrange("p o c -> p (o c)"), ALU.mult)
                line.then(dve.tensor_tensor(q2, B[:, t].rearrange("p o c -> p (o c)"),
                                            B[:, t].rearrange("p o c -> p (o c)"), ALU.mult))
                dve.tensor_tensor(q, q, q2, ALU.add).then_inc(sq_done, 1)
                dve.wait_ge(sq_done, t + 1)
            dve.wait_ge(sums_done, NT)
            line.then(dve.tensor_scalar(root[:], ps[:, 4 * HALF:8 * HALF]
                                        .rearrange("p (g n) -> p g n", g=2),
                                        0.5, EPS, ALU.mult, ALU.add))
            dve.reciprocal(root[:], root[:]).then_inc(rooted, 1)
            dve.wait_ge(act_line, 2)
            for t in range(NT):
                for taps in (A, B):
                    v = taps[:, t].rearrange("p o c -> p (o c)")
                    dve.tensor_tensor(v, v, root[:, group_of(t), :], ALU.mult).then_inc(scaled, 1)


def reduce_turns(dve, line, arg, turn):
    hi = 6.28125
    line.then(dve.tensor_scalar(turn[:], arg[:], 1.0 / TWO_PI, ROUND, ALU.mult, ALU.add))
    line.then(dve.tensor_scalar(turn[:], turn[:], ROUND, None, ALU.subtract))
    line.then(dve.scalar_tensor_tensor(out=arg[:], in0=turn[:], scalar=-hi, in1=arg[:],
                                       op0=ALU.mult, op1=ALU.add))
    line.then(dve.scalar_tensor_tensor(out=arg[:], in0=turn[:], scalar=-(TWO_PI - hi),
                                       in1=arg[:], op0=ALU.mult, op1=ALU.add))
    line.then(dve.tensor_scalar(arg[:], arg[:], PI_BELOW, -PI_BELOW, ALU.min, ALU.max))


def short_conv(dve, line, out, x, taps):
    line.then(dve.tensor_scalar(out, x, taps(1), taps(3), ALU.mult, ALU.add))
    for tap, lead in ((0, 1), (2, 0)):
        for a, b in GROUPS:
            n = b - a - 1
            ins = dve.scalar_tensor_tensor(
                out=out[:, a + lead:a + lead + n], in0=x[:, a + 1 - lead:a + 1 - lead + n],
                scalar=taps(tap), in1=out[:, a + lead:a + lead + n], op0=ALU.mult, op1=ALU.add)
        line.then(ins)


def hyena_inputs(nc, T, ps, PH, VG, ident):
    blocks = 3 * HYW // P
    with stage(nc, "taps_in", "conv_done", "turned", "out_done", "dve_line") as (
            ctx, (taps_in, conv_done, turned, out_done, dve_line)):
        taps = buf(ctx, nc, "conv_taps", [P, blocks, 4])
        cur = buf(ctx, nc, "conv_taps_cur", [P, 4])
        y = buf(ctx, nc, "conv_block", [P, 2, TOK])
        x = buf(ctx, nc, "conv_source", [P, TOK])
        block = ctx.enter_context(nc.Block())

        @block.sync
        def _(sp):
            sp.dma_start(taps[:], T["hy_taps"]).then_inc(taps_in, 16)
            sp.wait_ge(taps_in, 16)

        @block.vector
        def _(dve):
            line = Line(dve, dve_line)
            dve.wait_ge(taps_in, 16)
            dve.sem_inc(turned, 2)
            with line.loop(0, blocks // 2, 8) as i:
                for b in range(2):
                    dve.tensor_copy(x[:, :].unsqueeze(1), PH[:, bass.ds(i * 2 + b, 1), :])
                    line.then(dve.tensor_copy(cur[:, :].unsqueeze(1),
                                              taps[:, bass.ds(i * 2 + b, 1), :]))
                    dve.wait_ge(turned, i * 2 + (b + 1))
                    short_conv(dve, line, y[:, b, :], x[:, :], lambda k: cur[:, k:k + 1])
                    dve.sem_inc(conv_done, 1)

        @block.tensor
        def _(pe):
            pe.sem_inc(out_done, 2)
            with pe.Fori(0, blocks // 2) as i:
                for b in range(2):
                    pe.wait_ge(out_done, i * 2 + (b + 1))
                    pe.wait_ge(conv_done, i * 2 + (b + 1))
                    for t in range(NT):
                        at = 2 * b * HALF + t * P
                        mm = pe.transpose(ps[:, at:at + P], y[:, b, t * P:(t + 1) * P], ident[:])
                    mm.then_inc(turned, 1)

        @block.scalar
        def _(act):
            with act.Fori(0, blocks // 2) as i:
                for b in range(2):
                    act.wait_ge(turned, i * 2 + (b + 3))
                    act.activation(VG[:, :, bass.ds((i * 2 + b) * P, P)],
                                   ps[:, 2 * b * HALF:2 * b * HALF + TOK]
                                   .rearrange("p (t c) -> p t c", c=P), ACT.Copy).then_inc(out_done, 1)


def hyena_convolve(nc, T, ps, VG, KC, KS, MIXT, ident):
    with stage(nc, "mats_in", "angles", "mixed", "lines", "z_ready", "turned", "out_done",
               "dve_line") as (
            ctx, (mats_in, angles, mixed, lines, z_ready, turned, out_done, dve_line)):
        cf = buf(ctx, nc, "cos_fwd", [P, DFT])
        sf = buf(ctx, nc, "sin_fwd", [P, DFT])
        ci = buf(ctx, nc, "cos_inv", [P, DFT])
        si = buf(ctx, nc, "sin_inv", [P, DFT])
        bias = buf(ctx, nc, "hy_bias", [P, 2, HYW])
        R = buf(ctx, nc, "product_re", [P, NT, HYW])
        I = buf(ctx, nc, "product_im", [P, NT, HYW])
        t1 = buf(ctx, nc, "part1", [P, HYW])
        t2 = buf(ctx, nc, "part2", [P, HYW])
        t3 = buf(ctx, nc, "part3", [P, HYW])
        t4 = buf(ctx, nc, "part4", [P, HYW])
        z = VG[:, :, 0:HYW]
        block = ctx.enter_context(nc.Block())

        @block.sync
        def _(sp):
            for dst, src in ((cf, "cos_fwd"), (sf, "sin_fwd"), (ci, "cos_inv"), (si, "sin_inv")):
                sp.dma_start(dst[:], T[src]).then_inc(mats_in, 16)
            sp.dma_start(bias[:], T["hy_bias"].partition_broadcast(P)).then_inc(mats_in, 16)

        @block.tensor
        def _(pe):
            pe.wait_ge(mats_in, 80)
            for o in range(2):
                pe.wait_ge(z_ready, NT * o) if o else None
                for t in range(NT):
                    n = NT * o + t
                    if n >= 2:
                        pe.wait_ge(mixed, n - 1)
                    for j, m in enumerate((cf, sf)):
                        at = (2 * (n % 2) + j) * HALF
                        for k in sources(t):
                            mm = pe.matmul(ps[:, at:at + HALF], dft_block(m, k, t), z[:, k, :],
                                           start=(k == sources(t)[0]), stop=(k == sources(t)[-1]))
                    mm.then_inc(angles, 1)
                for t in range(NT):
                    n = NT * o + t
                    pe.wait_ge(mixed, NT * o + sources(t)[-1] + 1)
                    if n >= 2:
                        pe.wait_ge(z_ready, n - 1)
                    at = (4 + n % 2) * HALF
                    for k in sources(t):
                        pe.matmul(ps[:, at:at + HALF], dft_block(ci, k, t), R[:, k, :],
                                  start=(k == sources(t)[0]), stop=False)
                        mm = pe.matmul(ps[:, at:at + HALF], dft_block(si, k, t), I[:, k, :],
                                       start=False, stop=(k == sources(t)[-1]))
                    mm.then_inc(lines, 1)
            for t in range(NT):
                pe.wait_ge(z_ready, NT + t + 1)
                if t >= 2:
                    pe.wait_ge(out_done, t - 1)
                for m in range(4):
                    at = (6 + t % 2) * HALF + m * P
                    mm = pe.transpose(ps[:, at:at + P], z[:, t, m * P:(m + 1) * P], ident[:])
                mm.then_inc(turned, 1)

        @block.scalar
        def _(act):
            for t in range(NT):
                act.wait_ge(turned, t + 1)
                at = (6 + t % 2) * HALF
                act.activation(MIXT[:, 0:4, t * P:(t + 1) * P], ps[:, at:at + HALF]
                               .rearrange("p (m c) -> p m c", c=P), ACT.Copy).then_inc(out_done, 1)

        @block.vector
        def _(dve):
            line = Line(dve, dve_line)
            dve.wait_ge(mats_in, 80)
            for o in range(2):
                for t in range(NT):
                    n = NT * o + t
                    dve.wait_ge(angles, n + 1)
                    b = 2 * (n % 2) * HALF
                    zc, zs = ps[:, b:b + HALF], ps[:, b + HALF:b + 2 * HALF]
                    dve.tensor_tensor(t1[:], zc, KC[:, t, o, :], ALU.mult)
                    dve.tensor_tensor(t2[:], zs, KS[:, t, o, :], ALU.mult)
                    dve.tensor_tensor(t3[:], zs, KC[:, t, o, :], ALU.mult)
                    line.then(dve.tensor_tensor(t4[:], zc, KS[:, t, o, :], ALU.mult))
                    dve.tensor_tensor(R[:, t, :], t1[:], t2[:], ALU.subtract)
                    line.then(dve.tensor_tensor(I[:, t, :], t3[:], t4[:], ALU.add))
                    dve.sem_inc(mixed, 1)
                for t in range(NT):
                    n = NT * o + t
                    dve.wait_ge(lines, n + 1)
                    at = (4 + n % 2) * HALF
                    line.then(dve.tensor_tensor(t1[:], z[:, t, :], bias[:, o, :], ALU.mult))
                    line.then(dve.tensor_tensor(t1[:], t1[:], ps[:, at:at + HALF], ALU.add))
                    dve.tensor_tensor(z[:, t, :], t1[:], VG[:, t, (o + 1) * HYW:(o + 2) * HYW],
                                      ALU.mult).then_inc(z_ready, 1)
                    dve.wait_ge(z_ready, n + 1)


PAIRS = 16
S5C = 16
UNITS = 8
SEGMENTS = (((0, CTX, False), (CTX, TOK, True)), ((0, LAT, True), (LAT, TOK, False)))


def exact_exp(dve, one, out, x, n, y, bits):
    one(dve.tensor_scalar(n, x, 1.0 / math.log(2.0), ROUND, ALU.mult, ALU.add))
    one(dve.tensor_scalar(n, n, ROUND, None, ALU.subtract))
    one(dve.tensor_scalar(n, n, -126.0, 127.0, ALU.max, ALU.min))
    one(dve.scalar_tensor_tensor(out=y, in0=n, scalar=-0.693359375, in1=x, op0=ALU.mult, op1=ALU.add))
    one(dve.scalar_tensor_tensor(out=y, in0=n, scalar=0.693359375 - math.log(2.0), in1=y,
                                 op0=ALU.mult, op1=ALU.add))
    one(dve.tensor_scalar(y, y, -0.35, 0.35, ALU.max, ALU.min))
    one(dve.tensor_scalar(n, n, 127.0, None, ALU.add))
    one(dve.tensor_copy(bits, n))
    one(dve.tensor_scalar(bits, bits, 23, None, ALU.logical_shift_left))
    one(dve.tensor_scalar(out, y, 1.0 / 5040, 1.0 / 720, ALU.mult, ALU.add))
    for c in (1.0 / 120, 1.0 / 24, 1.0 / 6, 0.5, 1.0, 1.0):
        one(dve.tensor_tensor(out, out, y, ALU.mult))
        one(dve.tensor_scalar(out, out, c, None, ALU.add))
    one(dve.tensor_tensor(out, out, bits.bitcast(F32), ALU.mult))


def s5(nc, T, ps, US, G, ident, out_re, out_im):
    with stage(nc, "par_in", "d_in", "dve_line", "act_line", "pool_line", "bd_ready", "bt_raw",
               "bt_ready", "bu_done", "bu_used", "turn_set", "turn_used", "trig_set", "trig_used",
               "prod_set", "prod_used", "y_done", "y_out", "states_out", "waited") as (
            ctx, (par_in, d_in, dve_line, act_line, pool_line, bd_ready, bt_raw, bt_ready, bu_done,
                  bu_used, turn_set, turn_used, trig_set, trig_used, prod_set, prod_used, y_done,
                  y_out, states_out, mark)):
        N2 = [P, 2, PAIRS]
        par = buf(ctx, nc, "s5_par", [P, 5, 2 * PAIRS])
        B = buf(ctx, nc, "s5_B", [P, 2, 2 * PAIRS, S5C])
        C = buf(ctx, nc, "s5_C", [P, 2, 2 * PAIRS, S5C])
        Bb = buf(ctx, nc, "s5_Bbar", [P, 2, 2 * PAIRS, S5C])
        tmpB = buf(ctx, nc, "s5_tmpB", [P, 2 * PAIRS, S5C])
        C3 = buf(ctx, nc, "s5_C3", [P, 3, 2 * PAIRS, S5C])
        dt = buf(ctx, nc, "s5_dt", [P, 2 * PAIRS])
        r = buf(ctx, nc, "s5_r", [P, 2 * PAIRS])
        hl = buf(ctx, nc, "s5_turns", [P, 3, 2 * PAIRS])
        phi = buf(ctx, nc, "s5_phi", [P, 2 * PAIRS])
        w1 = buf(ctx, nc, "s5_w1", [P, 2 * PAIRS])
        w2 = buf(ctx, nc, "s5_w2", [P, 2 * PAIRS])
        lr = buf(ctx, nc, "s5_lr", [P, 2 * PAIRS])
        li = buf(ctx, nc, "s5_li", [P, 2 * PAIRS])
        fr = buf(ctx, nc, "s5_fr", [P, 2 * PAIRS])
        fi = buf(ctx, nc, "s5_fi", [P, 2 * PAIRS])
        whole = buf(ctx, nc, "s5_exponent", [P, 2 * PAIRS], I32)
        quarter = buf(ctx, nc, "quarter_turn", [P, 1])
        steps = buf(ctx, nc, "steps", [P, 2, TOK])
        dcol = buf(ctx, nc, "s5_d", [P, 4])
        Bd = buf(ctx, nc, "s5_Bd", [P, 2, 2, 4, 2 * S5C])
        Cd = buf(ctx, nc, "s5_Cd", [P, 3, 2, 4, 2 * S5C])
        BT = buf(ctx, nc, "s5_BT", [P, 2, 2, P])
        cur = buf(ctx, nc, "s5_cur", [P, 3, 2, 4])
        turns = buf(ctx, nc, "s5_turns_cur", [P, 3, 2, 4])
        k_t = buf(ctx, nc, "s5_whole", [P, TOK])
        lo_t = buf(ctx, nc, "s5_rest", [P, TOK])
        ang = buf(ctx, nc, "s5_angle", [P, 2, TOK])
        ang_abs = buf(ctx, nc, "s5_angle_abs", [P, TOK])
        trig = buf(ctx, nc, "s5_trig", [P, 2, 2, TOK])
        g_in = buf(ctx, nc, "s5_g_in", [P, 4, TOK])
        g = buf(ctx, nc, "s5_g", [P, 2, TOK])
        prod = buf(ctx, nc, "s5_prod", [P, 2, 4, TOK])
        st = buf(ctx, nc, "s5_states", [P, 2, 2, PAIRS])
        y = buf(ctx, nc, "s5_y", [P, TOK])
        ucur = buf(ctx, nc, "s5_u", [P, TOK])
        dnow = buf(ctx, nc, "s5_d_cur", [P, 1])
        block = ctx.enter_context(nc.Block())
        BU = (slice(0, TOK), slice(1024, 1024 + TOK))
        Y0 = 4 * HALF
        BT0 = 6 * HALF
        SCALE = 6.283185

        def block_units(a, m):
            return a.rearrange("p c (d k) -> p c d k", d=2)[:, :, :, bass.ds(m * 4, 4)]

        @block.sync
        def _(sp):
            for dst, src in ((par, "s5_par"), (B, "s5_B"), (C, "s5_C"), (dcol, "s5_d")):
                sp.dma_start(dst[:], T[src]).then_inc(par_in, 16)
            sp.dma_start(steps[:], T["s5_steps"].partition_broadcast(P)).then_inc(d_in, 16)
            sp.wait_ge(y_out, 4)
            for part, out in ((0, out_re), (1, out_im)):
                sp.dma_start(out.rearrange("d (k g) s -> (g s) d k", g=2), st[:, part],
                             allow_slow_non_contiguous=True).then_inc(states_out, 16)
            sp.wait_ge(states_out, 32)

        @block.gpsimd
        def _(pool):
            line = Line(pool, pool_line)
            pool.wait_ge(d_in, 16)
            pool.wait_ge(bd_ready, 1)
            with line.loop(0, 4, 1 + UNITS * 7) as m:
                line.then(pool.tensor_copy(turns[:], block_units(hl, m)), mark)
                for u in range(UNITS):
                    q, d = u // 2, u % 2
                    b = u % 2
                    both, hi, lo = (turns[:, c, d, q:q + 1] for c in range(3))
                    s, a = steps[:, d, :], ang[:, b, :]
                    line.then(pool.tensor_scalar(k_t[:], s, both, ROUND, ALU.mult, ALU.add), mark)
                    wait_apart(pool, turn_used, m * UNITS + (u + 1), mark)
                    line.then(pool.tensor_scalar(k_t[:], k_t[:], ROUND, None, ALU.subtract), mark)
                    line.then(pool.tensor_scalar(a, s, hi, None, ALU.mult), mark)
                    line.then(pool.tensor_scalar(lo_t[:], s, lo, None, ALU.mult))
                    line.then(pool.tensor_tensor(a, a, k_t[:], ALU.subtract))
                    line.then(pool.tensor_tensor(a, a, lo_t[:], ALU.add), mark)
                    line.then(pool.tensor_scalar(a, a, 0.5, -0.5, ALU.min, ALU.max))
                    pool.sem_inc(turn_set, 1)

        @block.scalar
        def _(act):
            line = Line(act, act_line)
            act.wait_ge(bd_ready, 1)
            line.then(act.activation(w1[:], phi[:], ACT.Sin, scale=SCALE))
            line.then(act.activation(w2[:], phi[:], ACT.Abs))
            line.then(act.activation(w2[:], w2[:], ACT.Sin, bias=quarter[:], scale=-SCALE))
            act.sem_inc(turn_used, 2)
            with line.loop(0, 4, UNITS + 2) as m:
                for u in range(UNITS):
                    b = u % 2
                    act.wait_ge(turn_set, m * UNITS + (u + 1))
                    act.wait_ge(trig_used, m * UNITS + (u + 1))
                    line.then(act.activation(ang_abs[:], ang[:, b, :], ACT.Abs))
                    act.activation(trig[:, b, 1, :], ang[:, b, :], ACT.Sin, scale=SCALE
                                   ).then_inc(trig_set, 1)
                    act.activation(trig[:, b, 0, :], ang_abs[:], ACT.Sin, bias=quarter[:],
                                   scale=-SCALE).then_inc(trig_set, 1)
                    act.wait_ge(trig_set, m * (2 * UNITS) + (2 * u + 2))
                    act.sem_inc(turn_used, 1)
                    if u == 0:
                        act.wait_ge(bt_raw, m + 1)
                        line.then(act.activation(BT[:, :, :, :].rearrange("p a b n -> p (a b n)"),
                                                 ps[:, BT0:BT0 + 4 * P], ACT.Copy))
                        act.sem_inc(bt_ready, 1)
                act.wait_ge(y_done, m * 2 + 2)
                line.then(act.activation(G[:, bass.ds(m, 1), :], y[:, :].unsqueeze(1),
                                         ACT.Gelu_apprx_tanh))
                act.sem_inc(y_out, 1)

        @block.tensor
        def _(pe):
            def bu(m, u):
                q, d = u // 2, u % 2
                pe.wait_ge(bu_used, m * UNITS + (u + 1))
                rows = slice(32 * q, 32 * q + 32)
                for part in range(2):
                    at = BU[part].start
                    for c0, c1 in ((0, HALF), (HALF, TOK)):
                        mm = pe.matmul(ps[:, at + c0:at + c1], BT[rows, d, part, :],
                                       ucur[rows, c0:c1], start=True, stop=True)
                mm.then_inc(bu_done, 1)

            def readout(m, u):
                q, d = u // 2, u % 2
                pe.wait_ge(prod_set, m * UNITS + (u + 1))
                for j, c in enumerate((0, 1, 2, 2)):
                    for c0, c1 in ((0, HALF), (HALF, TOK)):
                        mm = pe.matmul(ps[32 * q:32 * q + 32, Y0 + c0:Y0 + c1],
                                       Cd[:, c, d, q, :], prod[:, u % 2, j, c0:c1],
                                       start=(d == 0 and j == 0), stop=(d == 1 and j == 3))
                mm.then_inc(prod_used, 1)

            with pe.Fori(0, 4) as m:
                pe.wait_ge(bd_ready, m + 2)
                for d in range(2):
                    for part in range(2):
                        at = BT0 + (2 * d + part) * P
                        mm = pe.transpose(ps[:, at:at + P],
                                          Bd[:, d, part].rearrange("p q c -> p (q c)"), ident[:])
                mm.then_inc(bt_raw, 1)
                pe.wait_ge(bt_ready, m + 1)
                for u in range(UNITS):
                    bu(m, u)
                    if u:
                        readout(m, u - 1)
                readout(m, UNITS - 1)

        @block.vector
        def _(dve):
            line = Line(dve, dve_line)
            one = line.then
            tt, ts = dve.tensor_tensor, dve.tensor_scalar
            dve.memset(Bd[:], 0.0)
            dve.memset(Cd[:], 0.0)
            one(dve.memset(quarter[:], math.pi / 2))
            dve.wait_ge(par_in, 64)
            exact_exp(dve, one, dt[:], par[:, 2, :], w1[:], w2[:], whole[:])
            one(tt(lr[:], par[:, 0, :], dt[:], ALU.mult))
            exact_exp(dve, one, r[:], lr[:], w1[:], w2[:], whole[:])
            one(tt(phi[:], par[:, 1, :], dt[:], ALU.mult))
            one(ts(phi[:], phi[:], 1.0 / TWO_PI, None, ALU.mult))
            one(ts(w1[:], phi[:], ROUND, None, ALU.add))
            one(ts(w1[:], w1[:], ROUND, None, ALU.subtract))
            one(tt(phi[:], phi[:], w1[:], ALU.subtract))
            one(ts(w2[:], phi[:], 1536.0, None, ALU.add))
            one(ts(hl[:, 1, :], w2[:], 1536.0, None, ALU.subtract))
            one(tt(hl[:, 2, :], phi[:], hl[:, 1, :], ALU.subtract))
            one(dve.tensor_copy(hl[:, 0, :], phi[:]))
            dve.sem_inc(bd_ready, 1)
            dve.wait_ge(act_line, 3)
            one(tt(lr[:], r[:], w2[:], ALU.mult))
            one(tt(li[:], r[:], w1[:], ALU.mult))
            one(ts(lr[:], lr[:], -1.0, None, ALU.add))
            one(tt(w1[:], par[:, 0, :], par[:, 0, :], ALU.mult))
            one(tt(w2[:], par[:, 1, :], par[:, 1, :], ALU.mult))
            one(tt(w1[:], w1[:], w2[:], ALU.add))
            one(dve.reciprocal(w1[:], w1[:]))
            one(tt(fr[:], lr[:], par[:, 0, :], ALU.mult))
            one(tt(w2[:], li[:], par[:, 1, :], ALU.mult))
            one(tt(fr[:], fr[:], w2[:], ALU.add))
            one(tt(fr[:], fr[:], w1[:], ALU.mult))
            one(tt(fi[:], li[:], par[:, 0, :], ALU.mult))
            one(tt(w2[:], lr[:], par[:, 1, :], ALU.mult))
            one(tt(fi[:], fi[:], w2[:], ALU.subtract))
            one(tt(fi[:], fi[:], w1[:], ALU.mult))
            wide = [P, 2 * PAIRS, S5C]
            fr_w, fi_w = (f[:, :].unsqueeze(2).to_broadcast(wide) for f in (fr, fi))
            one(tt(Bb[:, 0], B[:, 0], fr_w, ALU.mult))
            one(tt(tmpB[:], B[:, 1], fi_w, ALU.mult))
            one(tt(Bb[:, 0], Bb[:, 0], tmpB[:], ALU.subtract))
            one(tt(Bb[:, 1], B[:, 1], fr_w, ALU.mult))
            one(tt(tmpB[:], B[:, 0], fi_w, ALU.mult))
            one(tt(Bb[:, 1], Bb[:, 1], tmpB[:], ALU.add))
            one(dve.tensor_copy(C3[:, 0], C[:, 0]))
            one(ts(C3[:, 1], C[:, 0], -1.0, None, ALU.mult))
            one(ts(C3[:, 2], C[:, 1], -1.0, None, ALU.mult))
            dve.sem_inc(trig_used, 2)
            dve.sem_inc(bu_used, 1)
            dve.wait_ge(d_in, 16)
            with line.loop(0, 4, 5 * UNITS + 2) as m:
                for n, (src, dst) in enumerate(((Bb, Bd), (C3, Cd))):
                    for part in range(2 + n):
                        for gr in range(2):
                            half = slice(64 * gr, 64 * gr + 64)
                            view = src[half, part].rearrange("p (d k) j -> p d k j", d=2)
                            to = dst[half, :, part] if n == 0 else dst[half, part]
                            dve.tensor_copy(to[:, :, :, S5C * gr:S5C * gr + S5C],
                                            view[:, :, bass.ds(m * 4, 4), :])
                dve.tensor_copy(ucur[:, :].unsqueeze(1), US[:, bass.ds(m, 1), :])
                dve.tensor_copy(cur[:, 0:1], block_units(r[:, :].unsqueeze(1), m))
                one(dve.tensor_copy(cur[:, 1:3], block_units(par[:, 3:5, :], m)))
                dve.sem_inc(bd_ready, 1)
                for u in range(UNITS):
                    q, d, b = u // 2, u % 2, u % 2
                    cos, sin = trig[:, b, 0, :], trig[:, b, 1, :]
                    way = (lambda a: a) if d == 0 else (lambda a: a[:, ::-1])
                    bre, bim = way(ps[:, BU[0]]), way(ps[:, BU[1]])
                    dve.wait_ge(bu_done, m * UNITS + (u + 1))
                    dve.wait_ge(trig_set, m * (2 * UNITS) + (2 * u + 2))
                    tt(g_in[:, 0], bre, cos, ALU.mult)
                    tt(g_in[:, 1], bim, sin, ALU.mult)
                    tt(g_in[:, 2], bim, cos, ALU.mult)
                    one(tt(g_in[:, 3], bre, sin, ALU.mult))
                    dve.sem_inc(bu_used, 1)
                    tt(g_in[:, 0], g_in[:, 0], g_in[:, 1], ALU.add)
                    one(tt(g_in[:, 2], g_in[:, 2], g_in[:, 3], ALU.subtract))
                    for part in range(2):
                        for a, z, cached in SEGMENTS[d]:
                            first = cur[:, 1 + part, d, q:q + 1] if cached else 0.0
                            ins = dve.tensor_tensor_scan(
                                g[:, part, a:z], cur[:, 0, d, q:q + 1].to_broadcast([P, z - a]),
                                g_in[:, 2 * part, a:z], first, ALU.mult, ALU.add)
                    one(ins)
                    dve.wait_ge(prod_used, m * UNITS + u - 1) if u >= 2 else None
                    for j, (part, f) in enumerate(((0, cos), (1, sin), (0, sin), (1, cos))):
                        ins = tt(way(prod[:, b, j, :]), g[:, part, :], f, ALU.mult)
                    one(ins)
                    dve.sem_inc(prod_set, 1)
                    dve.sem_inc(trig_used, 1)
                    last = CTX - 1 if d == 0 else 0
                    one_st = [prod[:, b, j, last:last + 1].unsqueeze(1) for j in range(4)]
                    at = bass.ds(m * 4 + q, 1)
                    tt(st[:, 0, d:d + 1, at], one_st[0], one_st[1], ALU.subtract)
                    one(tt(st[:, 1, d:d + 1, at], one_st[2], one_st[3], ALU.add))
                dve.wait_ge(prod_used, m * UNITS + UNITS)
                dve.tensor_copy(dnow[:], dcol[:, bass.ds(m, 1)]).then_inc(y_done, 1)
                dve.wait_ge(y_done, m * 2 + 1)
                one(dve.scalar_tensor_tensor(out=y[:], in0=ucur[:], scalar=dnow[:],
                                             in1=ps[:, Y0:Y0 + TOK], op0=ALU.mult, op1=ALU.add))
                dve.sem_inc(y_done, 1)


def s5_gate(nc, T, ps, G, MIXT):
    with stage(nc, "w_in", "mm_done", "sig_done", "bank_free") as (
            ctx, (w_in, mm_done, sig_done, bank_free)):
        w = buf(ctx, nc, "glu_w", [P, 4, 4 * P])
        bcol = buf(ctx, nc, "glu_b", [P, 4])
        sig = buf(ctx, nc, "glu_gate", [P, 4, TOK])
        block = ctx.enter_context(nc.Block())

        @block.sync
        def _(sp):
            sp.dma_start(w[:], T["glu_w"]).then_inc(w_in, 16)
            sp.dma_start(bcol[:], T["glu_b"]).then_inc(w_in, 16)
            sp.wait_ge(w_in, 32)

        @block.tensor
        def _(pe):
            pe.wait_ge(w_in, 32)
            for m in range(4):
                at = 2 * m * HALF
                for k in range(4):
                    lhs = w[:, k, m * P:(m + 1) * P]
                    pe.matmul(ps[:, at:at + HALF], lhs, G[:, k, 0:HALF], start=(k == 0), stop=(k == 3))
                    mm = pe.matmul(ps[:, at + HALF:at + TOK], lhs, G[:, k, HALF:TOK],
                                   start=(k == 0), stop=(k == 3))
                mm.then_inc(mm_done, 1)

        @block.scalar
        def _(act):
            for m in range(4):
                act.wait_ge(mm_done, m + 1)
                act.activation(sig[:, m, :], ps[:, 2 * m * HALF:2 * m * HALF + TOK], ACT.Sigmoid,
                               bias=bcol[:, m:m + 1]).then_inc(sig_done, 1)

        @block.vector
        def _(dve):
            for m in range(4):
                dve.wait_ge(sig_done, m + 1)
                dve.tensor_tensor(MIXT[:, 4 + m, :], sig[:, m, :], G[:, m, :],
                                  ALU.mult).then_inc(bank_free, 1)
            dve.wait_ge(bank_free, 4)


def project_out(nc, ps, MIXT, W, X, mod, layer, g_chunk):
    with stage(nc, "w_in", "g_in", "mm_done", "bank_free", "dve_line") as (
            ctx, (w_in, g_in, mm_done, bank_free, dve_line)):
        w = buf(ctx, nc, "w_out", [P, KD, D])
        g_row = buf(ctx, nc, "gate_row", [P, 2, D])
        tmp = buf(ctx, nc, "gated", [P, 2, HALF])
        block = ctx.enter_context(nc.Block())

        @block.sync
        def _(sp):
            sp.dma_start(w[:], W).then_inc(w_in, 16)
            for g in range(2):
                sp.dma_start(g_row[:, g, :], mod[layer, g, g_chunk * D:(g_chunk + 1) * D]
                             .partition_broadcast(P)).then_inc(g_in, 16)

        @block.tensor
        def _(pe):
            pe.wait_ge(w_in, 16)
            for n in range(2 * NT):
                t, c = n // 2, n % 2
                if n >= 4:
                    pe.wait_ge(bank_free, n - 3)
                at = (n % 4) * HALF
                for k in range(KD):
                    mm = pe.matmul(ps[:, at:at + HALF], MIXT[:, k, t * P:(t + 1) * P],
                                   w[:, k, c * HALF:(c + 1) * HALF], start=(k == 0), stop=(k == KD - 1))
                mm.then_inc(mm_done, 1)

        @block.vector
        def _(dve):
            dve.wait_ge(g_in, 32)
            for n in range(2 * NT):
                t, c = n // 2, n % 2
                dve.wait_ge(mm_done, n + 1)
                at = (n % 4) * HALF
                col = slice(c * HALF, (c + 1) * HALF)
                dve.tensor_tensor(tmp[:, c, :], ps[:, at:at + HALF], g_row[:, group_of(t), col],
                                  ALU.mult).then_inc(bank_free, 1)
                dve.wait_ge(bank_free, n + 1)
                dve.tensor_tensor(X[:, t, col], X[:, t, col], tmp[:, c, :], ALU.add
                                  ).then_inc(dve_line, 1)
            dve.wait_ge(dve_line, 2 * NT)


MLH = 8
VN = P + 1
KINDS = 4
ML_UNITS = ((0, 0), (1, 0), (0, 1), (1, 4), (0, 2), (1, 3), (0, 3), (1, 2), (0, 4), (1, 1))
NU = len(ML_UNITS)


def mlstm_conv(nc, T, QK):
    blocks = 2 * MLH
    with stage(nc, "taps_in", "conv_done", "silu_done", "dve_line") as (
            ctx, (taps_in, conv_done, silu_done, dve_line)):
        taps = buf(ctx, nc, "conv_taps", [P, blocks, 4])
        cur = buf(ctx, nc, "conv_taps_cur", [P, 4])
        x = buf(ctx, nc, "conv_source", [P, TOK])
        y = buf(ctx, nc, "conv_block", [P, 2, TOK])
        block = ctx.enter_context(nc.Block())

        @block.sync
        def _(sp):
            sp.dma_start(taps[:], T["ml_taps"]).then_inc(taps_in, 16)

        @block.vector
        def _(dve):
            line = Line(dve, dve_line)
            dve.wait_ge(taps_in, 16)
            dve.sem_inc(silu_done, 2)
            with line.loop(0, blocks // 2, 8) as i:
                for b in range(2):
                    dve.tensor_copy(x[:, :].unsqueeze(1), QK[:, bass.ds(i * 2 + b, 1), :])
                    line.then(dve.tensor_copy(cur[:, :].unsqueeze(1),
                                              taps[:, bass.ds(i * 2 + b, 1), :]))
                    dve.wait_ge(silu_done, i * 2 + (b + 1))
                    short_conv(dve, line, y[:, b, :], x[:, :], lambda k: cur[:, k:k + 1])
                    dve.sem_inc(conv_done, 1)
            dve.wait_ge(silu_done, blocks + 2)
            line.then(dve.tensor_scalar(QK[:, 0:MLH, :], QK[:, 0:MLH, :], float(P) ** -0.5, None,
                                        ALU.mult))

        @block.scalar
        def _(act):
            with act.Fori(0, blocks // 2) as i:
                for b in range(2):
                    act.wait_ge(conv_done, i * 2 + (b + 1))
                    act.activation(QK[:, bass.ds(i * 2 + b, 1), :], y[:, b, :].unsqueeze(1),
                                   ACT.Silu).then_inc(silu_done, 1)


def project_tokens(nc, ps, HT, W, place):
    with stage(nc, "w_in0", "w_in1", "mm_done", "out_done") as (
            ctx, (w_in0, w_in1, mm_done, out_done)):
        w_in = (w_in0, w_in1)
        w = buf(ctx, nc, "w_block", [P, 2, KD * HALF])
        block = ctx.enter_context(nc.Block())

        @block.sync
        def _(sp):
            for c in range(2):
                sp.dma_start(w[:, c, :], W[c]).then_inc(w_in[c], 16)

        @block.tensor
        def _(pe):
            for n in range(2 * NT):
                c, t = n // NT, n % NT
                if t == 0:
                    pe.wait_ge(w_in[c], 16)
                if n >= 4:
                    pe.wait_ge(out_done, n - 3)
                at = (n % 4) * HALF
                for k in range(KD):
                    mm = pe.matmul(ps[:, at:at + HALF], HT[:, k, t * P:(t + 1) * P],
                                   w[:, c, k * HALF:(k + 1) * HALF], start=(k == 0), stop=(k == KD - 1))
                mm.then_inc(mm_done, 1)

        @block.scalar
        def _(act):
            for n in range(2 * NT):
                act.wait_ge(mm_done, n + 1)
                at = (n % 4) * HALF
                act.activation(place(n % NT, n // NT), ps[:, at:at + HALF]
                               .rearrange("p (h v) -> p h v", v=P), ACT.Copy).then_inc(out_done, 1)


def mlstm_gates(nc, T, ps, HT, ident, negM, COLS, KEEP, out_m):
    R = 2 * TOK
    with stage(nc, "in_done", "mm_done", "raw_ready", "abs_done", "e_ready", "ln_done", "x_ready",
               "exp_done", "dve_line", "turned", "m_out") as (
            ctx, (in_done, mm_done, raw_ready, abs_done, e_ready, ln_done, x_ready, exp_done,
                  dve_line, turned, m_out)):
        wg = buf(ctx, nc, "gate_w", [P, KD, 4 * MLH])
        gb = buf(ctx, nc, "gate_b", [MLH, 4])
        m0 = buf(ctx, nc, "m_cached", [MLH, 2])
        raw = buf(ctx, nc, "gate_raw", [MLH, 4, TOK])
        e = buf(ctx, nc, "gate_exp", [MLH, 2, TOK])
        ig = buf(ctx, nc, "gate_i", [MLH, 2, TOK])
        lf = buf(ctx, nc, "gate_logf", [MLH, 2, TOK])
        keepers = buf(ctx, nc, "chunk_keep", [MLH, R])
        drop = buf(ctx, nc, "chunk_drop", [MLH, R])
        b = buf(ctx, nc, "gate_b_sum", [MLH, R])
        w = buf(ctx, nc, "gate_w_row", [MLH, R])
        M = buf(ctx, nc, "gate_max", [MLH, R])
        mp = buf(ctx, nc, "m_before", [MLH, 2, NT])
        ML = buf(ctx, nc, "M_last", [MLH, 2, NT])
        mn = buf(ctx, nc, "m_after", [MLH, 2, NT])
        kp = buf(ctx, nc, "state_keep", [MLH, 2 * NT])
        X4 = buf(ctx, nc, "gate_args", [MLH, 3, R])
        nat = buf(ctx, nc, "gate_rows", [MLH, KINDS, 2, TOK])
        diag = buf(ctx, nc, "keep_diag", [MLH, 2 * NT, MLH])
        ones8 = buf(ctx, nc, "ones8", [MLH, P])
        block = ctx.enter_context(nc.Block())
        chunks = lambda a: a.rearrange("h (c s) -> h c s", s=P)

        @block.sync
        def _(sp):
            for dst, src in ((wg, "gate_w"), (gb, "gate_b"), (m0, "ml_m0")):
                sp.dma_start(dst[:], T[src]).then_inc(in_done, 16)
            sp.wait_ge(x_ready, 1)
            sp.dma_start(out_m[0].unsqueeze(1), mn[:, 0, 0:1],
                         allow_slow_non_contiguous=True).then_inc(m_out, 16)
            sp.dma_start(out_m[1].unsqueeze(1), mn[:, 1, NT - 1:NT],
                         allow_slow_non_contiguous=True).then_inc(m_out, 16)
            sp.wait_ge(m_out, 32)

        @block.tensor
        def _(pe):
            pe.wait_ge(in_done, 48)
            for j in range(4):
                at = 2 * j * HALF
                for k in range(KD):
                    lhs = wg[:, k, j * MLH:(j + 1) * MLH]
                    pe.matmul(ps[0:MLH, at:at + HALF], lhs, HT[:, k, 0:HALF],
                              start=(k == 0), stop=(k == KD - 1))
                    mm = pe.matmul(ps[0:MLH, at + HALF:at + TOK], lhs, HT[:, k, HALF:TOK],
                                   start=(k == 0), stop=(k == KD - 1))
                mm.then_inc(mm_done, 1)
            pe.wait_ge(exp_done, 2)
            for kind in range(KINDS):
                for d in range(2):
                    for t in range(NT):
                        at = ((kind * 2 + d) * NT + t) * MLH
                        mm = pe.transpose(ps[:, at:at + MLH], nat[:, kind, d, t * P:(t + 1) * P],
                                          ident[0:MLH, 0:MLH])
            mm.then_inc(turned, 1)
            pe.matmul(ps[:, HALF:HALF + 2 * NT * MLH], ones8[:],
                      diag[:, :, :].rearrange("h c g -> h (c g)"), start=True, stop=True
                      ).then_inc(turned, 1)

        @block.scalar
        def _(act):
            act.wait_ge(raw_ready, 1)
            act.activation(e[:], raw[:, 2:4, :], ACT.Abs).then_inc(abs_done, 1)
            act.wait_ge(abs_done, 1)
            act.activation(e[:], e[:], ACT.Exp, scale=-1.0).then_inc(abs_done, 1)
            act.wait_ge(e_ready, 1)
            act.activation(e[:], e[:], ACT.Ln).then_inc(ln_done, 1)
            act.wait_ge(x_ready, 1)
            act.activation(X4[:], X4[:], ACT.Exp).then_inc(exp_done, 1)
            act.activation(kp[:], kp[:], ACT.Exp).then_inc(abs_done, 1)

        @block.vector
        def _(dve):
            line = Line(dve, dve_line)
            one, tt, ts = line.then, dve.tensor_tensor, dve.tensor_scalar
            one(dve.memset(keepers[:], 1.0))
            one(dve.memset(drop[:], 0.0))
            dve.memset(chunks(keepers[:, :])[:, :, 0:1], 0.0)
            dve.memset(chunks(drop[:, :])[:, :, 0:1], LOWEST)
            one(dve.memset(ones8[:], 1.0))
            dve.wait_ge(in_done, 48)
            for j in range(4):
                dve.wait_ge(mm_done, j + 1)
                at = 2 * j * HALF
                one(ts(raw[:, j, :], ps[0:MLH, at:at + TOK], gb[:, j:j + 1], None, ALU.add))
            dve.sem_inc(raw_ready, 1)
            dve.wait_ge(abs_done, 2)
            one(ts(e[:], e[:], 1.0, None, ALU.add))
            dve.sem_inc(e_ready, 1)
            dve.wait_ge(ln_done, 1)
            for d in range(2):
                way = (lambda a: a) if d == 0 else (lambda a: a[:, ::-1])
                one(dve.scalar_tensor_tensor(out=lf[:, d, :], in0=way(raw[:, 2 + d, :]), scalar=0.0,
                                             in1=way(e[:, d, :]), op0=ALU.min, op1=ALU.subtract))
                one(dve.tensor_copy(ig[:, d, :], way(raw[:, d, :])))
            flat = lambda a: a[:, :, :].rearrange("h d s -> h (d s)")
            one(dve.tensor_tensor_scan(b[:], keepers[:], flat(lf), 0.0, ALU.mult, ALU.add))
            one(tt(w[:], flat(ig), b[:], ALU.subtract))
            one(dve.tensor_tensor_scan(M[:], drop[:], w[:], LOWEST, ALU.add, ALU.max))
            last = lambda a, c: chunks(a[:, :])[:, c, P - 1:P]
            one(dve.memset(mp[:], 0.0))
            one(dve.tensor_copy(mp[:, 0, 1:2], m0[:, 0:1]))
            one(dve.tensor_copy(mp[:, 1, 0:1], m0[:, 1:2]))
            for d in range(2):
                for c, after in (((0, None), (1, 2), (2, 3), (3, 4), (4, None)),
                                 ((4, None), (0, 1), (1, 2), (2, 3), (3, None)))[d]:
                    one(tt(ML[:, d, c:c + 1], mp[:, d, c:c + 1], last(M, d * NT + c), ALU.max))
                    one(tt(mn[:, d, c:c + 1], ML[:, d, c:c + 1], last(b, d * NT + c), ALU.add))
                    if after is not None:
                        one(dve.tensor_copy(mp[:, d, after:after + 1], mn[:, d, c:c + 1]))
            wide = [MLH, 2 * NT, P]
            flat2 = lambda a: a[:, :, :].rearrange("h d c -> h (d c)")
            mpw = flat2(mp).unsqueeze(2).to_broadcast(wide)
            mlw = flat2(ML).unsqueeze(2).to_broadcast(wide)
            one(tt(chunks(M[:, :]), chunks(M[:, :]), mpw, ALU.max))
            one(tt(chunks(X4[:, 0, :]), chunks(w[:, :]), mlw, ALU.subtract))
            one(tt(chunks(X4[:, 1, :]), mpw, chunks(M[:, :]), ALU.subtract))
            one(dve.scalar_tensor_tensor(out=X4[:, 2, :], in0=b[:], scalar=-1.0, in1=M[:],
                                         op0=ALU.mult, op1=ALU.subtract))
            one(tt(kp[:], flat2(mp), flat2(ML), ALU.subtract))
            dve.sem_inc(x_ready, 1)
            one(ts(M[:], M[:], -1.0, None, ALU.mult))
            dve.wait_ge(exp_done, 1)
            dve.wait_ge(abs_done, 3)
            rows = [w[:, :]] + [X4[:, j, :] for j in range(3)]
            for d in range(2):
                way = (lambda a: a) if d == 0 else (lambda a: a[:, ::-1])
                for kind, row in enumerate(rows):
                    one(dve.tensor_copy(nat[:, kind, d, :], way(row[:, d * TOK:(d + 1) * TOK])))
                one(dve.tensor_copy(negM[:, d, :], way(M[:, d * TOK:(d + 1) * TOK])))
            w8 = [MLH, 2 * NT, MLH]
            one(tt(diag[:], ident[0:MLH, 0:MLH].unsqueeze(1).to_broadcast(w8),
                   kp[:, :].unsqueeze(2).to_broadcast(w8), ALU.mult))
            dve.sem_inc(exp_done, 1)
            dve.wait_ge(turned, 2)
            one(dve.tensor_copy(COLS[:, :, :].rearrange("p c h -> p (c h)"),
                                ps[:, 0:KINDS * 2 * NT * MLH]))
            one(dve.tensor_copy(KEEP[:, :, :].rearrange("p c h -> p (c h)"),
                                ps[:, HALF:HALF + 2 * NT * MLH]))


def turn_keys(nc, ps, QK, KT, ident):
    with stage(nc, "turned", "out_done") as (ctx, (turned, out_done)):
        block = ctx.enter_context(nc.Block())

        @block.tensor
        def _(pe):
            for n in range(2 * NT):
                t, q = n // 2, n % 2
                if n >= 4:
                    pe.wait_ge(out_done, n - 3)
                for h in range(4):
                    at = (n % 4) * HALF + h * P
                    mm = pe.transpose(ps[:, at:at + P], QK[:, MLH + 4 * q + h, t * P:(t + 1) * P],
                                      ident[:])
                mm.then_inc(turned, 1)

        @block.scalar
        def _(act):
            for n in range(2 * NT):
                t, q = n // 2, n % 2
                act.wait_ge(turned, n + 1)
                at = (n % 4) * HALF
                act.activation(KT[:, t, 4 * q:4 * q + 4, :], ps[:, at:at + HALF]
                               .rearrange("p (h v) -> p h v", v=P), ACT.Copy).then_inc(out_done, 1)


def mlstm_cells(nc, T, ps, QK, KT, VX, HM, negM, COLS, KEEP, ident, out_C, out_n):
    with stage(nc, "cn_in", "v_ones", "mask_line", "mask_done", "head_set", "head_copied",
               "first_done", "exp_done", "st_done", "second_done", "tail_done", "dve_line",
               "state_out") as (
            ctx, (cn_in, v_ones, mask_line, mask_done, head_set, head_copied, first_done, exp_done,
                  st_done, second_done, tail_done, dve_line, state_out)):
        CN0 = buf(ctx, nc, "state_cached", [P, 2, MLH, VN])
        CNo = buf(ctx, nc, "state_ctx", [P, 2, MLH, VN])
        CN = buf(ctx, nc, "state", [P, 2, VN])
        mask = buf(ctx, nc, "mask", [P, 2, P])
        ones8 = buf(ctx, nc, "ones8", [MLH, P])
        q = buf(ctx, nc, "q_head", [P, TOK])
        k = buf(ctx, nc, "k_head", [P, TOK])
        v = buf(ctx, nc, "v_head", [P, NT, VN])
        nm = buf(ctx, nc, "negM_head", [MLH, 2, TOK])
        cols = buf(ctx, nc, "cols_head", [P, KINDS * 2 * NT, 1])
        keep = buf(ctx, nc, "keep_head", [P, 2 * NT, 1])
        E = buf(ctx, nc, "weights", [P, 2, P])
        ST = buf(ctx, nc, "scores_T", [P, 2, P])
        kw = buf(ctx, nc, "k_weighted", [P, 2, P])
        nd = buf(ctx, nc, "num_den", [P, VN])
        den = buf(ctx, nc, "den", [P, 1])
        block = ctx.enter_context(nc.Block())

        def bank(d, n):
            return (4 * d + n) * HALF

        def col(kind, d, t):
            c = (kind * 2 + d) * NT + t
            return cols[:, c, :]

        @block.sync
        def _(sp):
            sp.dma_start(CN0[:], T["ml_CN0"]).then_inc(cn_in, 16)
            sp.wait_ge(tail_done, MLH * NU)
            for d in range(2):
                sp.dma_start(out_C[d].rearrange("h k v -> k h v"), CNo[:, d, :, 0:P]
                             ).then_inc(state_out, 16)
                sp.dma_start(out_n[d].rearrange("h k -> k h").unsqueeze(2), CNo[:, d, :, P:VN],
                             allow_slow_non_contiguous=True).then_inc(state_out, 16)
            sp.wait_ge(state_out, 64)

        @block.gpsimd
        def _(pool):
            pool.memset(VX[:, :, :, P:VN], 1.0).then_inc(v_ones, 1)
            pool.memset(ones8[:], 1.0).then_inc(mask_line, 1)
            pool.memset(mask[:], 0.0).then_inc(mask_line, 1)
            pool.wait_ge(mask_line, 2)
            for d, way in ((0, 1), (1, -1)):
                pool.affine_select(out=mask[:, d, :], in_=mask[:, d, :], compare_op=ALU.is_ge,
                                   fill=-1.0e30, base=0, pattern=[[way, P]],
                                   channel_multiplier=-way).then_inc(mask_done, 1)
            pool.wait_ge(mask_done, 2)
            pool.wait_ge(v_ones, 1)

        @block.scalar
        def _(act):
            act.wait_ge(v_ones, 1)
            with act.Fori(0, MLH) as h:
                act.wait_ge(tail_done, h * NU + 1)
                act.activation(q[:, :].unsqueeze(1), QK[:, bass.ds(h, 1), :], ACT.Copy)
                act.activation(k[:, :].unsqueeze(1), QK[:, bass.ds(h + MLH, 1), :], ACT.Copy)
                act.activation(v[:, :, :].unsqueeze(2), VX[:, :, bass.ds(h, 1), :], ACT.Copy
                               ).then_inc(head_copied, 1)
                for n, (d, t) in enumerate(ML_UNITS):
                    act.wait_ge(first_done, h * NU + (n + 1))
                    if n == 0:
                        act.wait_ge(head_set, h + 1)
                    act.activation(E[:, d, :], ps[:, bank(d, 0):bank(d, 0) + P], ACT.Exp,
                                   bias=col(0, d, t)).then_inc(exp_done, 1)

        @block.tensor
        def _(pe):
            pe.wait_ge(mask_done, 2)

            def first(h, n):
                d, t = ML_UNITS[n]
                pe.wait_ge(tail_done, h * NU + n) if n >= 2 else None
                at = bank(d, 0)
                tile = slice(t * P, (t + 1) * P)
                pe.matmul(ps[:, at:at + P], ident[:], mask[:, d, :], start=True, stop=False)
                pe.matmul(ps[:, at:at + P], ones8[:], nm[:, d, tile], start=False, stop=True)
                pe.matmul(ps[:, at + P:at + 2 * P], k[:, tile], q[:, tile], start=True, stop=True)
                at = bank(d, 1)
                pe.matmul(ps[:, at:at + VN], q[:, tile], CN[:, d, :], start=True, stop=True
                          ).then_inc(first_done, 1)

            def second(h, n):
                d, t = ML_UNITS[n]
                pe.wait_ge(st_done, h * NU + (n + 1))
                at = bank(d, 2)
                pe.matmul(ps[:, at:at + VN], ST[:, d, :], v[:, t, :], start=True, stop=True)
                at = bank(d, 3)
                pe.matmul(ps[:, at:at + VN], kw[:, d, :], v[:, t, :], start=True, stop=True
                          ).then_inc(second_done, 1)

            with pe.Fori(0, MLH) as h:
                pe.wait_ge(head_set, h + 1)
                pe.wait_ge(head_copied, h + 1)
                for n in range(NU):
                    first(h, n)
                    if n:
                        second(h, n - 1)
                second(h, NU - 1)

        @block.vector
        def _(dve):
            line = Line(dve, dve_line)
            one, tt, ts = line.then, dve.tensor_tensor, dve.tensor_scalar
            dve.wait_ge(cn_in, 16)
            dve.sem_inc(tail_done, 1)

            def tail(h, n):
                d, t = ML_UNITS[n]
                dve.wait_ge(second_done, h * NU + (n + 1))
                c = d * NT + (t if d == 0 else NT - 1 - t)
                s0, s1, s2 = bank(d, 1), bank(d, 2), bank(d, 3)
                one(dve.scalar_tensor_tensor(out=CN[:, d, :], in0=CN[:, d, :], scalar=keep[:, c, :],
                                             in1=ps[:, s2:s2 + VN], op0=ALU.mult, op1=ALU.add))
                if t == 0:
                    one(dve.tensor_copy(CNo[:, d, bass.ds(h, 1), :], CN[:, d, :].unsqueeze(1)))
                    one(dve.tensor_copy(CN[:, d, :].unsqueeze(1), CN0[:, d, bass.ds(h, 1), :]))
                one(ts(nd[:], ps[:, s0:s0 + VN], col(2, d, t), None, ALU.mult))
                one(tt(nd[:], nd[:], ps[:, s1:s1 + VN], ALU.add))
                one(dve.scalar_tensor_tensor(out=den[:], in0=nd[:, P:VN], scalar=-1.0,
                                             in1=nd[:, P:VN], op0=ALU.mult, op1=ALU.max))
                one(ts(den[:], den[:], col(3, d, t), None, ALU.max))
                one(dve.reciprocal(den[:], den[:]))
                out = HM[:, t, bass.ds(h, 1), :]
                row = nd[:, 0:P].unsqueeze(1)
                if (d, t) in ((0, 0), (0, 1), (0, 2), (1, 4), (1, 3)):
                    one(ts(out, row, den[:, 0:1], None, ALU.mult))
                else:
                    one(dve.scalar_tensor_tensor(out=out, in0=row, scalar=den[:, 0:1], in1=out,
                                                 op0=ALU.mult, op1=ALU.add))
                dve.sem_inc(tail_done, 1)

            per = 3 + NU * (1 + 7) + 2 * 2
            with line.loop(0, MLH, per) as h:
                one(ts(nm[:], negM[:], ident[0:MLH, bass.ds(h, 1)], None, ALU.mult))
                dve.tensor_copy(cols[:], COLS[:, :, bass.ds(h, 1)])
                one(dve.tensor_copy(keep[:], KEEP[:, :, bass.ds(h, 1)]))
                one(dve.memset(CN[:], 0.0))
                dve.sem_inc(head_set, 1)
                for n, (d, t) in enumerate(ML_UNITS):
                    dve.wait_ge(exp_done, h * NU + (n + 1))
                    if n >= 2:
                        dve.wait_ge(second_done, h * NU + (n - 1))
                    at = bank(d, 0) + P
                    tt(ST[:, d, :], ps[:, at:at + P], E[:, d, :], ALU.mult)
                    one(ts(kw[:, d, :].unsqueeze(1), KT[:, t, bass.ds(h, 1), :], col(1, d, t), None,
                           ALU.mult))
                    dve.sem_inc(st_done, 1)
                    if n:
                        tail(h, n - 1)
                tail(h, NU - 1)


def mlstm_finish(nc, T, ps, HM, O, MIXT, ident):
    with stage(nc, "g_in", "silu_done", "ms_ready", "rooted", "dve_line", "h_ready", "turned",
               "out_done") as (ctx, (g_in, silu_done, ms_ready, rooted, dve_line, h_ready, turned,
                                     out_done)):
        g = buf(ctx, nc, "norm_row", [P, D])
        sq = buf(ctx, nc, "squares", [P, MLH, P])
        ms = buf(ctx, nc, "mean_square", [P, NT, MLH])
        block = ctx.enter_context(nc.Block())

        @block.sync
        def _(sp):
            sp.dma_start(g[:], T["ml_norm_g"].partition_broadcast(P)).then_inc(g_in, 16)

        @block.scalar
        def _(act):
            for t in range(NT):
                act.activation(O[:, t, :], O[:, t, :], ACT.Silu).then_inc(silu_done, 1)
            act.wait_ge(ms_ready, 1)
            act.activation(ms[:], ms[:], ACT.Sqrt).then_inc(rooted, 1)
            for n in range(2 * NT):
                t, q = n // 2, n % 2
                act.wait_ge(turned, n + 1)
                at = (n % 4) * HALF
                act.activation(MIXT[:, 4 * q:4 * q + 4, t * P:(t + 1) * P], ps[:, at:at + HALF]
                               .rearrange("p (k c) -> p k c", k=4), ACT.Copy).then_inc(out_done, 1)

        @block.vector
        def _(dve):
            line = Line(dve, dve_line)
            one, tt = line.then, dve.tensor_tensor
            for t in range(NT):
                one(tt(sq[:], HM[:, t], HM[:, t], ALU.mult))
                one(dve.tensor_reduce(ms[:, t, :], sq[:], AX.X, ALU.add))
            one(dve.tensor_scalar(ms[:], ms[:], 1.0 / P, EPS, ALU.mult, ALU.add))
            dve.reciprocal(ms[:], ms[:]).then_inc(ms_ready, 1)
            dve.wait_ge(rooted, 1)
            dve.wait_ge(g_in, 16)
            dve.wait_ge(silu_done, NT)
            for t in range(NT):
                flat = HM[:, t].rearrange("p h v -> p (h v)")
                one(tt(HM[:, t], HM[:, t], ms[:, t, :].unsqueeze(2).to_broadcast([P, MLH, P]),
                       ALU.mult))
                one(tt(flat, flat, g[:], ALU.mult))
                tt(flat, flat, O[:, t, :], ALU.mult).then_inc(h_ready, 1)

        @block.tensor
        def _(pe):
            for n in range(2 * NT):
                t, q = n // 2, n % 2
                pe.wait_ge(h_ready, t + 1)
                if n >= 4:
                    pe.wait_ge(out_done, n - 3)
                for k in range(4):
                    at = (n % 4) * HALF + k * P
                    mm = pe.transpose(ps[:, at:at + P], HM[:, t, 4 * q + k, :], ident[:])
                mm.then_inc(turned, 1)


def finish(nc, T, X, out):
    with stage(nc, "g_in", "squared", "ms_ready", "rooted", "y_ready", "dve_line", "y_out") as (
            ctx, (g_in, squared, ms_ready, rooted, y_ready, dve_line, y_out)):
        g = buf(ctx, nc, "final_row", [P, D])
        junk = buf(ctx, nc, "squares", [P, D])
        ms = buf(ctx, nc, "mean_square", [P, NT])
        block = ctx.enter_context(nc.Block())

        @block.sync
        def _(sp):
            sp.dma_start(g[:], T["final_g"].partition_broadcast(P)).then_inc(g_in, 16)
            for t in range(NT):
                sp.wait_ge(y_ready, t + 1)
                sp.dma_start(out[t * P:(t + 1) * P, :], X[:, t, :]).then_inc(y_out, 16)
            sp.wait_ge(y_out, 16 * NT)

        @block.scalar
        def _(act):
            for t in range(NT):
                act.activation(junk[:], X[:, t, :], ACT.Square,
                               accum_out=ms[:, t:t + 1]).then_inc(squared, 1)
                act.wait_ge(squared, t + 1)
            act.wait_ge(ms_ready, 1)
            act.activation(ms[:], ms[:], ACT.Sqrt).then_inc(rooted, 1)

        @block.vector
        def _(dve):
            line = Line(dve, dve_line)
            dve.wait_ge(squared, NT)
            line.then(dve.tensor_scalar(ms[:], ms[:], 1.0 / D, EPS, ALU.mult, ALU.add))
            dve.reciprocal(ms[:], ms[:]).then_inc(ms_ready, 1)
            dve.wait_ge(rooted, 1)
            dve.wait_ge(g_in, 16)
            for t in range(NT):
                dve.scalar_tensor_tensor(out=X[:, t, :], in0=X[:, t, :], scalar=ms[:, t:t + 1],
                                         in1=g[:], op0=ALU.mult, op1=ALU.mult).then_inc(y_ready, 1)



def trunk(nc, T, O, upto=99, dbg=None):
    mod = nc.dram_tensor("mod_rows_dram", [2, 2, 6 * D], F32, kind="Internal").ap()
    with ExitStack() as ctx:
        ps = ctx.enter_context(nc.psum_tensor("banks", [P, 8 * HALF], F32))
        X = buf(ctx, nc, "X", [P, NT, D])
        ident = buf(ctx, nc, "ident", [P, P])
        load_and_modulate(nc, T, ps, X, ident, mod)

        def peer(layer):
            with ExitStack() as c1:
                H = buf(c1, nc, "H", [P, NT, D])
                idx = buf(c1, nc, "expert", [P, NT, SLOTS], U32)
                gate = buf(c1, nc, "expert_gate", [P, NT, SLOTS])
                with ExitStack() as c2:
                    QT = buf(c2, nc, "QT", [P, CODES, TOK])
                    with ExitStack() as c3:
                        HT = buf(c3, nc, "HT", [P, KD, TOK])
                        norm_modulate(nc, ps, X, H, HT, ident, mod, T["norm_g"][layer, 1], layer, 3, 4)
                        project_channels(nc, ps, HT, T[f"pk_w_q{layer}"], QT, CODES)
                    choose_experts(nc, T, ps, QT, idx, gate, layer)
                    if dbg: dbg(nc, "idx", idx); dbg(nc, "gate", gate); dbg(nc, "H", H)
                apply_experts(nc, ps, H, X, mod, idx, gate, T[f"pk_u{layer}"], T[f"pk_v{layer}"],
                              layer, 5)
        if upto == 1:
            peer(0)
            dbg(nc, "X", X)
            return
        with ExitStack() as c1:
            MIXT = buf(c1, nc, "MIXT", [P, KD, TOK])
            US = buf(c1, nc, "US", [P, 4, TOK])
            with ExitStack() as c0:
                KC = buf(c0, nc, "KC", [P, NT, 2, HYW])
                KS = buf(c0, nc, "KS", [P, NT, 2, HYW])
                with ExitStack() as c2:
                    hyena_filters(nc, T, ps, KC, KS)
                VG = buf(c0, nc, "VG", [P, NT, 3 * HYW])
                with ExitStack() as c2:
                    HT = buf(c2, nc, "HT", [P, KD, TOK])
                    with ExitStack() as c3:
                        H = buf(c3, nc, "H", [P, NT, D])
                        norm_modulate(nc, ps, X, H, HT, ident, mod, T["norm_g"][0, 0], 0, 0, 1)
                    project_channels(nc, ps, HT, T["ev_w_in"][12:16], US, 4)
                    PH = buf(c2, nc, "PH", [P, 12, TOK])
                    project_channels(nc, ps, HT, T["ev_w_in"][0:12], PH, 12)
                    hyena_inputs(nc, T, ps, PH, VG, ident)
                if dbg: dbg(nc, "KC", KC); dbg(nc, "KS", KS); dbg(nc, "VG", VG)
                hyena_convolve(nc, T, ps, VG, KC, KS, MIXT, ident)
                if dbg: dbg(nc, "MIXT", MIXT[:, 0:4, :])
            G = buf(c1, nc, "G", [P, 4, TOK])
            s5(nc, T, ps, US, G, ident, O["s5_re"], O["s5_im"])
            s5_gate(nc, T, ps, G, MIXT)
            if dbg: dbg(nc, "MIXS", MIXT[:, 4:8, :])
            project_out(nc, ps, MIXT, T["ev_w_out"], X, mod, 0, 2)
        if upto == 2:
            return
        if upto != 3:
            peer(0)
        with ExitStack() as c1:
            negM = buf(c1, nc, "negM", [MLH, 2, TOK])
            COLS = buf(c1, nc, "COLS", [P, KINDS * 2 * NT, MLH])
            KEEP = buf(c1, nc, "KEEP", [P, 2 * NT, MLH])
            with ExitStack() as c2:
                HT = c2.enter_context(nc.sbuf_tensor(numbered("HT"), [P, KD, TOK], F32,
                                                     side="right"))
                with ExitStack() as c3:
                    H = buf(c3, nc, "H", [P, NT, D])
                    norm_modulate(nc, ps, X, H, HT, ident, mod, T["norm_g"][1, 0], 1, 0, 1)
                mlstm_gates(nc, T, ps, HT, ident, negM, COLS, KEEP, O["ml_m"])
                QK = buf(c1, nc, "QK", [P, 2 * MLH, TOK])
                VX = buf(c1, nc, "VX", [P, NT, MLH, VN])
                O_ = buf(c1, nc, "Ogate", [P, NT, D])
                project_channels(nc, ps, HT, T["od_w_qk"], QK, 2 * MLH)
                project_tokens(nc, ps, HT, T["od_w_vo"][0:2],
                               lambda t, c: VX[:, t, 4 * c:4 * c + 4, 0:P])
                project_tokens(nc, ps, HT, T["od_w_vo"][2:4],
                               lambda t, c: O_[:, t, c * HALF:(c + 1) * HALF]
                               .rearrange("p (h v) -> p h v", v=P))
            mlstm_conv(nc, T, QK)
            with ExitStack() as c2:
                HM = buf(c2, nc, "HM", [P, NT, MLH, P])
                with ExitStack() as c3:
                    KT = buf(c3, nc, "KT", [P, NT, MLH, P])
                    turn_keys(nc, ps, QK, KT, ident)
                    mlstm_cells(nc, T, ps, QK, KT, VX, HM, negM, COLS, KEEP, ident, O["ml_C"],
                                O["ml_n"])
                MIXT = buf(c2, nc, "MIXT", [P, KD, TOK])
                if dbg: dbg(nc, "HM", HM)
                mlstm_finish(nc, T, ps, HM, O_, MIXT, ident)
                if dbg: dbg(nc, "Xb", X)
                project_out(nc, ps, MIXT, T["od_w_out"], X, mod, 1, 2)
                if dbg: dbg(nc, "Xa", X)
        if upto == 3:
            return
        peer(1)
        finish(nc, T, X, O["y"])


OUTS = {"y": [TOK, D], "s5_re": [2, 32, 64], "s5_im": [2, 32, 64], "ml_C": [2, 8, P, P],
        "ml_n": [2, 8, P], "ml_m": [2, 8]}


def host_arrays(inp):
    f = np.float32

    def slices(w, width):
        n = w.shape[1] // width
        return np.ascontiguousarray(w.reshape(KD, P, n, width).transpose(2, 1, 0, 3)).reshape(n, P, KD * width)

    a = {}
    a["cond"] = np.stack([inp["c_ctx"], inp["c"][0]], -1).reshape(KD, P, 2).transpose(1, 0, 2)
    a["ada_w"] = np.concatenate([slices(inp["ada_w"][l], HALF) for l in range(2)])
    a["ada_b"] = inp["ada_b"].reshape(1, -1)
    a["x"] = np.concatenate([inp["x_prompt"][0], inp["x_sample"][0]]).reshape(NT, P, D).transpose(1, 0, 2)
    a["norm_g"] = inp["norm_g"]
    a["ev_w_in"] = slices(inp["ev_w_in"][0], P)
    quarter = D // 4
    omega = (1.0 / (f(10000.0) ** (np.arange(quarter, dtype=f) / f(quarter)))).astype(f)

    def emb(n):
        ang = np.arange(n, dtype=f)[:, None] * omega[None]
        return np.concatenate([np.sin(ang), np.cos(ang)], -1)
    er, ec = emb(LAT // 64), emb(64)
    pe = np.concatenate([np.repeat(er, 64, 0), np.tile(ec, (LAT // 64, 1))], -1)
    a["pos"] = pe.reshape(NT - 1, P, D).transpose(1, 0, 2)
    feats, times = [], np.ones((2, NT, P), f)
    for g, n in ((0, CTX), (1, LAT)):
        t = np.arange(n, dtype=f) / f(n)
        bands = np.linspace(1e-4, 15, 16, dtype=f)
        ang = f(2.0 * math.pi) * t[:, None] * bands[None]
        feats.append(np.concatenate([t[:, None], np.cos(ang), np.sin(ang)], -1))
        times[0, g:g + 1 + 3 * g] = -t.reshape(-1, P)
        times[1, g, 0] = 0.0
        w = (2 * np.arange(n)[None] + 1) * np.arange(n)[:, None] % (4 * n) * (math.pi / (2 * n))
        for name, m in (("cos", np.cos(w)), ("sin", np.sin(w))):
            for way, mat in (("fwd", m), ("inv", m.T / n)):
                part = mat.reshape(n // P, P, n).transpose(1, 0, 2).reshape(P, -1).astype(f)
                a[f"{name}_{way}"] = np.concatenate([a[f"{name}_{way}"], part], 1) if g else part
    a["hy_z"] = np.concatenate(feats).T
    a["hy_times"] = times.transpose(2, 0, 1)
    a["hy_w1"], a["hy_w2"], a["hy_w3"] = inp["hy_w1"][0], inp["hy_w2"][0], inp["hy_w3"][0]
    a["hy_cols"] = np.stack([inp["hy_b1"][0], inp["hy_b2"][0], inp["hy_freq"][0]], -1)
    a["hy_decay"], a["hy_bias"] = inp["hy_decay"][0], inp["hy_bias"][0]

    def taps(w, b):
        return np.concatenate([w, b[None]]).reshape(4, -1, P).transpose(2, 1, 0)
    a["hy_taps"] = taps(inp["hy_conv_w"][0], inp["hy_conv_b"][0])
    def states(v):
        v = v.reshape(2, PAIRS, 2, 64, *v.shape[3:])
        return np.moveaxis(v, (2, 3), (0, 1)).reshape(P, 2 * PAIRS, *v.shape[4:])
    step = np.broadcast_to(inp["s5_log_step"][0][:, :, None], (2, 32, 64))
    a["s5_par"] = np.stack([states(v) for v in (
        inp["s5_a_re"][0], inp["s5_a_im"][0], step, inp["state_s5_re"][0, 0],
        inp["state_s5_im"][0, 0])], 1)
    a["s5_B"] = np.stack([states(inp["s5_b_re"][0]), states(inp["s5_b_im"][0])], 1)
    a["s5_C"] = np.stack([states(inp[n][0].transpose(0, 1, 3, 2)) for n in ("s5_c_re", "s5_c_im")], 1)
    a["s5_d"] = inp["s5_d"][0].reshape(4, P).T
    ctx_steps, lat_steps = np.arange(1, CTX + 1, dtype=f), np.arange(1, LAT + 1, dtype=f)
    a["s5_steps"] = np.stack([np.concatenate([ctx_steps, lat_steps]),
                              np.concatenate([lat_steps, ctx_steps])])
    a["glu_w"] = inp["s5_glu_w"][0].reshape(4, P, 512).transpose(1, 0, 2)
    a["glu_b"] = inp["s5_glu_b"][0].reshape(4, P).T
    a["ev_w_out"] = inp["ev_w_out"][0].reshape(KD, P, D).transpose(1, 0, 2)
    w = inp["od_w_in"][0]
    a["od_w_qk"], a["od_w_vo"] = slices(w[:, 0:2 * D], P), slices(w[:, 2 * D:4 * D], HALF)
    a["gate_w"] = w[:, 4 * D:].reshape(KD, P, 4 * MLH).transpose(1, 0, 2)
    a["gate_b"], a["ml_m0"] = inp["od_gate_b"][0].T, inp["state_mlstm_m"][0, 0].T
    a["ml_taps"] = taps(inp["ml_conv_w"][0], inp["ml_conv_b"][0])
    a["ml_CN0"] = np.concatenate([inp["state_mlstm_C"][0, 0], inp["state_mlstm_n"][0, 0][..., None]],
                                 -1).transpose(2, 0, 1, 3)
    a["ml_norm_g"], a["final_g"] = inp["ml_norm_g"][0], inp["final_g"]
    a["od_w_out"] = inp["od_w_out"][0].reshape(KD, P, D).transpose(1, 0, 2)
    for l in range(2):
        a[f"pk_w_q{l}"] = slices(inp["pk_w_q"][l], P)
        a[f"pk_u{l}"], a[f"pk_v{l}"] = inp["pk_u"][l], inp["pk_v"][l]
    a["pk_keys"] = inp["pk_keys"].transpose(0, 4, 1, 2, 3).reshape(2, P, CODES, P)
    return {k: np.ascontiguousarray(v, dtype=v.dtype) for k, v in a.items()}


def kernel(**inputs):
    import concourse.bacc as bacc
    from concourse.bass_utils import run_bass_kernel_spmd as run

    USED.clear()
    arrays = {f"in_{n}_dram": a for n, a in host_arrays(inputs).items()}
    nc = bacc.Bacc("TRN2", target_bir_lowering=False, num_devices=1)
    T = {n[3:-5]: nc.dram_tensor(n, a.shape, mybir.dt.from_np(a.dtype), kind="ExternalInput").ap()
         for n, a in arrays.items()}
    O = {n: nc.dram_tensor(f"out_{n}_dram", shape, F32, kind="ExternalOutput").ap()
         for n, shape in OUTS.items()}
    trunk(nc, T, O)
    r = run(nc, [arrays], core_ids=[0]).results[0]
    y, re, im, C, n, m = (r[f"out_{k}_dram"] for k in OUTS)
    return (y[None, :CTX], y[None, CTX:], re[None, None], im[None, None], C[None, None],
            n[None, None], m[None, None])
```

```python
import math
from contextlib import ExitStack, contextmanager

import numpy as np

import concourse.bass as bass
from concourse import mybir

F32 = mybir.dt.float32
U32 = mybir.dt.uint32
I32 = mybir.dt.int32
ALU = mybir.AluOpType
ACT = mybir.ActivationFunctionType
AX = mybir.AxisListType

P = 128
D = 1024
KD = D // P
CTX = 128
LAT = 512
TOK = CTX + LAT
NT = TOK // P
GROUPS = ((0, CTX), (CTX, TOK))
EPS = 1e-6
HALF = 512
TWO_PI = 2.0 * math.pi
PI_BELOW = 3.1415925
ROUND = 1.5 * 2.0 ** 23


def group_of(tile):
    return 0 if tile == 0 else 1


def wait_apart(eng, sem, count, mark):
    eng.wait_ge(sem, count)
    eng.sem_inc(mark, 1)


class Line:

    def __init__(self, eng, sem):
        self.eng, self.sem, self.n, self.at = eng, sem, 0, 0

    def then(self, ins, mark=None):
        self.count(ins)
        self.settle(mark)

    def count(self, ins):
        self.n += 1
        ins.then_inc(self.sem, 1)

    def settle(self, mark=None):
        if mark is None:
            self.eng.wait_ge(self.sem, self.at + self.n)
        else:
            wait_apart(self.eng, self.sem, self.at + self.n, mark)

    @contextmanager
    def loop(self, start, stop, per):
        before, was = self.n, self.at
        assert isinstance(was, int)
        with self.eng.Fori(start, stop) as i:
            self.at, self.n = was + before + (i - start) * per, 0
            yield i
            assert self.n == per, (self.n, per)
        self.at, self.n = was + before + (stop - start) * per, 0


USED = {}


def numbered(name):
    USED[name] = USED.get(name, -1) + 1
    return f"{name}_{USED[name]}"


@contextmanager
def stage(nc, *names):
    sems = [nc.alloc_semaphore(numbered(n)) for n in names]
    with ExitStack() as ctx:
        yield ctx, sems
    nc.clear_and_free_semaphores(sems)
    nc.all_engine_barrier()


def buf(ctx, nc, name, shape, dt=F32):
    return ctx.enter_context(nc.sbuf_tensor(numbered(name), shape, dt))


MOD = 2 * 6 * D
MOD_FIRST = 2 * D
MOD_W = 320
MOD_BLOCKS = (MOD - MOD_FIRST) // MOD_W


def mod_row(mod, layer, g, chunk):
    at = (6 * layer + chunk) * D
    return mod[g, at:at + D].partition_broadcast(P)


def norm_modulate(nc, ps, X, H, HT, ident, mod, gain, layer, shift, scale):
    with stage(nc, "rows_in", "squared", "rooted", "dve_line", "h_ready", "turned",
               "copied") as (ctx, (rows_in, squared, rooted, dve_line, h_ready, turned, copied)):
        g_row = buf(ctx, nc, "g_row", [P, D])
        sc = buf(ctx, nc, "sc_row", [P, 2, D])
        sh = buf(ctx, nc, "sh_row", [P, 2, D])
        junk = buf(ctx, nc, "squares", [P, D])
        ss = buf(ctx, nc, "mean_square", [P, NT])
        rs = buf(ctx, nc, "root", [P, NT])
        block = ctx.enter_context(nc.Block())

        @block.sync
        def _(sp):
            sp.dma_start(g_row[:], gain.partition_broadcast(P)).then_inc(rows_in, 16)
            for g in range(2):
                for dst, c in ((sc, scale), (sh, shift)):
                    sp.dma_start(dst[:, g, :], mod_row(mod, layer, g, c)).then_inc(rows_in, 16)

        @block.scalar
        def _(act):
            for t in range(NT):
                act.activation(junk[:], X[:, t, :], ACT.Square,
                               accum_out=ss[:, t:t + 1]).then_inc(squared, 1)
                act.wait_ge(squared, t + 1)
            act.wait_ge(dve_line, 2)
            act.activation(rs[:], ss[:], ACT.Sqrt).then_inc(rooted, 1)
            for n in range(2 * NT):
                act.wait_ge(turned, n + 1)
                t, q = n // 2, n % 2
                act.activation(HT[:, 4 * q:4 * q + 4, t * P:(t + 1) * P],
                               ps[:, (n % 4) * HALF:(n % 4 + 1) * HALF].rearrange("p (k c) -> p k c", k=4),
                               ACT.Copy).then_inc(copied, 1)

        @block.vector
        def _(dve):
            line = Line(dve, dve_line)
            dve.wait_ge(squared, NT)
            line.then(dve.tensor_scalar(ss[:], ss[:], 1.0 / D, EPS, ALU.mult, ALU.add))
            line.then(dve.reciprocal(ss[:], ss[:]))
            dve.wait_ge(rows_in, 80)
            for g in range(2):
                line.then(dve.scalar_tensor_tensor(out=sc[:, g, :], in0=sc[:, g, :], scalar=1.0,
                                                   in1=g_row[:], op0=ALU.add, op1=ALU.mult))
            dve.wait_ge(rooted, 1)
            for t in range(NT):
                g = group_of(t)
                line.then(dve.scalar_tensor_tensor(out=H[:, t, :], in0=X[:, t, :],
                                                   scalar=rs[:, t:t + 1], in1=sc[:, g, :],
                                                   op0=ALU.mult, op1=ALU.mult))
                dve.tensor_tensor(H[:, t, :], H[:, t, :], sh[:, g, :], ALU.add).then_inc(h_ready, 1)
                dve.wait_ge(h_ready, t + 1)

        @block.tensor
        def _(pe):
            for n in range(2 * NT):
                t, q = n // 2, n % 2
                if q == 0:
                    pe.wait_ge(h_ready, t + 1)
                if n >= 4:
                    pe.wait_ge(copied, n - 3)
                for k in range(4):
                    mm = pe.transpose(ps[:, (n % 4) * HALF + k * P:(n % 4) * HALF + (k + 1) * P],
                                      H[:, t, (4 * q + k) * P:(4 * q + k + 1) * P], ident[:])
                mm.then_inc(turned, 1)


def project_channels(nc, ps, HT, W, OUT, blocks, width=P):
    with stage(nc, "w_in0", "w_in1", "used", "lat_out", "ctx_out") as (
            ctx, (w_in0, w_in1, used, lat_out, ctx_out)):
        w_in = (w_in0, w_in1)
        w = buf(ctx, nc, "w_block", [P, 2, KD * width])
        block = ctx.enter_context(nc.Block())

        @block.sync
        def _(sp):
            for b in range(2):
                sp.dma_start(w[:, b, :], W[b]).then_inc(w_in[b], 16)
            with sp.Fori(1, blocks // 2) as i:
                for b in range(2):
                    sp.wait_ge(used, 2 * i + (b - 1))
                    sp.dma_start(w[:, b, :], W[2 * i + b]).then_inc(w_in[b], 16)

        @block.tensor
        def _(pe):
            def products(b):
                for k in range(KD):
                    lhs = w[:, b, k * width:(k + 1) * width]
                    pe.matmul(ps[0:width, 2 * b * HALF:2 * b * HALF + LAT], lhs, HT[:, k, CTX:TOK],
                              start=(k == 0), stop=(k == KD - 1))
                    mm = pe.matmul(ps[0:width, (2 * b + 1) * HALF:(2 * b + 1) * HALF + CTX], lhs, HT[:, k, 0:CTX],
                                   start=(k == 0), stop=(k == KD - 1))
                mm.then_inc(used, 1)

            for b in range(2):
                pe.wait_ge(w_in[b], 16)
                products(b)
            with pe.Fori(1, blocks // 2) as i:
                for b in range(2):
                    pe.wait_ge(w_in[b], 16 * i + 16)
                    pe.wait_ge(lat_out, 2 * i + (b - 1))
                    pe.wait_ge(ctx_out, 2 * i + (b - 1))
                    products(b)

        @block.vector
        def _(dve):
            with dve.Fori(0, blocks // 2) as i:
                for b in range(2):
                    dve.wait_ge(used, 2 * i + (b + 1))
                    dve.tensor_copy(OUT[0:width, bass.ds(2 * i + b, 1), CTX:TOK],
                                    ps[0:width, 2 * b * HALF:2 * b * HALF + LAT].unsqueeze(1)).then_inc(lat_out, 1)

        @block.scalar
        def _(act):
            with act.Fori(0, blocks // 2) as i:
                for b in range(2):
                    act.wait_ge(used, 2 * i + (b + 1))
                    act.activation(OUT[0:width, bass.ds(2 * i + b, 1), 0:CTX],
                                   ps[0:width, (2 * b + 1) * HALF:(2 * b + 1) * HALF + CTX].unsqueeze(1),
                                   ACT.Copy).then_inc(ctx_out, 1)


HEADS = 8
TOPK = 16
SLOTS = HEADS * TOPK
CODES = 2 * HEADS
LOWEST = -3.0e38
RING = 16
FREED = 4
PE_OF_8 = (1, 4, 6)
DIAGS = 4
CODE_AT, CODE_GAP = 64, 4
HEAD_GAP = 8
LATE_AT, LATE_GAP = HEADS * HEAD_GAP + 1, 4
EXP_AT = LATE_AT + 12


def on_pe(slot):
    return slot % 8 in PE_OF_8


def pe_rows(slots):
    return sum(on_pe(n) for n in range(slots))


def experts(nc, T, ps, HT, H, X, mod, ident, layer, g_chunk):
    names = [f"row_in{b}" for b in range(RING)]
    with stage(nc, "keys_in", "w_in0", "w_in1", "used", "q_out", "q_cur", "scored", "s_free", "exp_in", "exp_out",
               "dve_line", "iota_done", "idx_ready", "idx_set", "h_set", "dve_used", "pe_used",
               "dots_done", "gelu_done", "weights_set", "diag_set", "v_idx_free", "g_in",
               "waited", *names) as (
            ctx, (keys_in, w_in0, w_in1, used, q_out, q_cur, scored, s_free, exp_in, exp_out, dve_line,
                  iota_done, idx_ready, idx_set, h_set, dve_used, pe_used, dots_done, gelu_done,
                  weights_set, diag_set, v_idx_free, g_in, mark, *row_in)):
        keys = buf(ctx, nc, "keys", [P, CODES, P])
        q = buf(ctx, nc, "q_tile", [P, CODES, P])
        QT = buf(ctx, nc, "QT", [P, CODES, LAT])
        s = ps[:, 0:4 * HALF].rearrange("p (c n) -> p c n", c=CODES)
        s2 = buf(ctx, nc, "scores_rest", [P, CODES, P])
        top = buf(ctx, nc, "top_value", [P, CODES, TOPK])
        where = buf(ctx, nc, "top_index", [P, CODES, TOPK], U32)
        where_f = top
        best = buf(ctx, nc, "best_value", [P, HEADS, TOPK])
        at = buf(ctx, nc, "best_at", [P, HEADS, TOPK], U32)
        at_part = buf(ctx, nc, "best_part", [P, 2, SLOTS], U32)
        at_f = buf(ctx, nc, "best_part_f", [P, 2, SLOTS])
        key_f = buf(ctx, nc, "key_f", [P, 2, SLOTS])
        iota = buf(ctx, nc, "iota16", [P, TOPK])
        e = buf(ctx, nc, "exp_score", [P, HEADS, TOPK])
        e_sum = buf(ctx, nc, "exp_sum", [P, HEADS])
        idx = buf(ctx, nc, "expert", [P, SLOTS], U32)
        gate = buf(ctx, nc, "expert_gate", [P, SLOTS])
        rows = buf(ctx, nc, "expert_rows", [P, RING, D])
        idx_u = buf(ctx, nc, "idx_u", [P, SLOTS], U32)
        idx_v = buf(ctx, nc, "idx_v", [P, SLOTS], U32)
        h = buf(ctx, nc, "h_tile", [P, D])
        acc = buf(ctx, nc, "acc", [P, 2, D])
        dots = buf(ctx, nc, "dots", [P, SLOTS])
        act_w = buf(ctx, nc, "expert_weight", [P, SLOTS])
        diag = buf(ctx, nc, "weight_diag", [P, DIAGS, P])
        block = ctx.enter_context(nc.Block())
        g_row = keys[:, :, :].rearrange("p (g c) n -> p g (c n)", g=2)
        w = acc
        w_in = (w_in0, w_in1)
        cand = s.rearrange("p (h a) n -> p h (a n)", a=2)
        cand2 = s2[:, :, :].rearrange("p (h a) n -> p h (a n)", a=2)
        pick = cand.rearrange("p h (k j) -> p h k j", j=TOPK)
        pair = top[:, :, :].rearrange("p (h a) k -> p h a k", a=2)
        half = where_f[:, :, :].rearrange("p (h a) k -> p h a k", a=2)
        table_u, table_v = T[f"pk_u{layer}"], T[f"pk_v{layer}"]
        dve_tile, pe_tile = 2 * SLOTS - pe_rows(SLOTS), pe_rows(SLOTS)
        pe_ring = len(PE_OF_8) * RING // 8
        v_sum = ps[:, 4 * HALF:6 * HALF]

        def dve_rows(n):
            return n - pe_rows(max(0, n - SLOTS)) if n >= 0 else n + pe_rows(SLOTS) - pe_rows(SLOTS + n)

        @block.sync
        def _(sp):
            W = T[f"pk_w_q{layer}"]
            for c in range(2):
                sp.dma_start(w[:, c, :], W[c]).then_inc(w_in[c], 16)
            sp.dma_start(keys[:], T["pk_keys"][layer]).then_inc(keys_in, 16)
            with sp.Fori(1, CODES // 2) as i:
                for c in range(2):
                    sp.wait_ge(used, 2 * i + (c - 1))
                    sp.dma_start(w[:, c, :], W[2 * i + c]).then_inc(w_in[c], 16)
            with sp.Fori(0, CODES // 2) as i:
                for c in range(2):
                    sp.wait_ge(used, 2 * i + (CODES + c - 1))
                    sp.dma_start(w[:, c, :], W[2 * i + c]).then_inc(w_in[c], 16)
            sp.wait_ge(scored, NT)
            for g in range(2):
                sp.dma_start(g_row[:, g, :], mod_row(mod, layer, g, g_chunk)).then_inc(g_in, 16)

        @block.gpsimd
        def _(pool):
            pool.iota(iota[:], pattern=[[1, TOPK]], base=0, channel_multiplier=0,
                      allow_small_or_imprecise_dtypes=True).then_inc(iota_done, 1)
            with pool.Fori(0, NT) as t:
                wait_apart(pool, idx_ready, t + 1, mark)
                for table, index, first in ((table_u, idx_u, 0), (table_v, idx_v, SLOTS)):
                    if first == 0:
                        wait_apart(pool, dots_done, t + 1, mark)
                        wait_apart(pool, v_idx_free, t + 1, mark)
                        pool.tensor_copy(idx_u[:], idx[:])
                        pool.tensor_copy(idx_v[:], idx[:]).then_inc(idx_set, 1)
                        pool.wait_ge(idx_set, t + 1)
                    for n in range(SLOTS):
                        b = n % RING
                        if n % FREED == 0:
                            before = first + n + FREED - RING
                            wait_apart(pool, dve_used, t * dve_tile
                                       + (RING - pe_ring + dve_rows(before)), mark)
                            if before < 0 or first:
                                wait_apart(pool, pe_used, t * pe_tile
                                           + (pe_ring + before - dve_rows(before)), mark)
                        pool.indirect_dma_start(
                            out=rows[:, b, :], out_offset=None, in_=table,
                            in_offset=bass.IndirectOffsetOnAxis(ap=index[:, n:n + 1], axis=0),
                        ).then_inc(row_in[b], 16)

        @block.scalar
        def _(act):
            def queries(i, c, context):
                n, at = 2 * i + c, (4 + c) * HALF
                act.wait_ge(used, 2 * i + ((0 if context else CODES) + c + 1))
                out, width = (q[:, bass.ds(n, 1), :], CTX) if context else (QT[:, bass.ds(n, 1), :], LAT)
                act.activation(out, ps[:, at:at + width].unsqueeze(1), ACT.Copy
                               ).then_inc(q_out, 1)

            def token_rows(t):
                act.activation(h[:, :].unsqueeze(1), H[:, bass.ds(t, 1), :],
                               ACT.Copy).then_inc(h_set, 1)

            def exponentials(t):
                act.wait_ge(exp_in, t + 1)
                act.activation(e[:], e[:], ACT.Exp).then_inc(exp_out, 1)

            def tile(t, more):
                if more:
                    act.wait_ge(scored, t + 1)
                    act.activation(q[:], QT[:, :, bass.ds(t * P, P)], ACT.Copy).then_inc(q_cur, 1)
                act.wait_ge(dots_done, t + 2)
                act.activation(act_w[:], dots[:], ACT.Gelu_apprx_tanh).then_inc(gelu_done, 1)
                if more:
                    token_rows(t + 1)
                act.wait_ge(weights_set, t + 1)
                for n in range(SLOTS):
                    if more and n == EXP_AT:
                        exponentials(t + 1)
                    if on_pe(n):
                        j = pe_rows(n)
                        act.wait_ge(pe_used, t * pe_tile + (pe_ring + j + 1 - DIAGS))
                        act.activation(diag[:, j % DIAGS, :], ident[:], ACT.Copy,
                                       scale=act_w[:, n:n + 1]).then_inc(diag_set, 1)

            token_rows(0)
            with act.Fori(0, CODES // 2) as i:
                for c in range(2):
                    queries(i, c, True)
            with act.Fori(0, CODES // 4) as i:
                for c in range(2):
                    queries(i, c, False)
            exponentials(0)
            with act.Fori(CODES // 4, CODES // 2) as i:
                for c in range(2):
                    queries(i, c, False)
            act.wait_ge(q_out, 2 * CODES)
            with act.Fori(0, NT - 1) as t:
                tile(t, True)
            tile(NT - 1, False)

        @block.tensor
        def _(pe):
            def queries(i, c, context):
                first = 0 if context else CODES
                pe.wait_ge(w_in[c], 16 * i + (8 * first + 16))
                if not (context and isinstance(i, int)):
                    pe.wait_ge(q_out, 2 * i + (first + c - 1))
                at = (4 + c) * HALF
                a, z = (0, CTX) if context else (CTX, TOK)
                for k in range(KD):
                    mm = pe.matmul(ps[:, at:at + z - a], w[:, c, k * P:(k + 1) * P],
                                   HT[:, k, a:z], start=(k == 0), stop=(k == KD - 1))
                mm.then_inc(used, 1)

            def scores(t):
                pe.wait_ge(s_free, t + 1)
                for c in range(CODES):
                    mm = pe.matmul(ps[:, c * P:(c + 1) * P], q[:, c, :],
                                   keys[:, c, :], start=True, stop=True)
                mm.then_inc(scored, 1)

            def weighted_rows(t):
                for n in range(SLOTS):
                    if on_pe(n):
                        j, b = pe_rows(n), n % RING
                        pe.wait_ge(row_in[b], t * (16 * 2 * SLOTS // RING)
                                   + 16 * ((SLOTS + n) // RING + 1))
                        pe.wait_ge(diag_set, t * pe_tile + (j + 1))
                        for k in range(2):
                            mm = pe.matmul(v_sum[:, k * HALF:(k + 1) * HALF], diag[:, j % DIAGS, :],
                                           rows[:, b, k * HALF:(k + 1) * HALF],
                                           start=(j == 0), stop=(j == pe_tile - 1))
                        mm.then_inc(pe_used, 1)

            pe.sem_inc(pe_used, pe_ring)
            pe.wait_ge(keys_in, 16)
            for c in range(2):
                queries(0, c, True)
            with pe.Fori(1, CODES // 2) as i:
                for c in range(2):
                    queries(i, c, True)
            pe.wait_ge(q_out, CODES)
            scores(0)
            with pe.Fori(0, CODES // 2) as i:
                for c in range(2):
                    queries(i, c, False)
            pe.wait_ge(q_out, 2 * CODES)
            with pe.Fori(0, NT - 1) as t:
                pe.wait_ge(q_cur, t + 1)
                scores(t + 1)
                weighted_rows(t)
            weighted_rows(NT - 1)

        @block.vector
        def _(dve):
            line = Line(dve, dve_line)
            dve.sem_inc(s_free, 1)
            dve.sem_inc(dve_used, RING - pe_ring)
            dve.sem_inc(dots_done, 1)
            dve.sem_inc(v_idx_free, 1)
            dve.wait_ge(iota_done, 1)

            def search(step, src, rest, values, places, r):
                if step == 0:
                    return dve.max(values[:, r, 0:8], src[:, r, :])
                if step == 1:
                    dve.max_index(places[:, r, 0:8], values[:, r, 0:8], src[:, r, :])
                    return dve.match_replace(rest[:, r, :], values[:, r, 0:8], src[:, r, :], LOWEST)
                if step == 2:
                    return dve.max(values[:, r, 8:16], rest[:, r, :])
                return dve.max_index(places[:, r, 8:16], values[:, r, 8:16], rest[:, r, :])

            by_code = (s, s2, top, where)
            by_head = (cand, cand2, best, at)

            def sums(h0, h1):
                n = h1 - h0
                return dve.tensor_tensor(
                    pick[:, h0:h1],
                    pair[:, h0:h1, 0, :].unsqueeze(3).to_broadcast([P, n, TOPK, TOPK]),
                    pair[:, h0:h1, 1, :].unsqueeze(2).to_broadcast([P, n, TOPK, TOPK]), ALU.add)

            def late(step, t):
                flat = at[:, :, :].rearrange("p h k -> p (h k)")
                if step == 0:
                    ins = dve.tensor_tensor(e[:], best[:], best[:, :, 0:1].to_broadcast(
                        [P, HEADS, TOPK]), ALU.subtract)
                elif step == 1:
                    dve.sem_inc(exp_in, 1)
                    dve.tensor_scalar(at_part[:, 0, :], flat, 4, None, ALU.logical_shift_right)
                    ins = dve.tensor_scalar(at_part[:, 1, :], flat, TOPK - 1, None,
                                            ALU.bitwise_and)
                elif step == 2:
                    dve.tensor_copy(where_f[:], where[:])
                    ins = dve.tensor_copy(at_f[:], at_part[:])
                elif step < 9:
                    a, part = (step - 3) // 3, (step - 3) % 3
                    if part == 0:
                        ins = dve.tensor_tensor(
                            pick.rearrange("p h k j -> p (h k) j"),
                            iota[:, :].unsqueeze(1).to_broadcast([P, SLOTS, TOPK]),
                            at_f[:, a, :].unsqueeze(2).to_broadcast([P, SLOTS, TOPK]), ALU.is_equal)
                    elif part == 1:
                        ins = dve.tensor_tensor(
                            pick, pick, half[:, :, a, :].unsqueeze(2)
                            .to_broadcast([P, HEADS, TOPK, TOPK]), ALU.mult)
                    else:
                        ins = dve.tensor_reduce(key_f[:, a, :], pick.rearrange(
                            "p h k j -> p (h k) j"), AX.X, ALU.add)
                elif step == 9:
                    dve.sem_inc(s_free, 1)
                    if not isinstance(t, int):
                        dve.wait_ge(idx_set, t)
                    ins = dve.scalar_tensor_tensor(
                        out=idx[:], in0=key_f[:, 0, :], scalar=float(P),
                        in1=key_f[:, 1, :], op0=ALU.mult, op1=ALU.add)
                elif step == 10:
                    dve.sem_inc(idx_ready, 1)
                    dve.wait_ge(exp_out, t + 1)
                    ins = dve.tensor_reduce(e_sum[:], e[:], AX.X, ALU.add)
                elif step == 11:
                    ins = dve.reciprocal(e_sum[:], e_sum[:])
                else:
                    ins = dve.tensor_tensor(
                        gate[:, :].rearrange("p (h k) -> p h k", h=HEADS), e[:],
                        e_sum[:, :].unsqueeze(2).to_broadcast([P, HEADS, TOPK]), ALU.mult)
                return ins

            def scale_and_add(t, step):
                if step == 0:
                    line.then(dve.tensor_tensor(H[:, t, :], H[:, t, :], g_row[:, group_of(t), :],
                                                ALU.mult))
                else:
                    line.then(dve.tensor_tensor(X[:, t, :], X[:, t, :], H[:, t, :], ALU.add))

            def tile(t, more):
                dve.wait_ge(h_set, t + 1)
                for n in range(SLOTS):
                    b = n % RING
                    dve.wait_ge(row_in[b], t * (16 * 2 * SLOTS // RING) + 16 * (n // RING + 1))
                    dve.tensor_tensor_reduce(rows[:, b, :], rows[:, b, :], h[:], 1.0, 0.0,
                                             ALU.mult, ALU.add, dots[:, n:n + 1]
                                             ).then_inc(dve_used, 1)
                    code, k = divmod(n - CODE_AT, CODE_GAP)
                    if more and 0 <= code < CODES and k < 4:
                        if n == CODE_AT:
                            wait_apart(dve, scored, t + 2, mark)
                        else:
                            line.settle(mark)
                        line.count(search(k, *by_code, code))
                    if not more and n % 8 == 7 and n // 8 < 2 * (NT - 1):
                        if n == 7:
                            dve.wait_ge(g_in, 32)
                        scale_and_add(n // 16, n // 8 % 2)
                credit = RING - pe_ring
                dve.wait_ge(dve_used, t * dve_tile + (credit + SLOTS))
                dve.sem_inc(dots_done, 1)
                dve.wait_ge(gelu_done, t + 1)
                line.then(dve.tensor_tensor(act_w[:], act_w[:], gate[:], ALU.mult))
                dve.sem_inc(weights_set, 1)
                mine = 0
                for n in range(SLOTS):
                    b = n % RING
                    if not on_pe(n):
                        dve.wait_ge(row_in[b], t * (16 * 2 * SLOTS // RING)
                                    + 16 * ((SLOTS + n) // RING + 1))
                        a, w = acc[:, mine % 2, :], act_w[:, n:n + 1]
                        if mine < 2:
                            ins = dve.tensor_scalar(a, rows[:, b, :], w, None, ALU.mult)
                        else:
                            dve.wait_ge(dve_used, t * dve_tile + (credit + SLOTS + mine - 1))
                            ins = dve.scalar_tensor_tensor(out=a, in0=rows[:, b, :], scalar=w,
                                                           in1=a, op0=ALU.mult, op1=ALU.add)
                        ins.then_inc(dve_used, 1)
                        mine += 1
                    if not more:
                        continue
                    head, k = divmod(n, HEAD_GAP)
                    if head < HEADS and k in (0, 2, 4, 6, 7):
                        line.settle(mark)
                        if k == 0:
                            line.count(sums(head, head + 1))
                        else:
                            line.count(search((2, 4, 6, 7).index(k), *by_head, head))
                    step, k = divmod(n - LATE_AT, LATE_GAP)
                    if 0 <= step <= 12 and k == 0:
                        line.settle(mark)
                        line.count(late(step, t + 1))
                dve.wait_ge(dve_used, t * dve_tile + (credit + dve_tile))
                dve.wait_ge(pe_used, t * pe_tile + (pe_ring + pe_tile))
                dve.sem_inc(v_idx_free, 1)
                line.then(dve.tensor_tensor(acc[:, 0, :], acc[:, 0, :], acc[:, 1, :], ALU.add))
                line.then(dve.tensor_tensor(H[:, bass.ds(t, 1), :], acc[:, 0:1, :],
                                            v_sum.unsqueeze(1), ALU.add))

            dve.wait_ge(scored, 1)
            for by, n in ((by_code, CODES), (by_head, HEADS)):
                for step in range(4):
                    for r in range(n):
                        ins = search(step, *by, r)
                    line.then(ins)
                if by is by_code:
                    line.then(sums(0, HEADS))
            for step in range(13):
                line.then(late(step, 0))
            with line.loop(0, NT - 1, 4 * CODES + 5 * HEADS + 13 + 3) as t:
                tile(t, True)
            tile(NT - 1, False)
            for step in range(2):
                scale_and_add(NT - 1, step)


HYW = 512
HYF = 64
EMB = 33
DFT = P + (LAT // P) * LAT


def dft_block(m, src, dst):
    if dst == 0:
        return m[:, 0:P]
    at = P + (src - 1) * LAT + (dst - 1) * P
    return m[:, at:at + P]


def sources(tile):
    return (0,) if tile == 0 else tuple(range(1, NT))


def start(nc, T, ps, X, ident, cond_s, mod, KC, KS):
    blocks = MOD_FIRST // HALF
    with stage(nc, "cond_in", "small_in", "decay_in", "ada_in0", "ada_in1", "x_in", "bias_in",
               "dft_in", "ident_set", "cond_ready", "ada_used", "rows_added", "mod_out", "x_ready",
               "layer_done", "args_ready", "sines_done", "taps_raw", "env_done", "taps_done",
               "ab_ready", "sq_done", "sums_done", "rooted", "sqrt_done", "dft_done", "dft_out",
               "dve_line", "act_line") as (
            ctx, (cond_in, small_in, decay_in, ada_in0, ada_in1, x_in, bias_in, dft_in, ident_set,
                  cond_ready, ada_used, rows_added, mod_out, x_ready, layer_done, args_ready,
                  sines_done, taps_raw, env_done, taps_done, ab_ready, sq_done, sums_done, rooted,
                  sqrt_done, dft_done, dft_out, dve_line, act_line)):
        ada_in = (ada_in0, ada_in1)
        cond = buf(ctx, nc, "cond", [P, KD, 2])
        z = buf(ctx, nc, "features", [EMB, TOK])
        w1 = buf(ctx, nc, "hy_w1", [EMB, HYF])
        w2 = buf(ctx, nc, "hy_w2", [HYF, HYF])
        w3 = buf(ctx, nc, "hy_w3", [HYF, 4 * HYW])
        col = buf(ctx, nc, "hy_cols", [HYF, 3])
        times = buf(ctx, nc, "hy_times", [P, 2, NT])
        decay = buf(ctx, nc, "decay", [P, 4 * HYW])
        arg = buf(ctx, nc, "sine_arg", [HYF, TOK])
        turn = buf(ctx, nc, "sine_turn", [HYF, TOK])
        h = buf(ctx, nc, "sine", [HYF, TOK])
        env = buf(ctx, nc, "envelope", [P, 4 * HYW])
        tmp = buf(ctx, nc, "bwd_taps", [P, 2, HYW])
        AB = buf(ctx, nc, "taps", [P, 2, NT, 2, HYW])
        ones = buf(ctx, nc, "ones", [P, P])
        root = buf(ctx, nc, "filter_norm", [P, 2, 2 * HYW])
        cf = buf(ctx, nc, "cos_fwd", [P, DFT])
        sf = buf(ctx, nc, "sin_fwd", [P, DFT])
        block = ctx.enter_context(nc.Block())
        A, B = AB[:, 0], AB[:, 1]
        four = ps[:, 0:4 * HALF]
        sq = env
        w = AB[:, :, :, :, :].rearrange("p a t o c -> p (a t o c)")[:, 0:2 * KD * HALF
                                                                    ].rearrange("p (b n) -> p b n", b=2)
        rows = KS[0:2, :, :, :].rearrange("p t o c -> p (t o c)")[:, 0:MOD_FIRST]
        pos = KC[:, 0:NT - 1, :, :].rearrange("p t o c -> p t (o c)")

        @block.sync
        def _(sp):
            for dst, src in ((z, "hy_z"), (w1, "hy_w1"), (w2, "hy_w2"), (col, "hy_cols"),
                             (w3, "hy_w3"), (times, "hy_times")):
                sp.dma_start(dst[:], T[src]).then_inc(small_in, 16)
            sp.dma_start(decay[:], T["hy_decay"].partition_broadcast(P)).then_inc(decay_in, 16)
            sp.dma_start(X[:], T["x"]).then_inc(x_in, 16)
            sp.dma_start(pos, T["pos"]).then_inc(x_in, 16)
            sp.dma_start(cf[:], T["cos_fwd"]).then_inc(dft_in, 16)
            sp.dma_start(sf[:], T["sin_fwd"]).then_inc(dft_in, 16)
            sp.wait_ge(rows_added, blocks)
            sp.dma_start(mod[:, 0:MOD_FIRST], rows).then_inc(mod_out, 16)
            sp.wait_ge(mod_out, 16)

        @block.gpsimd
        def _(pool):
            pool.memset(ident[:], 0.0).then_inc(ident_set, 1)
            pool.dma_start(cond[:], T["cond"]).then_inc(cond_in, 16)
            for b in range(blocks):
                if b >= 2:
                    pool.wait_ge(ada_used, b - 1)
                pool.dma_start(w[:, b % 2, :], T["ada_first"][b]).then_inc(ada_in[b % 2], 16)
                if b == 0:
                    for g in range(2):
                        pool.dma_start(rows[g:g + 1, :], T["ada_b"][:, 0:MOD_FIRST]
                                       ).then_inc(bias_in, 16)
            pool.wait_ge(ident_set, 1)
            pool.affine_select(out=ident[:], in_=ident[:], compare_op=ALU.not_equal, fill=1.0,
                               base=0, pattern=[[-1, P]], channel_multiplier=1
                               ).then_inc(ident_set, 1)
            pool.wait_ge(ident_set, 2)

        @block.tensor
        def _(pe):
            def sine_layer(wl, src):
                pe.matmul(ps[0:HYF, 0:HALF], wl[:], src[:, 0:HALF], start=True, stop=True)
                pe.matmul(ps[0:HYF, HALF:TOK], wl[:], src[:, HALF:TOK],
                          start=True, stop=True).then_inc(layer_done, 1)

            def modulation(b):
                pe.wait_ge(ada_in[b % 2], 16 * (b // 2 + 1))
                at = (4 + b) * HALF
                for k in range(KD):
                    mm = pe.matmul(ps[0:2, at:at + HALF], cond_s[:, k, :],
                                   w[:, b % 2, k * HALF:(k + 1) * HALF],
                                   start=(k == 0), stop=(k == KD - 1))
                mm.then_inc(ada_used, 1)

            pe.wait_ge(small_in, 6 * 16)
            sine_layer(w1, z)
            pe.wait_ge(cond_ready, 1)
            modulation(0)
            pe.wait_ge(sines_done, 1)
            sine_layer(w2, h)
            for b in range(1, blocks):
                modulation(b)
            pe.wait_ge(sines_done, 2)
            for t in range(NT):
                if t:
                    pe.wait_ge(taps_done, t)
                for j in range(4):
                    mm = pe.matmul(ps[:, j * HALF:(j + 1) * HALF], h[:, t * P:(t + 1) * P],
                                   w3[:, j * HYW:(j + 1) * HYW], start=True, stop=True)
                mm.then_inc(taps_raw, 1)
            pe.wait_ge(rows_added, blocks)
            pe.wait_ge(dft_in, 32)
            pe.wait_ge(taps_done, NT)
            for n in range(4 * NT):
                t, way, o = n // 4, n // 2 % 2, n % 2
                pe.wait_ge(ab_ready, NT if t else 1)
                if n >= 4:
                    pe.wait_ge(dft_out, n - 3)
                at = (n % 4) * HALF
                for k in sources(t):
                    mm = pe.matmul(ps[:, at:at + HALF], dft_block((cf, sf)[way], k, t),
                                   AB[:, way, k, o, :], start=(k == sources(t)[0]),
                                   stop=(k == sources(t)[-1]))
                mm.then_inc(dft_done, 1)
                if 3 <= n < 3 + NT:
                    ts = n - 3
                    pe.wait_ge(sq_done, ts + 1)
                    for o in range(2):
                        at = (4 + 2 * group_of(ts) + o) * HALF
                        mm = pe.matmul(ps[:, at:at + HALF], ones[:], sq[:, o * HYW:(o + 1) * HYW],
                                       start=(ts < 2), stop=(ts in (0, NT - 1)))
                    mm.then_inc(sums_done, 1)

        @block.scalar
        def _(act):
            line = Line(act, act_line)
            act.wait_ge(cond_in, 16)
            act.activation(cond_s[:], cond[:], ACT.Silu).then_inc(cond_ready, 1)
            act.wait_ge(decay_in, 16)
            line.then(act.activation(decay[:], decay[:], ACT.Abs))
            for layer in range(2):
                act.wait_ge(args_ready, layer + 1)
                act.activation(h[:], arg[:], ACT.Sin).then_inc(sines_done, 1)
            act.wait_ge(small_in, 6 * 16)
            for t in range(NT):
                if t:
                    act.wait_ge(taps_done, t)
                act.activation(env[:], decay[:], ACT.Exp,
                               scale=times[:, 0, t:t + 1]).then_inc(env_done, 1)
            act.wait_ge(x_ready, 1)
            act.wait_ge(mod_out, 16)
            for n in range(4 * NT):
                if n == 4 * NT - 6:
                    act.wait_ge(rooted, 1)
                    act.activation(root[:], root[:], ACT.Sqrt).then_inc(sqrt_done, 1)
                act.wait_ge(dft_done, n + 1)
                at = (n % 4) * HALF
                act.activation((KC, KS)[n // 2 % 2][:, n // 4, n % 2, :], ps[:, at:at + HALF],
                               ACT.Copy).then_inc(dft_out, 1)

        @block.vector
        def _(dve):
            line = Line(dve, dve_line)
            line.then(dve.memset(ones[:], 1.0))
            dve.wait_ge(small_in, 6 * 16)

            def add_bias(b):
                dve.wait_ge(ada_used, b + 1)
                r = rows[:, b * HALF:(b + 1) * HALF]
                at = (4 + b) * HALF
                dve.tensor_tensor(r, r, ps[0:2, at:at + HALF], ALU.add).then_inc(rows_added, 1)

            for layer in range(2):
                dve.wait_ge(layer_done, layer + 1)
                line.then(dve.tensor_scalar(arg[:], ps[0:HYF, 0:TOK], col[:, layer:layer + 1],
                                            col[:, 2:3], ALU.add, ALU.mult))
                reduce_turns(dve, line, arg, turn)
                dve.sem_inc(args_ready, 1)
            dve.wait_ge(bias_in, 32)
            for b in range(blocks):
                add_bias(b)
            dve.wait_ge(x_in, 32)
            dve.tensor_tensor(X[:, 1:NT, :], X[:, 1:NT, :], pos, ALU.add).then_inc(x_ready, 1)
            for t in range(NT):
                dve.wait_ge(taps_raw, t + 1)
                dve.wait_ge(env_done, t + 1)
                raw = four.rearrange("p (o d c) -> p o d c", o=2, d=2)
                e = env[:, :].rearrange("p (o d c) -> p o d c", o=2, d=2)
                dve.tensor_tensor(A[:, t], raw[:, :, 0, :], e[:, :, 0, :], ALU.mult)
                line.then(dve.scalar_tensor_tensor(out=tmp[:], in0=raw[:, :, 1, :],
                                                   scalar=times[:, 1, t:t + 1],
                                                   in1=e[:, :, 1, :], op0=ALU.mult, op1=ALU.mult))
                dve.sem_inc(taps_done, 1)
                dve.tensor_tensor(B[:, t], A[:, t], tmp[:], ALU.subtract)
                line.then(dve.tensor_tensor(A[:, t], A[:, t], tmp[:], ALU.add))
                dve.sem_inc(ab_ready, 1)
            q = sq[:, 0:2 * HYW]
            q2 = sq[:, 2 * HYW:4 * HYW]
            for t in range(NT):
                if t:
                    dve.wait_ge(sums_done, t)
                a, b = (v[:, t].rearrange("p o c -> p (o c)") for v in (A, B))
                dve.tensor_tensor(q, a, a, ALU.mult)
                line.then(dve.tensor_tensor(q2, b, b, ALU.mult))
                dve.tensor_tensor(q, q, q2, ALU.add).then_inc(sq_done, 1)
                dve.wait_ge(sq_done, t + 1)
            dve.wait_ge(sums_done, NT)
            line.then(dve.tensor_scalar(root[:], ps[:, 4 * HALF:8 * HALF]
                                        .rearrange("p (g n) -> p g n", g=2),
                                        0.5, EPS, ALU.mult, ALU.add))
            dve.reciprocal(root[:], root[:]).then_inc(rooted, 1)
            dve.wait_ge(sqrt_done, 1)
            for t in range(NT):
                dve.wait_ge(dft_out, 4 * t + 4)
                for K in (KC, KS):
                    v = K[:, t].rearrange("p o c -> p (o c)")
                    ins = dve.tensor_tensor(v, v, root[:, group_of(t), :], ALU.mult)
                line.then(ins)


def reduce_turns(dve, line, arg, turn):
    hi = 6.28125
    line.then(dve.tensor_scalar(turn[:], arg[:], 1.0 / TWO_PI, ROUND, ALU.mult, ALU.add))
    line.then(dve.tensor_scalar(turn[:], turn[:], ROUND, None, ALU.subtract))
    line.then(dve.scalar_tensor_tensor(out=arg[:], in0=turn[:], scalar=-hi, in1=arg[:],
                                       op0=ALU.mult, op1=ALU.add))
    line.then(dve.scalar_tensor_tensor(out=arg[:], in0=turn[:], scalar=-(TWO_PI - hi),
                                       in1=arg[:], op0=ALU.mult, op1=ALU.add))
    line.then(dve.tensor_scalar(arg[:], arg[:], PI_BELOW, -PI_BELOW, ALU.min, ALU.max))


def short_conv(dve, line, out, x, taps):
    line.then(dve.tensor_scalar(out, x, taps(1), taps(3), ALU.mult, ALU.add))
    for tap, lead in ((0, 1), (2, 0)):
        for a, b in GROUPS:
            n = b - a - 1
            ins = dve.scalar_tensor_tensor(
                out=out[:, a + lead:a + lead + n], in0=x[:, a + 1 - lead:a + 1 - lead + n],
                scalar=taps(tap), in1=out[:, a + lead:a + lead + n], op0=ALU.mult, op1=ALU.add)
        line.then(ins)


def hyena_inputs(nc, T, ps, PH, VG, ident):
    blocks = 3 * HYW // P
    with stage(nc, "taps_in", "conv_done", "turned", "out_done", "dve_line") as (
            ctx, (taps_in, conv_done, turned, out_done, dve_line)):
        taps = buf(ctx, nc, "conv_taps", [P, blocks, 4])
        cur = buf(ctx, nc, "conv_taps_cur", [P, 4])
        y = buf(ctx, nc, "conv_block", [P, 2, TOK])
        x = buf(ctx, nc, "conv_source", [P, TOK])
        block = ctx.enter_context(nc.Block())

        @block.sync
        def _(sp):
            sp.dma_start(taps[:], T["hy_taps"]).then_inc(taps_in, 16)
            sp.wait_ge(taps_in, 16)

        @block.vector
        def _(dve):
            line = Line(dve, dve_line)
            dve.wait_ge(taps_in, 16)
            dve.sem_inc(turned, 2)
            with line.loop(0, blocks // 2, 8) as i:
                for b in range(2):
                    dve.tensor_copy(x[:, :].unsqueeze(1), PH[:, bass.ds(i * 2 + b, 1), :])
                    line.then(dve.tensor_copy(cur[:, :].unsqueeze(1),
                                              taps[:, bass.ds(i * 2 + b, 1), :]))
                    dve.wait_ge(turned, i * 2 + (b + 1))
                    short_conv(dve, line, y[:, b, :], x[:, :], lambda k: cur[:, k:k + 1])
                    dve.sem_inc(conv_done, 1)

        @block.tensor
        def _(pe):
            pe.sem_inc(out_done, 2)
            with pe.Fori(0, blocks // 2) as i:
                for b in range(2):
                    pe.wait_ge(out_done, i * 2 + (b + 1))
                    pe.wait_ge(conv_done, i * 2 + (b + 1))
                    for t in range(NT):
                        at = 2 * b * HALF + t * P
                        mm = pe.transpose(ps[:, at:at + P], y[:, b, t * P:(t + 1) * P], ident[:])
                    mm.then_inc(turned, 1)

        @block.scalar
        def _(act):
            with act.Fori(0, blocks // 2) as i:
                for b in range(2):
                    act.wait_ge(turned, i * 2 + (b + 3))
                    act.activation(VG[:, :, bass.ds((i * 2 + b) * P, P)],
                                   ps[:, 2 * b * HALF:2 * b * HALF + TOK]
                                   .rearrange("p (t c) -> p t c", c=P), ACT.Copy).then_inc(out_done, 1)


def hyena_convolve(nc, T, ps, VG, KC, KS, MIXT, ident):
    with stage(nc, "mats_in", "angles", "mixed", "lines", "z_ready", "turned", "out_done",
               "dve_line") as (
            ctx, (mats_in, angles, mixed, lines, z_ready, turned, out_done, dve_line)):
        cf = buf(ctx, nc, "cos_fwd", [P, DFT])
        sf = buf(ctx, nc, "sin_fwd", [P, DFT])
        ci = buf(ctx, nc, "cos_inv", [P, DFT])
        si = buf(ctx, nc, "sin_inv", [P, DFT])
        bias = buf(ctx, nc, "hy_bias", [P, 2, HYW])
        R = buf(ctx, nc, "product_re", [P, NT, HYW])
        I = buf(ctx, nc, "product_im", [P, NT, HYW])
        t1 = buf(ctx, nc, "part1", [P, HYW])
        t2 = buf(ctx, nc, "part2", [P, HYW])
        t3 = buf(ctx, nc, "part3", [P, HYW])
        t4 = buf(ctx, nc, "part4", [P, HYW])
        z = VG[:, :, 0:HYW]
        block = ctx.enter_context(nc.Block())

        @block.sync
        def _(sp):
            for dst, src in ((cf, "cos_fwd"), (sf, "sin_fwd"), (ci, "cos_inv"), (si, "sin_inv")):
                sp.dma_start(dst[:], T[src]).then_inc(mats_in, 16)
            sp.dma_start(bias[:], T["hy_bias"].partition_broadcast(P)).then_inc(mats_in, 16)

        @block.tensor
        def _(pe):
            pe.wait_ge(mats_in, 80)
            for o in range(2):
                pe.wait_ge(z_ready, NT * o) if o else None
                for t in range(NT):
                    n = NT * o + t
                    if n >= 2:
                        pe.wait_ge(mixed, n - 1)
                    for j, m in enumerate((cf, sf)):
                        at = (2 * (n % 2) + j) * HALF
                        for k in sources(t):
                            mm = pe.matmul(ps[:, at:at + HALF], dft_block(m, k, t), z[:, k, :],
                                           start=(k == sources(t)[0]), stop=(k == sources(t)[-1]))
                    mm.then_inc(angles, 1)
                for t in range(NT):
                    n = NT * o + t
                    pe.wait_ge(mixed, NT * o + sources(t)[-1] + 1)
                    if n >= 2:
                        pe.wait_ge(z_ready, n - 1)
                    at = (4 + n % 2) * HALF
                    for k in sources(t):
                        pe.matmul(ps[:, at:at + HALF], dft_block(ci, k, t), R[:, k, :],
                                  start=(k == sources(t)[0]), stop=False)
                        mm = pe.matmul(ps[:, at:at + HALF], dft_block(si, k, t), I[:, k, :],
                                       start=False, stop=(k == sources(t)[-1]))
                    mm.then_inc(lines, 1)
            for t in range(NT):
                pe.wait_ge(z_ready, NT + t + 1)
                if t >= 2:
                    pe.wait_ge(out_done, t - 1)
                for m in range(4):
                    at = (6 + t % 2) * HALF + m * P
                    mm = pe.transpose(ps[:, at:at + P], z[:, t, m * P:(m + 1) * P], ident[:])
                mm.then_inc(turned, 1)

        @block.scalar
        def _(act):
            for t in range(NT):
                act.wait_ge(turned, t + 1)
                at = (6 + t % 2) * HALF
                act.activation(MIXT[:, 0:4, t * P:(t + 1) * P], ps[:, at:at + HALF]
                               .rearrange("p (m c) -> p m c", c=P), ACT.Copy).then_inc(out_done, 1)

        @block.vector
        def _(dve):
            line = Line(dve, dve_line)
            dve.wait_ge(mats_in, 80)
            for o in range(2):
                for t in range(NT):
                    n = NT * o + t
                    dve.wait_ge(angles, n + 1)
                    b = 2 * (n % 2) * HALF
                    zc, zs = ps[:, b:b + HALF], ps[:, b + HALF:b + 2 * HALF]
                    dve.tensor_tensor(t1[:], zc, KC[:, t, o, :], ALU.mult)
                    dve.tensor_tensor(t2[:], zs, KS[:, t, o, :], ALU.mult)
                    dve.tensor_tensor(t3[:], zs, KC[:, t, o, :], ALU.mult)
                    line.then(dve.tensor_tensor(t4[:], zc, KS[:, t, o, :], ALU.mult))
                    dve.tensor_tensor(R[:, t, :], t1[:], t2[:], ALU.subtract)
                    line.then(dve.tensor_tensor(I[:, t, :], t3[:], t4[:], ALU.add))
                    dve.sem_inc(mixed, 1)
                for t in range(NT):
                    n = NT * o + t
                    dve.wait_ge(lines, n + 1)
                    at = (4 + n % 2) * HALF
                    line.then(dve.tensor_tensor(t1[:], z[:, t, :], bias[:, o, :], ALU.mult))
                    line.then(dve.tensor_tensor(t1[:], t1[:], ps[:, at:at + HALF], ALU.add))
                    dve.tensor_tensor(z[:, t, :], t1[:], VG[:, t, (o + 1) * HYW:(o + 2) * HYW],
                                      ALU.mult).then_inc(z_ready, 1)
                    dve.wait_ge(z_ready, n + 1)


PAIRS = 16
S5C = 16
UNITS = 8
SEGMENTS = (((0, CTX, False), (CTX, TOK, True)), ((0, LAT, True), (LAT, TOK, False)))


def exact_exp(dve, one, out, x, n, y, bits):
    one(dve.tensor_scalar(n, x, 1.0 / math.log(2.0), ROUND, ALU.mult, ALU.add))
    one(dve.tensor_scalar(n, n, ROUND, None, ALU.subtract))
    one(dve.tensor_scalar(n, n, -126.0, 127.0, ALU.max, ALU.min))
    one(dve.scalar_tensor_tensor(out=y, in0=n, scalar=-0.693359375, in1=x, op0=ALU.mult, op1=ALU.add))
    one(dve.scalar_tensor_tensor(out=y, in0=n, scalar=0.693359375 - math.log(2.0), in1=y,
                                 op0=ALU.mult, op1=ALU.add))
    one(dve.tensor_scalar(y, y, -0.35, 0.35, ALU.max, ALU.min))
    one(dve.tensor_scalar(n, n, 127.0, None, ALU.add))
    one(dve.tensor_copy(bits, n))
    one(dve.tensor_scalar(bits, bits, 23, None, ALU.logical_shift_left))
    one(dve.tensor_scalar(out, y, 1.0 / 5040, 1.0 / 720, ALU.mult, ALU.add))
    for c in (1.0 / 120, 1.0 / 24, 1.0 / 6, 0.5, 1.0, 1.0):
        one(dve.tensor_tensor(out, out, y, ALU.mult))
        one(dve.tensor_scalar(out, out, c, None, ALU.add))
    one(dve.tensor_tensor(out, out, bits.bitcast(F32), ALU.mult))


def s5(nc, T, ps, US, G, ident, out_re, out_im, cond_s, mod):
    with stage(nc, "par_in", "d_in", "dve_line", "act_line", "pool_line", "bd_ready", "bt_raw",
               "bt_ready", "bu_done", "bu_used", "turn_set", "turn_used", "trig_set", "trig_used",
               "prod_set", "prod_used", "y_done", "y_out", "states_out", "waited",
               "ada_in0", "ada_in1", "ada_used", "ada_copied", "mod_out0", "mod_out1", "ones_set") as (
            ctx, (par_in, d_in, dve_line, act_line, pool_line, bd_ready, bt_raw, bt_ready, bu_done,
                  bu_used, turn_set, turn_used, trig_set, trig_used, prod_set, prod_used, y_done,
                  y_out, states_out, mark, ada_in0, ada_in1, ada_used, ada_copied, mod_out0,
                  mod_out1, ones_set)):
        ada_in, mod_out = (ada_in0, ada_in1), (mod_out0, mod_out1)
        assert MOD_BLOCKS == 4 * UNITS
        ada = buf(ctx, nc, "ada_block", [P, 2, KD * MOD_W])
        ada_b = buf(ctx, nc, "ada_bias", [1, 2, MOD_W])
        rows = buf(ctx, nc, "mod_rows", [2, 2, MOD_W])
        ones = buf(ctx, nc, "one_one", [1, 2])
        N2 = [P, 2, PAIRS]
        par = buf(ctx, nc, "s5_par", [P, 5, 2 * PAIRS])
        B = buf(ctx, nc, "s5_B", [P, 2, 2 * PAIRS, S5C])
        C = buf(ctx, nc, "s5_C", [P, 2, 2 * PAIRS, S5C])
        Bb = buf(ctx, nc, "s5_Bbar", [P, 2, 2 * PAIRS, S5C])
        tmpB = buf(ctx, nc, "s5_tmpB", [P, 2 * PAIRS, S5C])
        C3 = buf(ctx, nc, "s5_C3", [P, 3, 2 * PAIRS, S5C])
        dt = buf(ctx, nc, "s5_dt", [P, 2 * PAIRS])
        r = buf(ctx, nc, "s5_r", [P, 2 * PAIRS])
        hl = buf(ctx, nc, "s5_turns", [P, 3, 2 * PAIRS])
        phi = buf(ctx, nc, "s5_phi", [P, 2 * PAIRS])
        w1 = buf(ctx, nc, "s5_w1", [P, 2 * PAIRS])
        w2 = buf(ctx, nc, "s5_w2", [P, 2 * PAIRS])
        lr = buf(ctx, nc, "s5_lr", [P, 2 * PAIRS])
        li = buf(ctx, nc, "s5_li", [P, 2 * PAIRS])
        fr = buf(ctx, nc, "s5_fr", [P, 2 * PAIRS])
        fi = buf(ctx, nc, "s5_fi", [P, 2 * PAIRS])
        whole = buf(ctx, nc, "s5_exponent", [P, 2 * PAIRS], I32)
        quarter = buf(ctx, nc, "quarter_turn", [P, 1])
        steps = buf(ctx, nc, "steps", [P, 2, TOK])
        dcol = buf(ctx, nc, "s5_d", [P, 4])
        Bd = buf(ctx, nc, "s5_Bd", [P, 2, 2, 4, 2 * S5C])
        Cd = buf(ctx, nc, "s5_Cd", [P, 3, 2, 4, 2 * S5C])
        BT = buf(ctx, nc, "s5_BT", [P, 2, 2, P])
        cur = buf(ctx, nc, "s5_cur", [P, 3, 2, 4])
        turns = buf(ctx, nc, "s5_turns_cur", [P, 3, 2, 4])
        k_t = buf(ctx, nc, "s5_whole", [P, TOK])
        lo_t = buf(ctx, nc, "s5_rest", [P, TOK])
        ang = buf(ctx, nc, "s5_angle", [P, 2, TOK])
        ang_abs = buf(ctx, nc, "s5_angle_abs", [P, TOK])
        trig = buf(ctx, nc, "s5_trig", [P, 2, 2, TOK])
        g_in = buf(ctx, nc, "s5_g_in", [P, 4, TOK])
        g = buf(ctx, nc, "s5_g", [P, 2, TOK])
        prod = buf(ctx, nc, "s5_prod", [P, 2, 4, TOK])
        st = buf(ctx, nc, "s5_states", [P, 2, 2, PAIRS])
        y = buf(ctx, nc, "s5_y", [P, TOK])
        ucur = buf(ctx, nc, "s5_u", [P, TOK])
        dnow = buf(ctx, nc, "s5_d_cur", [P, 1])
        block = ctx.enter_context(nc.Block())
        BU = (slice(0, TOK), slice(1024, 1024 + TOK))
        Y0 = 4 * HALF
        BT0 = 6 * HALF
        ADA0 = 7 * HALF
        SCALE = 6.283185

        def block_units(a, m):
            return a.rearrange("p c (d k) -> p c d k", d=2)[:, :, :, bass.ds(m * 4, 4)]

        @block.sync
        def _(sp):
            for dst, src in ((par, "s5_par"), (B, "s5_B"), (C, "s5_C"), (dcol, "s5_d")):
                sp.dma_start(dst[:], T[src]).then_inc(par_in, 16)
            sp.dma_start(steps[:], T["s5_steps"].partition_broadcast(P)).then_inc(d_in, 16)

            def ada_load(n, b):
                sp.dma_start(ada[:, b, :], T["ada_rest"][n]).then_inc(ada_in[b], 16)
                sp.dma_start(ada_b[:, b, :], T["ada_b"][:, bass.ds(n * MOD_W + MOD_FIRST, MOD_W)]
                             ).then_inc(ada_in[b], 16)

            def ada_store(n, b):
                sp.wait_ge(ada_copied, n + 2)
                sp.dma_start(mod[:, bass.ds(n * MOD_W + MOD_FIRST, MOD_W)], rows[:, b, :]
                             ).then_inc(mod_out[b], 16)

            for b in range(2):
                ada_load(b, b)
            with sp.Fori(0, MOD_BLOCKS // 2 - 1) as i:
                for b in range(2):
                    sp.wait_ge(ada_used, i * 2 + (b + 1))
                    ada_load(i * 2 + (b + 2), b)
                    ada_store(i * 2 + b, b)
            for b in range(2):
                ada_store(MOD_BLOCKS - 2 + b, b)
                sp.wait_ge(mod_out[b], 16 * MOD_BLOCKS // 2 + 16)
            sp.wait_ge(y_out, 4)
            for part, out in ((0, out_re), (1, out_im)):
                sp.dma_start(out.rearrange("d (k g) s -> (g s) d k", g=2), st[:, part],
                             allow_slow_non_contiguous=True).then_inc(states_out, 16)
            sp.wait_ge(states_out, 32)

        @block.gpsimd
        def _(pool):
            line = Line(pool, pool_line)
            pool.wait_ge(d_in, 16)
            pool.wait_ge(bd_ready, 1)
            with line.loop(0, 4, 1 + UNITS * 7) as m:
                line.then(pool.tensor_copy(turns[:], block_units(hl, m)), mark)
                for u in range(UNITS):
                    q, d = u // 2, u % 2
                    b = u % 2
                    both, hi, lo = (turns[:, c, d, q:q + 1] for c in range(3))
                    s, a = steps[:, d, :], ang[:, b, :]
                    line.then(pool.tensor_scalar(k_t[:], s, both, ROUND, ALU.mult, ALU.add), mark)
                    wait_apart(pool, turn_used, m * UNITS + (u + 1), mark)
                    line.then(pool.tensor_scalar(k_t[:], k_t[:], 1.0, -ROUND, ALU.mult, ALU.add), mark)
                    line.then(pool.tensor_scalar(a, s, hi, 0.0, ALU.mult, ALU.add), mark)
                    line.then(pool.tensor_scalar(lo_t[:], s, lo, 0.0, ALU.mult, ALU.add))
                    line.then(pool.tensor_tensor(a, a, k_t[:], ALU.subtract))
                    line.then(pool.tensor_tensor(a, a, lo_t[:], ALU.add), mark)
                    line.then(pool.tensor_scalar(a, a, 0.5, -0.5, ALU.min, ALU.max))
                    pool.sem_inc(turn_set, 1)

        @block.scalar
        def _(act):
            line = Line(act, act_line)
            act.wait_ge(bd_ready, 1)
            line.then(act.activation(w1[:], phi[:], ACT.Sin, scale=SCALE))
            line.then(act.activation(w2[:], phi[:], ACT.Abs))
            line.then(act.activation(w2[:], w2[:], ACT.Sin, bias=quarter[:], scale=-SCALE))
            act.sem_inc(turn_used, 2)
            act.sem_inc(ada_copied, 1)
            for b in range(2):
                act.sem_inc(mod_out[b], 16)

            def ada_copy(m, u):
                b = u % 2
                act.wait_ge(ada_used, m * UNITS + (u + 1))
                act.wait_ge(mod_out[b], m * (16 * UNITS // 2) + 16 * (u // 2 + 1))
                act.activation(rows[:, b, :], ps[0:2, ADA0:ADA0 + MOD_W], ACT.Copy
                               ).then_inc(ada_copied, 1)
            with line.loop(0, 4, UNITS + 2) as m:
                for u in range(UNITS):
                    b = u % 2
                    act.wait_ge(turn_set, m * UNITS + (u + 1))
                    act.wait_ge(trig_used, m * UNITS + (u + 1))
                    line.then(act.activation(ang_abs[:], ang[:, b, :], ACT.Abs))
                    act.activation(trig[:, b, 1, :], ang[:, b, :], ACT.Sin, scale=SCALE
                                   ).then_inc(trig_set, 1)
                    act.activation(trig[:, b, 0, :], ang_abs[:], ACT.Sin, bias=quarter[:],
                                   scale=-SCALE).then_inc(trig_set, 1)
                    act.wait_ge(trig_set, m * (2 * UNITS) + (2 * u + 2))
                    act.sem_inc(turn_used, 1)
                    if u == 0:
                        act.wait_ge(bt_raw, m + 1)
                        line.then(act.activation(BT[:, :, :, :].rearrange("p a b n -> p (a b n)"),
                                                 ps[:, BT0:BT0 + 4 * P], ACT.Copy))
                        act.sem_inc(bt_ready, 1)
                    ada_copy(m, u)
                act.wait_ge(y_done, m * 2 + 2)
                line.then(act.activation(G[:, bass.ds(m, 1), :], y[:, :].unsqueeze(1),
                                         ACT.Gelu_apprx_tanh))
                act.sem_inc(y_out, 1)

        @block.tensor
        def _(pe):
            def bu(m, u):
                q, d = u // 2, u % 2
                pe.wait_ge(bu_used, m * UNITS + (u + 1))
                rows = slice(32 * q, 32 * q + 32)
                for part in range(2):
                    at = BU[part].start
                    for c0, c1 in ((0, HALF), (HALF, TOK)):
                        mm = pe.matmul(ps[:, at + c0:at + c1], BT[rows, d, part, :],
                                       ucur[rows, c0:c1], start=True, stop=True)
                mm.then_inc(bu_done, 1)

            def readout(m, u):
                q, d = u // 2, u % 2
                pe.wait_ge(prod_set, m * UNITS + (u + 1))
                for j, c in enumerate((0, 1, 2, 2)):
                    for c0, c1 in ((0, HALF), (HALF, TOK)):
                        mm = pe.matmul(ps[32 * q:32 * q + 32, Y0 + c0:Y0 + c1],
                                       Cd[:, c, d, q, :], prod[:, u % 2, j, c0:c1],
                                       start=(d == 0 and j == 0), stop=(d == 1 and j == 3))
                mm.then_inc(prod_used, 1)

            def ada_rows(m, u):
                b = u % 2
                pe.wait_ge(ada_in[b], m * (32 * UNITS // 2) + 32 * (u // 2 + 1))
                pe.wait_ge(ada_copied, m * UNITS + (u + 1))
                for k in range(KD):
                    pe.matmul(ps[0:2, ADA0:ADA0 + MOD_W], cond_s[:, k, :],
                              ada[:, b, k * MOD_W:(k + 1) * MOD_W], start=(k == 0), stop=False)
                pe.matmul(ps[0:2, ADA0:ADA0 + MOD_W], ones[:], ada_b[:, b, :],
                          start=False, stop=True).then_inc(ada_used, 1)

            pe.wait_ge(ones_set, 1)
            with pe.Fori(0, 4) as m:
                pe.wait_ge(bd_ready, m + 2)
                for d in range(2):
                    for part in range(2):
                        at = BT0 + (2 * d + part) * P
                        mm = pe.transpose(ps[:, at:at + P],
                                          Bd[:, d, part].rearrange("p q c -> p (q c)"), ident[:])
                mm.then_inc(bt_raw, 1)
                pe.wait_ge(bt_ready, m + 1)
                for u in range(UNITS):
                    bu(m, u)
                    ada_rows(m, u)
                    if u:
                        readout(m, u - 1)
                readout(m, UNITS - 1)

        @block.vector
        def _(dve):
            line = Line(dve, dve_line)
            one = line.then
            tt, ts = dve.tensor_tensor, dve.tensor_scalar
            dve.memset(ones[:], 1.0).then_inc(ones_set, 1)
            dve.memset(Bd[:], 0.0)
            dve.memset(Cd[:], 0.0)
            one(dve.memset(quarter[:], math.pi / 2))
            dve.wait_ge(par_in, 64)
            exact_exp(dve, one, dt[:], par[:, 2, :], w1[:], w2[:], whole[:])
            one(tt(lr[:], par[:, 0, :], dt[:], ALU.mult))
            exact_exp(dve, one, r[:], lr[:], w1[:], w2[:], whole[:])
            one(tt(phi[:], par[:, 1, :], dt[:], ALU.mult))
            one(ts(phi[:], phi[:], 1.0 / TWO_PI, None, ALU.mult))
            one(ts(w1[:], phi[:], ROUND, None, ALU.add))
            one(ts(w1[:], w1[:], ROUND, None, ALU.subtract))
            one(tt(phi[:], phi[:], w1[:], ALU.subtract))
            one(ts(w2[:], phi[:], 1536.0, None, ALU.add))
            one(ts(hl[:, 1, :], w2[:], 1536.0, None, ALU.subtract))
            one(tt(hl[:, 2, :], phi[:], hl[:, 1, :], ALU.subtract))
            one(dve.tensor_copy(hl[:, 0, :], phi[:]))
            dve.sem_inc(bd_ready, 1)
            dve.wait_ge(act_line, 3)
            one(tt(lr[:], r[:], w2[:], ALU.mult))
            one(tt(li[:], r[:], w1[:], ALU.mult))
            one(ts(lr[:], lr[:], -1.0, None, ALU.add))
            one(tt(w1[:], par[:, 0, :], par[:, 0, :], ALU.mult))
            one(tt(w2[:], par[:, 1, :], par[:, 1, :], ALU.mult))
            one(tt(w1[:], w1[:], w2[:], ALU.add))
            one(dve.reciprocal(w1[:], w1[:]))
            one(tt(fr[:], lr[:], par[:, 0, :], ALU.mult))
            one(tt(w2[:], li[:], par[:, 1, :], ALU.mult))
            one(tt(fr[:], fr[:], w2[:], ALU.add))
            one(tt(fr[:], fr[:], w1[:], ALU.mult))
            one(tt(fi[:], li[:], par[:, 0, :], ALU.mult))
            one(tt(w2[:], lr[:], par[:, 1, :], ALU.mult))
            one(tt(fi[:], fi[:], w2[:], ALU.subtract))
            one(tt(fi[:], fi[:], w1[:], ALU.mult))
            wide = [P, 2 * PAIRS, S5C]
            fr_w, fi_w = (f[:, :].unsqueeze(2).to_broadcast(wide) for f in (fr, fi))
            one(tt(Bb[:, 0], B[:, 0], fr_w, ALU.mult))
            one(tt(tmpB[:], B[:, 1], fi_w, ALU.mult))
            one(tt(Bb[:, 0], Bb[:, 0], tmpB[:], ALU.subtract))
            one(tt(Bb[:, 1], B[:, 1], fr_w, ALU.mult))
            one(tt(tmpB[:], B[:, 0], fi_w, ALU.mult))
            one(tt(Bb[:, 1], Bb[:, 1], tmpB[:], ALU.add))
            one(dve.tensor_copy(C3[:, 0], C[:, 0]))
            one(ts(C3[:, 1], C[:, 0], -1.0, None, ALU.mult))
            one(ts(C3[:, 2], C[:, 1], -1.0, None, ALU.mult))
            dve.sem_inc(trig_used, 2)
            dve.sem_inc(bu_used, 1)
            dve.wait_ge(d_in, 16)
            with line.loop(0, 4, 5 * UNITS + 2) as m:
                for n, (src, dst) in enumerate(((Bb, Bd), (C3, Cd))):
                    for part in range(2 + n):
                        for gr in range(2):
                            half = slice(64 * gr, 64 * gr + 64)
                            view = src[half, part].rearrange("p (d k) j -> p d k j", d=2)
                            to = dst[half, :, part] if n == 0 else dst[half, part]
                            dve.tensor_copy(to[:, :, :, S5C * gr:S5C * gr + S5C],
                                            view[:, :, bass.ds(m * 4, 4), :])
                dve.tensor_copy(ucur[:, :].unsqueeze(1), US[:, bass.ds(m, 1), :])
                dve.tensor_copy(cur[:, 0:1], block_units(r[:, :].unsqueeze(1), m))
                one(dve.tensor_copy(cur[:, 1:3], block_units(par[:, 3:5, :], m)))
                dve.sem_inc(bd_ready, 1)
                for u in range(UNITS):
                    q, d, b = u // 2, u % 2, u % 2
                    cos, sin = trig[:, b, 0, :], trig[:, b, 1, :]
                    way = (lambda a: a) if d == 0 else (lambda a: a[:, ::-1])
                    bre, bim = way(ps[:, BU[0]]), way(ps[:, BU[1]])
                    dve.wait_ge(bu_done, m * UNITS + (u + 1))
                    dve.wait_ge(trig_set, m * (2 * UNITS) + (2 * u + 2))
                    tt(g_in[:, 0], bre, cos, ALU.mult)
                    tt(g_in[:, 1], bim, sin, ALU.mult)
                    tt(g_in[:, 2], bim, cos, ALU.mult)
                    one(tt(g_in[:, 3], bre, sin, ALU.mult))
                    dve.sem_inc(bu_used, 1)
                    tt(g_in[:, 0], g_in[:, 0], g_in[:, 1], ALU.add)
                    one(tt(g_in[:, 2], g_in[:, 2], g_in[:, 3], ALU.subtract))
                    for part in range(2):
                        for a, z, cached in SEGMENTS[d]:
                            first = cur[:, 1 + part, d, q:q + 1] if cached else 0.0
                            ins = dve.tensor_tensor_scan(
                                g[:, part, a:z], cur[:, 0, d, q:q + 1].to_broadcast([P, z - a]),
                                g_in[:, 2 * part, a:z], first, ALU.mult, ALU.add)
                    one(ins)
                    dve.wait_ge(prod_used, m * UNITS + u - 1) if u >= 2 else None
                    for j, (part, f) in enumerate(((0, cos), (1, sin), (0, sin), (1, cos))):
                        ins = tt(way(prod[:, b, j, :]), g[:, part, :], f, ALU.mult)
                    one(ins)
                    dve.sem_inc(prod_set, 1)
                    dve.sem_inc(trig_used, 1)
                    last = CTX - 1 if d == 0 else 0
                    one_st = [prod[:, b, j, last:last + 1].unsqueeze(1) for j in range(4)]
                    at = bass.ds(m * 4 + q, 1)
                    tt(st[:, 0, d:d + 1, at], one_st[0], one_st[1], ALU.subtract)
                    one(tt(st[:, 1, d:d + 1, at], one_st[2], one_st[3], ALU.add))
                dve.wait_ge(prod_used, m * UNITS + UNITS)
                dve.tensor_copy(dnow[:], dcol[:, bass.ds(m, 1)]).then_inc(y_done, 1)
                dve.wait_ge(y_done, m * 2 + 1)
                one(dve.scalar_tensor_tensor(out=y[:], in0=ucur[:], scalar=dnow[:],
                                             in1=ps[:, Y0:Y0 + TOK], op0=ALU.mult, op1=ALU.add))
                dve.sem_inc(y_done, 1)


def s5_gate(nc, T, ps, G, MIXT):
    with stage(nc, "w_in", "mm_done", "sig_done", "bank_free") as (
            ctx, (w_in, mm_done, sig_done, bank_free)):
        w = buf(ctx, nc, "glu_w", [P, 4, 4 * P])
        bcol = buf(ctx, nc, "glu_b", [P, 4])
        sig = buf(ctx, nc, "glu_gate", [P, 4, TOK])
        block = ctx.enter_context(nc.Block())

        @block.sync
        def _(sp):
            sp.dma_start(w[:], T["glu_w"]).then_inc(w_in, 16)
            sp.dma_start(bcol[:], T["glu_b"]).then_inc(w_in, 16)
            sp.wait_ge(w_in, 32)

        @block.tensor
        def _(pe):
            pe.wait_ge(w_in, 32)
            for m in range(4):
                at = 2 * m * HALF
                for k in range(4):
                    lhs = w[:, k, m * P:(m + 1) * P]
                    pe.matmul(ps[:, at:at + HALF], lhs, G[:, k, 0:HALF], start=(k == 0), stop=(k == 3))
                    mm = pe.matmul(ps[:, at + HALF:at + TOK], lhs, G[:, k, HALF:TOK],
                                   start=(k == 0), stop=(k == 3))
                mm.then_inc(mm_done, 1)

        @block.scalar
        def _(act):
            for m in range(4):
                act.wait_ge(mm_done, m + 1)
                act.activation(sig[:, m, :], ps[:, 2 * m * HALF:2 * m * HALF + TOK], ACT.Sigmoid,
                               bias=bcol[:, m:m + 1]).then_inc(sig_done, 1)

        @block.vector
        def _(dve):
            for m in range(4):
                dve.wait_ge(sig_done, m + 1)
                dve.tensor_tensor(MIXT[:, 4 + m, :], sig[:, m, :], G[:, m, :],
                                  ALU.mult).then_inc(bank_free, 1)
            dve.wait_ge(bank_free, 4)


def project_out(nc, ps, MIXT, W, X, mod, layer, g_chunk):
    with stage(nc, "w_in", "g_in", "mm_done", "bank_free", "dve_line") as (
            ctx, (w_in, g_in, mm_done, bank_free, dve_line)):
        w = buf(ctx, nc, "w_out", [P, KD, D])
        g_row = buf(ctx, nc, "gate_row", [P, 2, D])
        tmp = buf(ctx, nc, "gated", [P, 2, HALF])
        block = ctx.enter_context(nc.Block())

        @block.sync
        def _(sp):
            sp.dma_start(w[:], W).then_inc(w_in, 16)
            for g in range(2):
                sp.dma_start(g_row[:, g, :], mod_row(mod, layer, g, g_chunk)).then_inc(g_in, 16)

        @block.tensor
        def _(pe):
            pe.wait_ge(w_in, 16)
            for n in range(2 * NT):
                t, c = n // 2, n % 2
                if n >= 4:
                    pe.wait_ge(bank_free, n - 3)
                at = (n % 4) * HALF
                for k in range(KD):
                    mm = pe.matmul(ps[:, at:at + HALF], MIXT[:, k, t * P:(t + 1) * P],
                                   w[:, k, c * HALF:(c + 1) * HALF], start=(k == 0), stop=(k == KD - 1))
                mm.then_inc(mm_done, 1)

        @block.vector
        def _(dve):
            dve.wait_ge(g_in, 32)
            for n in range(2 * NT):
                t, c = n // 2, n % 2
                dve.wait_ge(mm_done, n + 1)
                at = (n % 4) * HALF
                col = slice(c * HALF, (c + 1) * HALF)
                dve.tensor_tensor(tmp[:, c, :], ps[:, at:at + HALF], g_row[:, group_of(t), col],
                                  ALU.mult).then_inc(bank_free, 1)
                dve.wait_ge(bank_free, n + 1)
                dve.tensor_tensor(X[:, t, col], X[:, t, col], tmp[:, c, :], ALU.add
                                  ).then_inc(dve_line, 1)
            dve.wait_ge(dve_line, 2 * NT)


MLH = 8
VN = P + 1
KINDS = 4


def mlstm_inputs(nc, T, ps, HT, ident, QK, VX, O, negM, COLS, KEEP, out_m):
    R = 2 * TOK
    blocks = 2 * MLH
    W2 = 2 * P
    FIRST = 6
    with stage(nc, "in_done", "mm_done", "raw_ready", "abs_done", "e_ready", "ln_done", "x_ready",
               "exp_done", "rows_ready", "dve_line", "turned", "m_out", "w_in0", "w_in1", "used",
               "qk_out", "taps_in", "conv_done", "silu_done", "tok_done", "tok_out") as (
            ctx, (in_done, mm_done, raw_ready, abs_done, e_ready, ln_done, x_ready, exp_done,
                  rows_ready, dve_line, turned, m_out, w_in0, w_in1, used, qk_out, taps_in,
                  conv_done, silu_done, tok_done, tok_out)):
        w_in = (w_in0, w_in1)
        wblk = buf(ctx, nc, "w_block", [P, 2, KD * W2])
        taps = buf(ctx, nc, "conv_taps", [P, blocks, 4])
        cur = buf(ctx, nc, "conv_taps_cur", [P, 4])
        src = buf(ctx, nc, "conv_source", [P, TOK])
        y = buf(ctx, nc, "conv_block", [P, 2, TOK])
        wg = buf(ctx, nc, "gate_w", [P, KD, P])
        gb = buf(ctx, nc, "gate_b", [MLH, 4])
        m0 = buf(ctx, nc, "m_cached", [MLH, 2])
        nat = buf(ctx, nc, "gate_rows", [MLH, KINDS, 2, TOK])
        flat4 = nat[:, :, :, :].rearrange("h k d s -> h (k d s)")
        raw = flat4[:, 0:4 * TOK].rearrange("h (j s) -> h j s", j=4)
        e = flat4[:, 4 * TOK:6 * TOK].rearrange("h (d s) -> h d s", d=2)
        ig = flat4[:, 6 * TOK:8 * TOK].rearrange("h (d s) -> h d s", d=2)
        lf = buf(ctx, nc, "gate_logf", [MLH, 2, TOK])
        b = buf(ctx, nc, "gate_b_sum", [MLH, R])
        w = buf(ctx, nc, "gate_w_row", [MLH, R])
        M = lf[:, :, :].rearrange("h d s -> h (d s)")
        mp = buf(ctx, nc, "m_before", [MLH, 2, NT])
        ML = buf(ctx, nc, "M_last", [MLH, 2, NT])
        mn = buf(ctx, nc, "m_after", [MLH, 2, NT])
        kp = buf(ctx, nc, "state_keep", [MLH, 2 * NT])
        X4 = buf(ctx, nc, "gate_args", [MLH, 3, R])
        keeper = X4[:, 0, :]
        drop = X4[:, 1, :]
        diag = buf(ctx, nc, "keep_diag", [MLH, 2 * NT, MLH])
        ones8 = buf(ctx, nc, "ones8", [MLH, P])
        block = ctx.enter_context(nc.Block())
        chunks = lambda a: a.rearrange("h (c s) -> h c s", s=P)
        LATB, CTXB = (2 * HALF, 4 * HALF), (3 * HALF, 5 * HALF)
        TOKB = (6 * HALF, 7 * HALF)

        @block.sync
        def _(sp):
            for dst, src_ in ((wg, "gate_w"), (gb, "gate_b"), (m0, "ml_m0")):
                sp.dma_start(dst[:], T[src_]).then_inc(in_done, 16)
            for c in range(2):
                sp.dma_start(wblk[:, c, 0:KD * P], T["od_w_qk"][c]).then_inc(w_in[c], 16)
            sp.dma_start(taps[:], T["ml_taps"]).then_inc(taps_in, 16)
            with sp.Fori(1, blocks // 2) as i:
                for c in range(2):
                    sp.wait_ge(used, 2 * i + (c - 1))
                    sp.dma_start(wblk[:, c, 0:KD * P], T["od_w_qk"][2 * i + c]
                                 ).then_inc(w_in[c], 16)
            for n in range(8):
                c = n % 2
                if n < 2:
                    sp.wait_ge(used, blocks - 1 + n)
                else:
                    sp.wait_ge(tok_done, NT * (n - 1))
                sp.dma_start(wblk[:, c, :], T["od_w_vo"][n]).then_inc(w_in[c], 16)
            sp.wait_ge(x_ready, 1)
            sp.dma_start(out_m[0].unsqueeze(1), mn[:, 0, 0:1],
                         allow_slow_non_contiguous=True).then_inc(m_out, 16)
            sp.dma_start(out_m[1].unsqueeze(1), mn[:, 1, NT - 1:NT],
                         allow_slow_non_contiguous=True).then_inc(m_out, 16)
            sp.wait_ge(m_out, 32)

        @block.tensor
        def _(pe):
            pe.wait_ge(in_done, 48)
            for k in range(KD):
                pe.matmul(ps[:, 0:HALF], wg[:, k, :], HT[:, k, 0:HALF],
                          start=(k == 0), stop=(k == KD - 1))
                mm = pe.matmul(ps[:, HALF:TOK], wg[:, k, :], HT[:, k, HALF:TOK],
                               start=(k == 0), stop=(k == KD - 1))
            mm.then_inc(mm_done, 1)

            def channels(c):
                for k in range(KD):
                    lhs = wblk[:, c, k * P:(k + 1) * P]
                    pe.matmul(ps[:, LATB[c]:LATB[c] + LAT], lhs, HT[:, k, CTX:TOK],
                              start=(k == 0), stop=(k == KD - 1))
                    mm = pe.matmul(ps[:, CTXB[c]:CTXB[c] + CTX], lhs, HT[:, k, 0:CTX],
                                   start=(k == 0), stop=(k == KD - 1))
                mm.then_inc(used, 1)

            for c in range(2):
                pe.wait_ge(w_in[c], 16)
                channels(c)
            with pe.Fori(1, blocks // 2) as i:
                for c in range(2):
                    pe.wait_ge(w_in[c], 16 * i + 16)
                    pe.wait_ge(qk_out, 2 * i + (c - 1))
                    channels(c)
            with pe.Fori(0, 4) as i:
                for c in range(2):
                    pe.wait_ge(w_in[c], 16 * i + (16 * blocks // 2 + 16))
                    for t in range(NT):
                        g = c * NT + t
                        pe.wait_ge(tok_out, i * (2 * NT) + (g + 1))
                        at = TOKB[g % 2]
                        for k in range(KD):
                            mm = pe.matmul(ps[:, at:at + W2], HT[:, k, t * P:(t + 1) * P],
                                           wblk[:, c, k * W2:(k + 1) * W2],
                                           start=(k == 0), stop=(k == KD - 1))
                        mm.then_inc(tok_done, 1)
            pe.wait_ge(rows_ready, 1)
            for kind in range(KINDS):
                for d in range(2):
                    for t in range(NT):
                        at = ((kind * 2 + d) * NT + t) * MLH
                        mm = pe.transpose(ps[:, at:at + MLH], nat[:, kind, d, t * P:(t + 1) * P],
                                          ident[0:MLH, 0:MLH])
            mm.then_inc(turned, 1)
            pe.matmul(ps[:, HALF:HALF + 2 * NT * MLH], ones8[:],
                      diag[:, :, :].rearrange("h c g -> h (c g)"), start=True, stop=True
                      ).then_inc(turned, 1)

        @block.scalar
        def _(act):
            act.wait_ge(raw_ready, 1)
            act.sem_inc(tok_out, 2)
            act.activation(e[:], raw[:, 2:4, :], ACT.Abs).then_inc(abs_done, 1)
            act.wait_ge(abs_done, 1)
            act.activation(e[:], e[:], ACT.Exp, scale=-1.0).then_inc(abs_done, 1)
            act.wait_ge(e_ready, 1)
            act.activation(e[:], e[:], ACT.Ln).then_inc(ln_done, 1)

            def drain(i, c):
                act.wait_ge(used, 2 * i + (c + 1))
                act.activation(QK[:, bass.ds(2 * i + c, 1), CTX:TOK],
                               ps[:, LATB[c]:LATB[c] + LAT].unsqueeze(1), ACT.Copy)
                act.activation(QK[:, bass.ds(2 * i + c, 1), 0:CTX],
                               ps[:, CTXB[c]:CTXB[c] + CTX].unsqueeze(1), ACT.Copy
                               ).then_inc(qk_out, 1)

            def silu(n, c):
                act.wait_ge(conv_done, n + 1)
                act.activation(QK[:, bass.ds(n, 1), :], y[:, c, :].unsqueeze(1),
                               ACT.Silu).then_inc(silu_done, 1)

            def values(i, place, silus):
                for g in range(2 * NT):
                    act.wait_ge(tok_done, i * (2 * NT) + (g + 1))
                    act.activation(place(i, g // NT, g % NT),
                                   ps[:, TOKB[g % 2]:TOKB[g % 2] + W2]
                                   .rearrange("p (h v) -> p h v", v=P), ACT.Copy
                                   ).then_inc(tok_out, 1)
                    if silus and g % 3 == 2:
                        n = blocks - FIRST + i * 3 + g // 3
                        silu(n, n % 2)

            with act.Fori(0, FIRST // 2) as i:
                for c in range(2):
                    drain(i, c)
            act.wait_ge(x_ready, 1)
            act.activation(X4[:], X4[:], ACT.Exp).then_inc(exp_done, 1)
            act.activation(kp[:], kp[:], ACT.Exp).then_inc(exp_done, 1)
            with act.Fori(FIRST // 2, blocks // 2) as i:
                for c in range(2):
                    drain(i, c)
                    silu(i * 2 + (c - FIRST), c)
            for i in range(2):
                values(i, lambda i, c, t: VX[:, t, bass.ds(i * 4 + 2 * c, 2), 0:P], True)
            with act.Fori(2, 4) as i:
                values(i, lambda i, c, t: O[:, t, bass.ds(i * (2 * W2) + (c * W2 - 4 * W2), W2)]
                       .rearrange("p (h v) -> p h v", v=P), False)

        @block.vector
        def _(dve):
            line = Line(dve, dve_line)
            one, tt, ts = line.then, dve.tensor_tensor, dve.tensor_scalar
            dve.memset(keeper, 1.0)
            dve.memset(drop, 0.0)
            one(dve.memset(ones8[:], 1.0))
            dve.memset(chunks(keeper)[:, :, 0:1], 0.0)
            one(dve.memset(chunks(drop)[:, :, 0:1], LOWEST))
            dve.wait_ge(in_done, 48)
            dve.wait_ge(mm_done, 1)
            for j in (2, 3, 0, 1):
                ins = ts(raw[:, j, :], ps[32 * j:32 * j + MLH, 0:TOK], gb[:, j:j + 1], None, ALU.add)
            one(ins)
            dve.sem_inc(raw_ready, 1)
            dve.wait_ge(abs_done, 2)
            one(ts(e[:], e[:], 1.0, None, ALU.add))
            dve.sem_inc(e_ready, 1)
            dve.wait_ge(ln_done, 1)
            for d in range(2):
                way = (lambda a: a) if d == 0 else (lambda a: a[:, ::-1])
                dve.scalar_tensor_tensor(out=lf[:, d, :], in0=way(raw[:, 2 + d, :]), scalar=0.0,
                                         in1=way(e[:, d, :]), op0=ALU.min, op1=ALU.subtract)
                ins = dve.tensor_copy(ig[:, d, :], way(raw[:, d, :]))
            one(ins)
            flat = lambda a: a.rearrange("h d s -> h (d s)")
            wide = [MLH, 2 * NT, P]
            one(dve.tensor_tensor_scan(b[:], keeper, flat(lf[:, :, :]), 0.0, ALU.mult, ALU.add))
            one(tt(w[:], flat(ig), b[:], ALU.subtract))
            one(dve.tensor_tensor_scan(M, drop, w[:], LOWEST, ALU.add, ALU.max))
            last = lambda a, c: chunks(a)[:, c, P - 1:P]
            one(dve.memset(mp[:], 0.0))
            dve.tensor_copy(mp[:, 0, 1:2], m0[:, 0:1])
            one(dve.tensor_copy(mp[:, 1, 0:1], m0[:, 1:2]))
            for step in range(NT):
                both = [((0, None), (1, 2), (2, 3), (3, 4), (4, None))[step],
                        ((4, None), (0, 1), (1, 2), (2, 3), (3, None))[step]]
                for d, (c, after) in enumerate(both):
                    ins = tt(ML[:, d, c:c + 1], mp[:, d, c:c + 1], last(M, d * NT + c), ALU.max)
                one(ins)
                for d, (c, after) in enumerate(both):
                    ins = tt(mn[:, d, c:c + 1], ML[:, d, c:c + 1], last(b[:, :], d * NT + c),
                             ALU.add)
                one(ins)
                if both[0][1] is not None:
                    for d, (c, after) in enumerate(both):
                        ins = dve.tensor_copy(mp[:, d, after:after + 1], mn[:, d, c:c + 1])
                    one(ins)
            mpw = flat(mp[:, :, :]).unsqueeze(2).to_broadcast(wide)
            mlw = flat(ML[:, :, :]).unsqueeze(2).to_broadcast(wide)
            tt(chunks(X4[:, 0, :]), chunks(w[:, :]), mlw, ALU.subtract)
            one(tt(chunks(M), chunks(M), mpw, ALU.max))
            tt(chunks(X4[:, 1, :]), mpw, chunks(M), ALU.subtract)
            dve.scalar_tensor_tensor(out=X4[:, 2, :], in0=b[:], scalar=-1.0, in1=M,
                                     op0=ALU.mult, op1=ALU.subtract)
            one(tt(kp[:], flat(mp[:, :, :]), flat(ML[:, :, :]), ALU.subtract))
            dve.sem_inc(x_ready, 1)
            one(ts(M, M, -1.0, None, ALU.mult))
            dve.wait_ge(exp_done, 2)
            rows = [w[:, :]] + [X4[:, j, :] for j in range(3)]
            for d in range(2):
                way = (lambda a: a) if d == 0 else (lambda a: a[:, ::-1])
                for kind, row in enumerate(rows):
                    dve.tensor_copy(nat[:, kind, d, :], way(row[:, d * TOK:(d + 1) * TOK]))
                dve.tensor_copy(negM[:, d, :], way(M[:, d * TOK:(d + 1) * TOK]))
            w8 = [MLH, 2 * NT, MLH]
            one(tt(diag[:], ident[0:MLH, 0:MLH].unsqueeze(1).to_broadcast(w8),
                   kp[:, :].unsqueeze(2).to_broadcast(w8), ALU.mult))
            dve.sem_inc(rows_ready, 1)
            dve.wait_ge(taps_in, 16)
            dve.sem_inc(silu_done, 2)
            with line.loop(0, blocks // 2, 8) as i:
                for c in range(2):
                    dve.wait_ge(qk_out, i * 2 + (c + 1))
                    dve.tensor_copy(src[:, :].unsqueeze(1), QK[:, bass.ds(i * 2 + c, 1), :])
                    line.then(dve.tensor_copy(cur[:, :].unsqueeze(1),
                                              taps[:, bass.ds(i * 2 + c, 1), :]))
                    dve.wait_ge(silu_done, i * 2 + (c + 1))
                    short_conv(dve, line, y[:, c, :], src[:, :], lambda k: cur[:, k:k + 1])
                    dve.sem_inc(conv_done, 1)
            dve.wait_ge(turned, 2)
            one(dve.tensor_copy(COLS[:, :, :].rearrange("p c h -> p (c h)"),
                                ps[:, 0:KINDS * 2 * NT * MLH]))
            one(dve.tensor_copy(KEEP[:, :, :].rearrange("p c h -> p (c h)"),
                                ps[:, HALF:HALF + 2 * NT * MLH]))


def turn_keys(nc, ps, QK, KT, ident):
    with stage(nc, "turned", "out_done") as (ctx, (turned, out_done)):
        block = ctx.enter_context(nc.Block())

        @block.tensor
        def _(pe):
            for n in range(2 * NT):
                t, q = n // 2, n % 2
                if n >= 4:
                    pe.wait_ge(out_done, n - 3)
                for h in range(4):
                    at = (n % 4) * HALF + h * P
                    mm = pe.transpose(ps[:, at:at + P], QK[:, MLH + 4 * q + h, t * P:(t + 1) * P],
                                      ident[:])
                mm.then_inc(turned, 1)

        @block.scalar
        def _(act):
            for n in range(2 * NT):
                t, q = n // 2, n % 2
                act.wait_ge(turned, n + 1)
                at = (n % 4) * HALF
                act.activation(KT[:, t, 4 * q:4 * q + 4, :], ps[:, at:at + HALF]
                               .rearrange("p (h v) -> p h v", v=P), ACT.Copy).then_inc(out_done, 1)


def mlstm_cells(nc, T, ps, QK, KT, VX, HM, negM, COLS, KEEP, ident, out_C, out_n):
    with stage(nc, "cn_in", "v_ones", "mask_line", "mask_done", "pair_set", "pair_copied",
               "scores_done", "exp_done", "share_done", "share_out", "st_done", "second_done",
               "state_set", "tail_done", "dve_line", "state_out") as (
            ctx, (cn_in, v_ones, mask_line, mask_done, pair_set, pair_copied, scores_done,
                  exp_done, share_done, share_out, st_done, second_done, state_set, tail_done,
                  dve_line, state_out)):
        CN0 = buf(ctx, nc, "state_cached", [P, 2, MLH, VN])
        CNo = buf(ctx, nc, "state_ctx", [P, 2, MLH, VN])
        CN = buf(ctx, nc, "state", [P, 2, 2, VN])
        CNk = buf(ctx, nc, "state_kept", [P, 2, 2, VN])
        mask = buf(ctx, nc, "mask", [P, 2, P])
        pick = buf(ctx, nc, "head_pick", [MLH, 2, P])
        q = buf(ctx, nc, "q_heads", [P, 2, TOK])
        k = buf(ctx, nc, "k_heads", [P, 2, TOK])
        cols = buf(ctx, nc, "cols_heads", [P, KINDS * 2 * NT, 2])
        keep = buf(ctx, nc, "keep_heads", [P, 2 * NT, 2])
        E = buf(ctx, nc, "weights", [P, 2, 2, P])
        ST = buf(ctx, nc, "scores_T", [P, 2, 2, P])
        kw = buf(ctx, nc, "k_weighted", [P, 2, 2, P])
        share = buf(ctx, nc, "state_share", [P, 2, 2, 2, VN])
        nd = buf(ctx, nc, "num_den", [P, 2, 2, VN])
        den = buf(ctx, nc, "den", [P, 2, 2, 1])
        block = ctx.enter_context(nc.Block())
        pairs = MLH // 2
        es = ps[:, 0:2 * HALF].rearrange("p (d h e n) -> p d h e n", d=2, h=2, e=2)

        def units(bank):
            return (ps[:, bank * HALF:(bank + 2) * HALF].rearrange("p (d n) -> p d n", d=2)
                    [:, :, 0:2 * VN].rearrange("p d (h n) -> p d h n", h=2))
        shared, added, chunk = units(2), units(4), units(6)

        def tiles(i):
            return i, (NT - i) % NT

        def col(kind, i):
            a, z = (kind * 2 * NT + d * NT + t for d, t in enumerate(tiles(i)))
            return cols[:, a:z + 1:z - a, :]

        @block.sync
        def _(sp):
            sp.dma_start(CN0[:], T["ml_CN0"]).then_inc(cn_in, 16)
            sp.wait_ge(tail_done, pairs * NT + 1)
            for d in range(2):
                sp.dma_start(out_C[d].rearrange("h k v -> k h v"), CNo[:, d, :, 0:P]
                             ).then_inc(state_out, 16)
                sp.dma_start(out_n[d].rearrange("h k -> k h").unsqueeze(2), CNo[:, d, :, P:VN],
                             allow_slow_non_contiguous=True).then_inc(state_out, 16)
            sp.wait_ge(state_out, 64)

        @block.gpsimd
        def _(pool):
            pool.memset(VX[:, :, :, P:VN], 1.0).then_inc(v_ones, 1)
            pool.memset(mask[:], 0.0).then_inc(mask_line, 1)
            pool.wait_ge(mask_line, 1)
            for d, way in ((0, 1), (1, -1)):
                pool.affine_select(out=mask[:, d, :], in_=mask[:, d, :], compare_op=ALU.is_ge,
                                   fill=-1.0e30, base=0, pattern=[[way, P]],
                                   channel_multiplier=-way).then_inc(mask_done, 1)
            pool.wait_ge(mask_done, 2)
            pool.wait_ge(v_ones, 1)

        @block.scalar
        def _(act):
            with act.Fori(0, pairs) as p:
                act.wait_ge(second_done, p * NT + 1)
                act.activation(q[:], QK[:, bass.ds(p * 2, 2), :], ACT.Copy, scale=float(P) ** -0.5)
                act.activation(k[:], QK[:, bass.ds(p * 2 + MLH, 2), :], ACT.Copy
                               ).then_inc(pair_copied, 1)
                act.wait_ge(pair_set, p + 1)
                for i in range(NT):
                    act.wait_ge(scores_done, p * NT + (i + 1))
                    for d in range(2):
                        for h in range(2):
                            ins = act.activation(E[:, d, h, :], es[:, d, h, 0, :], ACT.Exp,
                                                 bias=col(0, i)[:, d, h:h + 1])
                    ins.then_inc(exp_done, 1)
                    act.wait_ge(share_done, p * NT + (i + 1))
                    act.wait_ge(tail_done, p * NT + max(i, 1))
                    for d in range(2):
                        for h in range(2):
                            ins = act.activation(share[:, i % 2, d, h, :], shared[:, d, h, :],
                                                 ACT.Copy, scale=col(2, i)[:, d, h:h + 1])
                    ins.then_inc(share_out, 1)

        @block.tensor
        def _(pe):
            pe.wait_ge(mask_done, 2)
            pe.wait_ge(v_ones, 1)

            def scores(i):
                for d, t in enumerate(tiles(i)):
                    tile = slice(t * P, (t + 1) * P)
                    for h in range(2):
                        pe.matmul(es[:, d, h, 0, :], ident[:], mask[:, d, :],
                                  start=True, stop=False)
                        pe.matmul(es[:, d, h, 0, :], pick[:, h, :], negM[:, d, tile],
                                  start=False, stop=True)
                        mm = pe.matmul(es[:, d, h, 1, :], k[:, h, tile], q[:, h, tile],
                                       start=True, stop=True)
                mm.then_inc(scores_done, 1)

            with pe.Fori(0, pairs) as p:
                pe.wait_ge(pair_set, p + 1)
                pe.wait_ge(pair_copied, p + 1)
                scores(0)
                for i in range(NT):
                    pe.wait_ge(state_set, p * (NT + 1) + (i + 1))
                    pe.wait_ge(share_out, p * NT + (i + 1))
                    for d, t in enumerate(tiles(i)):
                        for h in range(2):
                            mm = pe.matmul(shared[:, d, h, :], q[:, h, t * P:(t + 1) * P],
                                           CN[:, d, h, :], start=True, stop=True)
                    mm.then_inc(share_done, 1)
                    pe.wait_ge(st_done, p * NT + (i + 1))
                    for out, lhs in ((added, kw), (chunk, ST)):
                        for d, t in enumerate(tiles(i)):
                            for h in range(2):
                                v = VX[:, t, bass.ds(p * 2 + h, 1), :].rearrange("p h n -> p (h n)")
                                mm = pe.matmul(out[:, d, h, :], lhs[:, d, h, :], v,
                                               start=True, stop=True)
                    mm.then_inc(second_done, 1)
                    if i < NT - 1:
                        scores(i + 1)

        @block.vector
        def _(dve):
            line = Line(dve, dve_line)
            one, tt, ts = line.then, dve.tensor_tensor, dve.tensor_scalar
            full = [P, 2, 2, VN]
            dve.wait_ge(cn_in, 16)
            for free in (second_done, share_out, tail_done):
                dve.sem_inc(free, 1)

            def weigh_keys(p, i):
                for d, t in enumerate(tiles(i)):
                    ins = tt(kw[:, d], KT[:, t, bass.ds(p * 2, 2), :],
                             col(1, i)[:, d, :].unsqueeze(2).to_broadcast([P, 2, P]), ALU.mult)
                line.count(ins)

            with line.loop(0, pairs, 2 + 9 * NT) as p:
                dve.tensor_copy(pick[:], ident[0:MLH, bass.ds(p * 2, 2)].unsqueeze(2)
                                .to_broadcast([MLH, 2, P]))
                dve.tensor_copy(cols[:], COLS[:, :, bass.ds(p * 2, 2)])
                dve.tensor_copy(keep[:], KEEP[:, :, bass.ds(p * 2, 2)])
                one(dve.memset(CN[:], 0.0))
                dve.sem_inc(pair_set, 1)
                dve.sem_inc(state_set, 1)
                weigh_keys(p, 0)
                for i in range(NT):
                    dve.wait_ge(exp_done, p * NT + (i + 1))
                    one(tt(ST[:], es[:, :, :, 1, :], E[:], ALU.mult))
                    dve.sem_inc(st_done, 1)
                    a, z = i, NT + (NT - 1 - tiles(i)[1])
                    kept = keep[:, a:z + 1:z - a, :].unsqueeze(3).to_broadcast(full)
                    one(tt(CNk[:], CN[:], kept, ALU.mult))
                    dve.wait_ge(second_done, p * NT + (i + 2))
                    if i == 0:
                        tt(CNo[:, :, bass.ds(p * 2, 2), :], CNk[:], added, ALU.add)
                        one(dve.tensor_copy(CN[:], CN0[:, :, bass.ds(p * 2, 2), :]))
                    else:
                        one(tt(CN[:], CNk[:], added, ALU.add))
                    dve.sem_inc(state_set, 1)
                    dve.wait_ge(share_out, p * NT + (i + 2))
                    one(tt(nd[:], share[:, i % 2], chunk, ALU.add))
                    n_dot = nd[:, :, :, P:VN]
                    one(dve.scalar_tensor_tensor(out=den[:], in0=n_dot, scalar=-1.0, in1=n_dot,
                                                 op0=ALU.mult, op1=ALU.max))
                    one(tt(den[:], den[:], col(3, i).unsqueeze(3), ALU.max))
                    one(dve.reciprocal(den[:], den[:]))
                    for d, t in enumerate(tiles(i)):
                        out = HM[:, t, bass.ds(p * 2, 2), :]
                        row = nd[:, d, :, 0:P]
                        by = den[:, d].to_broadcast([P, 2, P])
                        if (d, t) in ((0, 0), (0, 1), (0, 2), (1, 4), (1, 3)):
                            ins = tt(out, row, by, ALU.mult)
                        else:
                            one(tt(row, row, by, ALU.mult))
                            ins = tt(out, row, out, ALU.add)
                    if i < NT - 1:
                        weigh_keys(p, i + 1)
                    else:
                        line.count(ins)
                    line.settle()
                    dve.sem_inc(tail_done, 1)


def mlstm_finish(nc, T, ps, HM, O, MIXT, ident):
    with stage(nc, "g_in", "silu_done", "ms_ready", "rooted", "dve_line", "h_ready", "turned",
               "out_done") as (ctx, (g_in, silu_done, ms_ready, rooted, dve_line, h_ready, turned,
                                     out_done)):
        g = buf(ctx, nc, "norm_row", [P, D])
        sq = buf(ctx, nc, "squares", [P, MLH, P])
        ms = buf(ctx, nc, "mean_square", [P, NT, MLH])
        block = ctx.enter_context(nc.Block())

        @block.sync
        def _(sp):
            sp.dma_start(g[:], T["ml_norm_g"].partition_broadcast(P)).then_inc(g_in, 16)

        @block.scalar
        def _(act):
            for t in range(NT):
                act.activation(O[:, t, :], O[:, t, :], ACT.Silu).then_inc(silu_done, 1)
            act.wait_ge(ms_ready, 1)
            act.activation(ms[:], ms[:], ACT.Sqrt).then_inc(rooted, 1)
            for n in range(2 * NT):
                t, q = n // 2, n % 2
                act.wait_ge(turned, n + 1)
                at = (n % 4) * HALF
                act.activation(MIXT[:, 4 * q:4 * q + 4, t * P:(t + 1) * P], ps[:, at:at + HALF]
                               .rearrange("p (k c) -> p k c", k=4), ACT.Copy).then_inc(out_done, 1)

        @block.vector
        def _(dve):
            line = Line(dve, dve_line)
            one, tt = line.then, dve.tensor_tensor
            for t in range(NT):
                one(tt(sq[:], HM[:, t], HM[:, t], ALU.mult))
                one(dve.tensor_reduce(ms[:, t, :], sq[:], AX.X, ALU.add))
            one(dve.tensor_scalar(ms[:], ms[:], 1.0 / P, EPS, ALU.mult, ALU.add))
            dve.reciprocal(ms[:], ms[:]).then_inc(ms_ready, 1)
            dve.wait_ge(rooted, 1)
            dve.wait_ge(g_in, 16)
            dve.wait_ge(silu_done, NT)
            for t in range(NT):
                flat = HM[:, t].rearrange("p h v -> p (h v)")
                one(tt(HM[:, t], HM[:, t], ms[:, t, :].unsqueeze(2).to_broadcast([P, MLH, P]),
                       ALU.mult))
                one(tt(flat, flat, g[:], ALU.mult))
                tt(flat, flat, O[:, t, :], ALU.mult).then_inc(h_ready, 1)

        @block.tensor
        def _(pe):
            for n in range(2 * NT):
                t, q = n // 2, n % 2
                pe.wait_ge(h_ready, t + 1)
                if n >= 4:
                    pe.wait_ge(out_done, n - 3)
                for k in range(4):
                    at = (n % 4) * HALF + k * P
                    mm = pe.transpose(ps[:, at:at + P], HM[:, t, 4 * q + k, :], ident[:])
                mm.then_inc(turned, 1)


def finish(nc, T, X, out):
    with stage(nc, "g_in", "squared", "ms_ready", "rooted", "y_ready", "dve_line", "y_out") as (
            ctx, (g_in, squared, ms_ready, rooted, y_ready, dve_line, y_out)):
        g = buf(ctx, nc, "final_row", [P, D])
        junk = buf(ctx, nc, "squares", [P, D])
        ms = buf(ctx, nc, "mean_square", [P, NT])
        block = ctx.enter_context(nc.Block())

        @block.sync
        def _(sp):
            sp.dma_start(g[:], T["final_g"].partition_broadcast(P)).then_inc(g_in, 16)
            for t in range(NT):
                sp.wait_ge(y_ready, t + 1)
                sp.dma_start(out[t * P:(t + 1) * P, :], X[:, t, :]).then_inc(y_out, 16)
            sp.wait_ge(y_out, 16 * NT)

        @block.scalar
        def _(act):
            for t in range(NT):
                act.activation(junk[:], X[:, t, :], ACT.Square,
                               accum_out=ms[:, t:t + 1]).then_inc(squared, 1)
                act.wait_ge(squared, t + 1)
            act.wait_ge(ms_ready, 1)
            act.activation(ms[:], ms[:], ACT.Sqrt).then_inc(rooted, 1)

        @block.vector
        def _(dve):
            line = Line(dve, dve_line)
            dve.wait_ge(squared, NT)
            line.then(dve.tensor_scalar(ms[:], ms[:], 1.0 / D, EPS, ALU.mult, ALU.add))
            dve.reciprocal(ms[:], ms[:]).then_inc(ms_ready, 1)
            dve.wait_ge(rooted, 1)
            dve.wait_ge(g_in, 16)
            for t in range(NT):
                dve.scalar_tensor_tensor(out=X[:, t, :], in0=X[:, t, :], scalar=ms[:, t:t + 1],
                                         in1=g[:], op0=ALU.mult, op1=ALU.mult).then_inc(y_ready, 1)




def trunk(nc, T, O, upto=99, dbg=None):
    mod = nc.dram_tensor("mod_rows_dram", [2, MOD], F32, kind="Internal").ap()
    with ExitStack() as ctx:
        ps = ctx.enter_context(nc.psum_tensor("banks", [P, 8 * HALF], F32))
        X = buf(ctx, nc, "X", [P, NT, D])
        ident = buf(ctx, nc, "ident", [P, P])
        cond_s = buf(ctx, nc, "cond_s", [P, KD, 2])

        def peer(layer):
            with ExitStack() as c1:
                H = buf(c1, nc, "H", [P, NT, D])
                HT = buf(c1, nc, "HT", [P, KD, TOK])
                norm_modulate(nc, ps, X, H, HT, ident, mod, T["norm_g"][layer, 1], layer, 3, 4)
                experts(nc, T, ps, HT, H, X, mod, ident, layer, 5)
        with ExitStack() as c1:
            MIXT = buf(c1, nc, "MIXT", [P, KD, TOK])
            US = buf(c1, nc, "US", [P, 4, TOK])
            with ExitStack() as c0:
                KC = buf(c0, nc, "KC", [P, NT, 2, HYW])
                KS = buf(c0, nc, "KS", [P, NT, 2, HYW])
                start(nc, T, ps, X, ident, cond_s, mod, KC, KS)
                VG = buf(c0, nc, "VG", [P, NT, 3 * HYW])
                with ExitStack() as c2:
                    HT = buf(c2, nc, "HT", [P, KD, TOK])
                    with ExitStack() as c3:
                        H = buf(c3, nc, "H", [P, NT, D])
                        norm_modulate(nc, ps, X, H, HT, ident, mod, T["norm_g"][0, 0], 0, 0, 1)
                    project_channels(nc, ps, HT, T["ev_w_in"][12:16], US, 4)
                    PH = buf(c2, nc, "PH", [P, 12, TOK])
                    project_channels(nc, ps, HT, T["ev_w_in"][0:12], PH, 12)
                    hyena_inputs(nc, T, ps, PH, VG, ident)
                if dbg: dbg(nc, "KC", KC); dbg(nc, "KS", KS); dbg(nc, "VG", VG)
                hyena_convolve(nc, T, ps, VG, KC, KS, MIXT, ident)
                if dbg: dbg(nc, "MIXT", MIXT[:, 0:4, :])
            G = buf(c1, nc, "G", [P, 4, TOK])
            s5(nc, T, ps, US, G, ident, O["s5_re"], O["s5_im"], cond_s, mod)
            s5_gate(nc, T, ps, G, MIXT)
            if dbg: dbg(nc, "MIXS", MIXT[:, 4:8, :])
            project_out(nc, ps, MIXT, T["ev_w_out"], X, mod, 0, 2)
        if upto == 2:
            return
        if upto == 4:
            dbg(nc, "Xb", X)
        if upto != 3:
            peer(0)
        if upto == 4:
            dbg(nc, "X", X)
            return
        with ExitStack() as c1:
            negM = buf(c1, nc, "negM", [MLH, 2, TOK])
            COLS = buf(c1, nc, "COLS", [P, KINDS * 2 * NT, MLH])
            KEEP = buf(c1, nc, "KEEP", [P, 2 * NT, MLH])
            with ExitStack() as c2:
                HT = c2.enter_context(nc.sbuf_tensor(numbered("HT"), [P, KD, TOK], F32,
                                                     side="right"))
                with ExitStack() as c3:
                    H = buf(c3, nc, "H", [P, NT, D])
                    norm_modulate(nc, ps, X, H, HT, ident, mod, T["norm_g"][1, 0], 1, 0, 1)
                QK = buf(c1, nc, "QK", [P, 2 * MLH, TOK])
                VX = buf(c1, nc, "VX", [P, NT, MLH, VN])
                O_ = buf(c1, nc, "Ogate", [P, NT, D])
                mlstm_inputs(nc, T, ps, HT, ident, QK, VX, O_, negM, COLS, KEEP, O["ml_m"])
            with ExitStack() as c2:
                HM = buf(c2, nc, "HM", [P, NT, MLH, P])
                with ExitStack() as c3:
                    KT = buf(c3, nc, "KT", [P, NT, MLH, P])
                    turn_keys(nc, ps, QK, KT, ident)
                    mlstm_cells(nc, T, ps, QK, KT, VX, HM, negM, COLS, KEEP, ident, O["ml_C"],
                                O["ml_n"])
                MIXT = buf(c2, nc, "MIXT", [P, KD, TOK])
                if dbg: dbg(nc, "HM", HM)
                mlstm_finish(nc, T, ps, HM, O_, MIXT, ident)
                if dbg: dbg(nc, "Xb", X)
                project_out(nc, ps, MIXT, T["od_w_out"], X, mod, 1, 2)
                if dbg: dbg(nc, "Xa", X)
        if upto == 3:
            return
        peer(1)
        finish(nc, T, X, O["y"])


OUTS = {"y": [TOK, D], "s5_re": [2, 32, 64], "s5_im": [2, 32, 64], "ml_C": [2, 8, P, P],
        "ml_n": [2, 8, P], "ml_m": [2, 8]}


def host_arrays(inp):
    f = np.float32

    def slices(w, width):
        n = w.shape[1] // width
        return np.ascontiguousarray(w.reshape(KD, P, n, width).transpose(2, 1, 0, 3)).reshape(n, P, KD * width)

    a = {}
    a["cond"] = np.stack([inp["c_ctx"], inp["c"][0]], -1).reshape(KD, P, 2).transpose(1, 0, 2)
    ada = np.concatenate(list(inp["ada_w"]), 1)
    a["ada_first"], a["ada_rest"] = slices(ada[:, :MOD_FIRST], HALF), slices(ada[:, MOD_FIRST:], MOD_W)
    a["ada_b"] = inp["ada_b"].reshape(1, -1)
    a["x"] = np.concatenate([inp["x_prompt"][0], inp["x_sample"][0]]).reshape(NT, P, D).transpose(1, 0, 2)
    a["norm_g"] = inp["norm_g"]
    a["ev_w_in"] = slices(inp["ev_w_in"][0], P)
    quarter = D // 4
    omega = (1.0 / (f(10000.0) ** (np.arange(quarter, dtype=f) / f(quarter)))).astype(f)

    def emb(n):
        ang = np.arange(n, dtype=f)[:, None] * omega[None]
        return np.concatenate([np.sin(ang), np.cos(ang)], -1)
    er, ec = emb(LAT // 64), emb(64)
    pe = np.concatenate([np.repeat(er, 64, 0), np.tile(ec, (LAT // 64, 1))], -1)
    a["pos"] = pe.reshape(NT - 1, P, D).transpose(1, 0, 2)
    feats, times = [], np.ones((2, NT, P), f)
    for g, n in ((0, CTX), (1, LAT)):
        t = np.arange(n, dtype=f) / f(n)
        bands = np.linspace(1e-4, 15, 16, dtype=f)
        ang = f(2.0 * math.pi) * t[:, None] * bands[None]
        feats.append(np.concatenate([t[:, None], np.cos(ang), np.sin(ang)], -1))
        times[0, g:g + 1 + 3 * g] = -t.reshape(-1, P)
        times[1, g, 0] = 0.0
        w = (2 * np.arange(n)[None] + 1) * np.arange(n)[:, None] % (4 * n) * (math.pi / (2 * n))
        for name, m in (("cos", np.cos(w)), ("sin", np.sin(w))):
            for way, mat in (("fwd", m), ("inv", m.T / n)):
                part = mat.reshape(n // P, P, n).transpose(1, 0, 2).reshape(P, -1).astype(f)
                a[f"{name}_{way}"] = np.concatenate([a[f"{name}_{way}"], part], 1) if g else part
    a["hy_z"] = np.concatenate(feats).T
    a["hy_times"] = times.transpose(2, 0, 1)
    a["hy_w1"], a["hy_w2"], a["hy_w3"] = inp["hy_w1"][0], inp["hy_w2"][0], inp["hy_w3"][0]
    a["hy_cols"] = np.stack([inp["hy_b1"][0], inp["hy_b2"][0], inp["hy_freq"][0]], -1)
    a["hy_decay"], a["hy_bias"] = inp["hy_decay"][0], inp["hy_bias"][0]

    def taps(w, b):
        return np.concatenate([w, b[None]]).reshape(4, -1, P).transpose(2, 1, 0)
    a["hy_taps"] = taps(inp["hy_conv_w"][0], inp["hy_conv_b"][0])
    def states(v):
        v = v.reshape(2, PAIRS, 2, 64, *v.shape[3:])
        return np.moveaxis(v, (2, 3), (0, 1)).reshape(P, 2 * PAIRS, *v.shape[4:])
    step = np.broadcast_to(inp["s5_log_step"][0][:, :, None], (2, 32, 64))
    a["s5_par"] = np.stack([states(v) for v in (
        inp["s5_a_re"][0], inp["s5_a_im"][0], step, inp["state_s5_re"][0, 0],
        inp["state_s5_im"][0, 0])], 1)
    a["s5_B"] = np.stack([states(inp["s5_b_re"][0]), states(inp["s5_b_im"][0])], 1)
    a["s5_C"] = np.stack([states(inp[n][0].transpose(0, 1, 3, 2)) for n in ("s5_c_re", "s5_c_im")], 1)
    a["s5_d"] = inp["s5_d"][0].reshape(4, P).T
    ctx_steps, lat_steps = np.arange(1, CTX + 1, dtype=f), np.arange(1, LAT + 1, dtype=f)
    a["s5_steps"] = np.stack([np.concatenate([ctx_steps, lat_steps]),
                              np.concatenate([lat_steps, ctx_steps])])
    a["glu_w"] = inp["s5_glu_w"][0].reshape(4, P, 512).transpose(1, 0, 2)
    a["glu_b"] = inp["s5_glu_b"][0].reshape(4, P).T
    a["ev_w_out"] = inp["ev_w_out"][0].reshape(KD, P, D).transpose(1, 0, 2)
    w = inp["od_w_in"][0]
    a["od_w_qk"], a["od_w_vo"] = slices(w[:, 0:2 * D], P), slices(w[:, 2 * D:4 * D], 2 * P)
    a["gate_w"] = np.zeros((P, KD, 4, 32), f)
    a["gate_w"][:, :, :, 0:MLH] = w[:, 4 * D:].reshape(KD, P, 4, MLH).transpose(1, 0, 2, 3)
    a["gate_w"] = a["gate_w"].reshape(P, KD, P)
    a["gate_b"], a["ml_m0"] = inp["od_gate_b"][0].T, inp["state_mlstm_m"][0, 0].T
    a["ml_taps"] = taps(inp["ml_conv_w"][0], inp["ml_conv_b"][0])
    a["ml_CN0"] = np.concatenate([inp["state_mlstm_C"][0, 0], inp["state_mlstm_n"][0, 0][..., None]],
                                 -1).transpose(2, 0, 1, 3)
    a["ml_norm_g"], a["final_g"] = inp["ml_norm_g"][0], inp["final_g"]
    a["od_w_out"] = inp["od_w_out"][0].reshape(KD, P, D).transpose(1, 0, 2)
    for l in range(2):
        a[f"pk_w_q{l}"] = slices(inp["pk_w_q"][l], P)
        a[f"pk_u{l}"], a[f"pk_v{l}"] = inp["pk_u"][l], inp["pk_v"][l]
    a["pk_keys"] = inp["pk_keys"].transpose(0, 4, 1, 2, 3).reshape(2, P, CODES, P)
    return {k: np.ascontiguousarray(v, dtype=v.dtype) for k, v in a.items()}


def kernel(**inputs):
    import concourse.bacc as bacc
    from concourse.bass_utils import run_bass_kernel_spmd as run

    USED.clear()
    arrays = {f"in_{n}_dram": a for n, a in host_arrays(inputs).items()}
    nc = bacc.Bacc("TRN2", target_bir_lowering=False, num_devices=1)
    T = {n[3:-5]: nc.dram_tensor(n, a.shape, mybir.dt.from_np(a.dtype), kind="ExternalInput").ap()
         for n, a in arrays.items()}
    O = {n: nc.dram_tensor(f"out_{n}_dram", shape, F32, kind="ExternalOutput").ap()
         for n, shape in OUTS.items()}
    trunk(nc, T, O)
    r = run(nc, [arrays], core_ids=[0]).results[0]
    y, re, im, C, n, m = (r[f"out_{k}_dram"] for k in OUTS)
    return (y[None, :CTX], y[None, CTX:], re[None, None], im[None, None], C[None, None],
            n[None, None], m[None, None])
```

```python
import math
from contextlib import ExitStack, contextmanager

import numpy as np

import concourse.bass as bass
from concourse import mybir

F32 = mybir.dt.float32
U32 = mybir.dt.uint32
I32 = mybir.dt.int32
ALU = mybir.AluOpType
ACT = mybir.ActivationFunctionType
AX = mybir.AxisListType

P = 128
D = 1024
KD = D // P
CTX = 128
LAT = 512
TOK = CTX + LAT
NT = TOK // P
GROUPS = ((0, CTX), (CTX, TOK))
EPS = 1e-6
HALF = 512
TWO_PI = 2.0 * math.pi
PI_BELOW = 3.1415925
ROUND = 1.5 * 2.0 ** 23


def group_of(tile):
    return 0 if tile == 0 else 1


def wait_apart(eng, sem, count, mark):
    eng.wait_ge(sem, count)
    eng.sem_inc(mark, 1)


class Line:

    def __init__(self, eng, sem):
        self.eng, self.sem, self.n, self.at = eng, sem, 0, 0

    def then(self, ins, mark=None):
        self.count(ins)
        self.settle(mark)

    def count(self, ins):
        self.n += 1
        ins.then_inc(self.sem, 1)
        return self.n

    def settle(self, mark=None, upto=None):
        if mark is None:
            self.eng.wait_ge(self.sem, self.at + (upto or self.n))
        else:
            wait_apart(self.eng, self.sem, self.at + self.n, mark)

    @contextmanager
    def loop(self, start, stop, per):
        before, was = self.n, self.at
        assert isinstance(was, int)
        with self.eng.Fori(start, stop) as i:
            self.at, self.n = was + before + (i - start) * per, 0
            yield i
            assert self.n == per, (self.n, per)
        self.at, self.n = was + before + (stop - start) * per, 0


USED = {}


def numbered(name):
    USED[name] = USED.get(name, -1) + 1
    return f"{name}_{USED[name]}"


@contextmanager
def stage(nc, *names):
    sems = [nc.alloc_semaphore(numbered(n)) for n in names]
    with ExitStack() as ctx:
        yield ctx, sems
    nc.clear_and_free_semaphores(sems)
    nc.all_engine_barrier()


@contextmanager
def carried(nc, name):
    sem = nc.alloc_semaphore(numbered(name))
    yield sem
    nc.clear_and_free_semaphores([sem])
    nc.all_engine_barrier()


def buf(ctx, nc, name, shape, dt=F32):
    return ctx.enter_context(nc.sbuf_tensor(numbered(name), shape, dt))


MOD = 2 * 6 * D
MOD_FIRST = 2 * D
MOD_W = 320
MOD_BLOCKS = (MOD - MOD_FIRST) // MOD_W


def mod_row(mod, layer, g, chunk):
    at = (6 * layer + chunk) * D
    return mod[g, at:at + D].partition_broadcast(P)


def norm_modulate(nc, ps, X, H, HT, ident, mod, gain, layer, shift, scale):
    with stage(nc, "rows_in", "squared", "rooted", "dve_line", "h_ready", "turned",
               "copied") as (ctx, (rows_in, squared, rooted, dve_line, h_ready, turned, copied)):
        g_row = buf(ctx, nc, "g_row", [P, D])
        sc = buf(ctx, nc, "sc_row", [P, 2, D])
        sh = buf(ctx, nc, "sh_row", [P, 2, D])
        junk = buf(ctx, nc, "squares", [P, D])
        ss = buf(ctx, nc, "mean_square", [P, NT])
        rs = buf(ctx, nc, "root", [P, NT])
        block = ctx.enter_context(nc.Block())

        @block.sync
        def _(sp):
            sp.dma_start(g_row[:], gain.partition_broadcast(P)).then_inc(rows_in, 16)
            for g in range(2):
                for dst, c in ((sc, scale), (sh, shift)):
                    sp.dma_start(dst[:, g, :], mod_row(mod, layer, g, c)).then_inc(rows_in, 16)

        @block.scalar
        def _(act):
            for t in range(NT):
                act.activation(junk[:], X[:, t, :], ACT.Square,
                               accum_out=ss[:, t:t + 1]).then_inc(squared, 1)
                act.wait_ge(squared, t + 1)
            act.wait_ge(dve_line, 2)
            act.activation(rs[:], ss[:], ACT.Sqrt).then_inc(rooted, 1)
            for n in range(2 * NT):
                act.wait_ge(turned, n + 1)
                t, q = n // 2, n % 2
                act.activation(HT[:, 4 * q:4 * q + 4, t * P:(t + 1) * P],
                               ps[:, (n % 4) * HALF:(n % 4 + 1) * HALF].rearrange("p (k c) -> p k c", k=4),
                               ACT.Copy).then_inc(copied, 1)

        @block.vector
        def _(dve):
            line = Line(dve, dve_line)
            dve.wait_ge(squared, NT)
            line.then(dve.tensor_scalar(ss[:], ss[:], 1.0 / D, EPS, ALU.mult, ALU.add))
            line.then(dve.reciprocal(ss[:], ss[:]))
            dve.wait_ge(rows_in, 80)
            for g in range(2):
                line.then(dve.scalar_tensor_tensor(out=sc[:, g, :], in0=sc[:, g, :], scalar=1.0,
                                                   in1=g_row[:], op0=ALU.add, op1=ALU.mult))
            dve.wait_ge(rooted, 1)
            for t in range(NT):
                g = group_of(t)
                line.then(dve.scalar_tensor_tensor(out=H[:, t, :], in0=X[:, t, :],
                                                   scalar=rs[:, t:t + 1], in1=sc[:, g, :],
                                                   op0=ALU.mult, op1=ALU.mult))
                dve.tensor_tensor(H[:, t, :], H[:, t, :], sh[:, g, :], ALU.add).then_inc(h_ready, 1)
                dve.wait_ge(h_ready, t + 1)

        @block.tensor
        def _(pe):
            for n in range(2 * NT):
                t, q = n // 2, n % 2
                if q == 0:
                    pe.wait_ge(h_ready, t + 1)
                if n >= 4:
                    pe.wait_ge(copied, n - 3)
                for k in range(4):
                    mm = pe.transpose(ps[:, (n % 4) * HALF + k * P:(n % 4) * HALF + (k + 1) * P],
                                      H[:, t, (4 * q + k) * P:(4 * q + k + 1) * P], ident[:])
                mm.then_inc(turned, 1)


HEADS = 8
TOPK = 16
SLOTS = HEADS * TOPK
CODES = 2 * HEADS
LOWEST = -3.0e38
RING = 16
FREED = 4
PE_OF_8 = (1, 4, 6)
DIAGS = 4
CODE_AT, CODE_GAP = 64, 4
HEAD_GAP = 8
LATE_AT, LATE_GAP = HEADS * HEAD_GAP + 1, 4
EXP_AT = LATE_AT + 12


def on_pe(slot):
    return slot % 8 in PE_OF_8


def pe_rows(slots):
    return sum(on_pe(n) for n in range(slots))


def experts(nc, T, ps, HT, H, X, mod, ident, layer):
    names = [f"row_in{b}" for b in range(RING)]
    with stage(nc, "rows_in", "squared", "ms_ready", "rooted", "h_ready", "turned", "ht_out",
               "keys_in", "w_in0", "w_in1", "w_in2", "w_in3", "used", "q_out", "q_cur",
               "scored", "code_scored",
               "s_free", "exp_in", "exp_out",
               "dve_line", "iota_done", "idx_ready", "idx_set", "h_set", "dve_used", "pe_used",
               "dots_done", "gelu_done", "weights_set", "diag_set", "v_idx_free", "g_in",
               "waited", *names) as (
            ctx, (rows_in, squared, ms_ready, rooted, h_ready, turned, ht_out, keys_in,
                  w_in0, w_in1, w_in2, w_in3, used, q_out, q_cur, scored, code_scored,
                  s_free, exp_in, exp_out, dve_line,
                  iota_done, idx_ready, idx_set, h_set, dve_used, pe_used, dots_done, gelu_done,
                  weights_set, diag_set, v_idx_free, g_in, mark, *row_in)):
        keys = buf(ctx, nc, "keys", [P, CODES, P])
        q = buf(ctx, nc, "q_tile", [P, CODES, P])
        QT = buf(ctx, nc, "QT", [P, CODES, LAT])
        s = ps[:, 0:4 * HALF].rearrange("p (c n) -> p c n", c=CODES)
        s2 = buf(ctx, nc, "scores_rest", [P, CODES, P])
        top = buf(ctx, nc, "top_value", [P, CODES, TOPK])
        where = buf(ctx, nc, "top_index", [P, CODES, TOPK], U32)
        where_f = top
        best = buf(ctx, nc, "best_value", [P, HEADS, TOPK])
        at = buf(ctx, nc, "best_at", [P, HEADS, TOPK], U32)
        at_part = buf(ctx, nc, "best_part", [P, 2, SLOTS], U32)
        at_f = buf(ctx, nc, "best_part_f", [P, 2, SLOTS])
        key_f = buf(ctx, nc, "key_f", [P, 2, SLOTS])
        iota = buf(ctx, nc, "iota16", [P, TOPK])
        e = buf(ctx, nc, "exp_score", [P, HEADS, TOPK])
        e_sum = buf(ctx, nc, "exp_sum", [P, HEADS])
        idx = buf(ctx, nc, "expert", [P, SLOTS], U32)
        gate = buf(ctx, nc, "expert_gate", [P, SLOTS])
        rows = buf(ctx, nc, "expert_rows", [P, RING, D])
        idx_u = buf(ctx, nc, "idx_u", [P, SLOTS], U32)
        idx_v = buf(ctx, nc, "idx_v", [P, SLOTS], U32)
        h = buf(ctx, nc, "h_tile", [P, D])
        acc = buf(ctx, nc, "acc", [P, 2, D])
        dots = buf(ctx, nc, "dots", [P, SLOTS])
        act_w = buf(ctx, nc, "expert_weight", [P, SLOTS])
        diag = buf(ctx, nc, "weight_diag", [P, DIAGS, P])
        ms = buf(ctx, nc, "mean_square", [P, NT])
        root = buf(ctx, nc, "root", [P, NT])
        gain, scale, shift, junk = rows[:, 0, :], rows[:, 1:3, :], rows[:, 3:5, :], rows[:, 5, :]
        FIRST, OTHERS = slice(0, 1), slice(1, NT)
        block = ctx.enter_context(nc.Block())
        g_row = keys[:, :, :].rearrange("p (g c) n -> p g (c n)", g=2)
        q_flat = q[:, :, :].rearrange("p (b c) n -> p b (c n)", b=2)
        w = (acc[:, 0, :], acc[:, 1, :], q_flat[:, 0, :], q_flat[:, 1, :])
        w_in = (w_in0, w_in1, w_in2, w_in3)
        cand = s.rearrange("p (h a) n -> p h (a n)", a=2)
        cand2 = s2[:, :, :].rearrange("p (h a) n -> p h (a n)", a=2)
        pick = cand.rearrange("p h (k j) -> p h k j", j=TOPK)
        pair = top[:, :, :].rearrange("p (h a) k -> p h a k", a=2)
        half = where_f[:, :, :].rearrange("p (h a) k -> p h a k", a=2)
        table_u, table_v = T[f"pk_u{layer}"], T[f"pk_v{layer}"]
        dve_tile, pe_tile = 2 * SLOTS - pe_rows(SLOTS), pe_rows(SLOTS)
        pe_ring = len(PE_OF_8) * RING // 8
        v_sum = ps[:, 4 * HALF:6 * HALF]

        def dve_rows(n):
            return n - pe_rows(max(0, n - SLOTS)) if n >= 0 else n + pe_rows(SLOTS) - pe_rows(SLOTS + n)

        @block.sync
        def _(sp):
            sp.dma_start(gain, T["norm_g"][layer, 1].partition_broadcast(P)).then_inc(rows_in, 16)
            for g in range(2):
                for dst, c in ((scale, 4), (shift, 3)):
                    sp.dma_start(dst[:, g, :], mod_row(mod, layer, g, c)).then_inc(rows_in, 16)
            W = T[f"pk_w_q{layer}"]
            for c in range(2):
                sp.dma_start(w[c], W[c]).then_inc(w_in[c], 16)
            sp.dma_start(keys[:], T["pk_keys"][layer]).then_inc(keys_in, 16)
            with sp.Fori(1, CODES // 2) as i:
                for c in range(2):
                    sp.wait_ge(used, 2 * i + (c - 1))
                    sp.dma_start(w[c], W[2 * i + c]).then_inc(w_in[c], 16)
            for c in range(4):
                if c < 2:
                    sp.wait_ge(used, CODES + c - 1)
                else:
                    sp.wait_ge(scored, 1)
                sp.dma_start(w[c], W[c]).then_inc(w_in[c], 16)
            with sp.Fori(1, CODES // 4) as i:
                for c in range(4):
                    sp.wait_ge(used, 4 * i + (CODES + c - 3))
                    sp.dma_start(w[c], W[4 * i + c]).then_inc(w_in[c], 16)
            sp.wait_ge(scored, NT)
            for g in range(2):
                sp.dma_start(g_row[:, g, :], mod_row(mod, layer, g, 5)).then_inc(g_in, 16)

        @block.gpsimd
        def _(pool):
            pool.iota(iota[:], pattern=[[1, TOPK]], base=0, channel_multiplier=0,
                      allow_small_or_imprecise_dtypes=True).then_inc(iota_done, 1)
            with pool.Fori(0, NT) as t:
                wait_apart(pool, idx_ready, t + 1, mark)
                for table, index, first in ((table_u, idx_u, 0), (table_v, idx_v, SLOTS)):
                    if first == 0:
                        wait_apart(pool, dots_done, t + 1, mark)
                        wait_apart(pool, v_idx_free, t + 1, mark)
                        pool.tensor_copy(idx_u[:], idx[:])
                        pool.tensor_copy(idx_v[:], idx[:]).then_inc(idx_set, 1)
                        pool.wait_ge(idx_set, t + 1)
                    for n in range(SLOTS):
                        b = n % RING
                        if n % FREED == 0:
                            before = first + n + FREED - RING
                            wait_apart(pool, dve_used, t * dve_tile
                                       + (RING - pe_ring + dve_rows(before)), mark)
                            if before < 0 or first:
                                wait_apart(pool, pe_used, t * pe_tile
                                           + (pe_ring + before - dve_rows(before)), mark)
                        pool.indirect_dma_start(
                            out=rows[:, b, :], out_offset=None, in_=table,
                            in_offset=bass.IndirectOffsetOnAxis(ap=index[:, n:n + 1], axis=0),
                        ).then_inc(row_in[b], 16)

        @block.scalar
        def _(act):
            def queries(i, c, context):
                n, at = 4 * i + c, (4 + c % 2) * HALF
                act.wait_ge(used, 4 * i + ((0 if context else CODES) + c + 1))
                out, width = (q[:, bass.ds(n, 1), :], CTX) if context else (QT[:, bass.ds(n, 1), :], LAT)
                act.activation(out, ps[:, at:at + width].unsqueeze(1), ACT.Copy
                               ).then_inc(q_out, 1)

            def token_rows(t):
                act.activation(h[:, :].unsqueeze(1), H[:, bass.ds(t, 1), :],
                               ACT.Copy).then_inc(h_set, 1)

            def exponentials(t):
                act.wait_ge(exp_in, t + 1)
                act.activation(e[:], e[:], ACT.Exp).then_inc(exp_out, 1)

            def tile(t, more):
                if more:
                    act.wait_ge(scored, t + 1)
                    act.activation(q[:], QT[:, :, bass.ds(t * P, P)], ACT.Copy).then_inc(q_cur, 1)
                act.wait_ge(dots_done, t + 2)
                act.activation(act_w[:], dots[:], ACT.Gelu_apprx_tanh).then_inc(gelu_done, 1)
                if more:
                    token_rows(t + 1)
                act.wait_ge(weights_set, t + 1)
                for n in range(SLOTS):
                    if more and n == EXP_AT:
                        exponentials(t + 1)
                    if on_pe(n):
                        j = pe_rows(n)
                        act.wait_ge(pe_used, t * pe_tile + (pe_ring + j + 1 - DIAGS))
                        act.activation(diag[:, j % DIAGS, :], ident[:], ACT.Copy,
                                       scale=act_w[:, n:n + 1]).then_inc(diag_set, 1)

            def squares(tiles):
                for t in range(NT)[tiles]:
                    act.activation(junk, X[:, t, :], ACT.Square,
                                   accum_out=ms[:, t:t + 1]).then_inc(squared, 1)
                    act.wait_ge(squared, t + 1)

            def square_roots(tiles, n):
                act.wait_ge(ms_ready, n)
                act.activation(root[:, tiles], ms[:, tiles], ACT.Sqrt).then_inc(rooted, 1)

            def turned_out(n):
                t, half_ = n // 2, n % 2
                act.wait_ge(turned, n + 1)
                at = (6 + n % 2) * HALF
                act.activation(HT[:, 4 * half_:4 * half_ + 4, t * P:(t + 1) * P],
                               ps[:, at:at + HALF].rearrange("p (k c) -> p k c", k=4),
                               ACT.Copy).then_inc(ht_out, 1)

            squares(FIRST)
            square_roots(FIRST, 1)
            squares(OTHERS)
            for n in range(2):
                turned_out(n)
            square_roots(OTHERS, 2)
            act.wait_ge(h_ready, 1)
            token_rows(0)
            for n in range(CODES):
                queries(n // 4, n % 4, True)
                if n % 2:
                    turned_out(2 + n // 2)
            for c in range(4):
                queries(0, c, False)
            exponentials(0)
            with act.Fori(1, CODES // 4) as i:
                for c in range(4):
                    queries(i, c, False)
            act.wait_ge(q_out, 2 * CODES)
            with act.Fori(0, NT - 1) as t:
                tile(t, True)
            tile(NT - 1, False)

        @block.tensor
        def _(pe):
            def queries(i, c, context):
                if context:
                    n = 4 * i + c
                    wb, loaded = n % 2, 16 * (n // 2 + 1)
                    if n >= 2:
                        pe.wait_ge(q_out, n - 1)
                else:
                    wb, loaded = c, 16 * i + (8 * CODES + 16 if c < 2 else 16)
                    pe.wait_ge(q_out, 4 * i + (CODES + c - 1))
                pe.wait_ge(w_in[wb], loaded)
                at = (4 + c % 2) * HALF
                a, z = (0, CTX) if context else (CTX, TOK)
                for k in range(KD):
                    mm = pe.matmul(ps[:, at:at + z - a], w[wb][:, k * P:(k + 1) * P],
                                   HT[:, k, a:z], start=(k == 0), stop=(k == KD - 1))
                mm.then_inc(used, 1)

            def scores(t):
                pe.wait_ge(s_free, t + 1)
                for c in range(CODES):
                    mm = pe.matmul(ps[:, c * P:(c + 1) * P], q[:, c, :],
                                   keys[:, c, :], start=True, stop=True)
                mm.then_inc(scored, 1)

            def weighted_rows(t):
                for n in range(SLOTS):
                    if on_pe(n):
                        j, b = pe_rows(n), n % RING
                        pe.wait_ge(row_in[b], t * (16 * 2 * SLOTS // RING)
                                   + 16 * ((SLOTS + n) // RING + 1))
                        pe.wait_ge(diag_set, t * pe_tile + (j + 1))
                        for k in range(2):
                            mm = pe.matmul(v_sum[:, k * HALF:(k + 1) * HALF], diag[:, j % DIAGS, :],
                                           rows[:, b, k * HALF:(k + 1) * HALF],
                                           start=(j == 0), stop=(j == pe_tile - 1))
                        mm.then_inc(pe_used, 1)

            pe.sem_inc(pe_used, pe_ring)
            pe.wait_ge(keys_in, 16)
            def score(c):
                return pe.matmul(ps[:, c * P:(c + 1) * P], q[:, c, :], keys[:, c, :],
                                 start=True, stop=True)

            def turn(n):
                t, half_ = n // 2, n % 2
                pe.wait_ge(h_ready, t + 1)
                if n >= 2:
                    pe.wait_ge(ht_out, n - 1)
                for k in range(4):
                    at = (6 + n % 2) * HALF + k * P
                    mm = pe.transpose(ps[:, at:at + P],
                                      H[:, t, (4 * half_ + k) * P:(4 * half_ + k + 1) * P], ident[:])
                mm.then_inc(turned, 1)

            for n in range(2):
                turn(n)
            pe.wait_ge(ht_out, 2)
            for n in range(CODES):
                queries(n // 4, n % 4, True)
                if n % 2:
                    turn(2 + n // 2)
                if n:
                    pe.wait_ge(q_out, n)
                    score(n - 1).then_inc(code_scored, 1)
            pe.wait_ge(q_out, CODES)
            score(CODES - 1).then_inc(scored, 1)
            pe.wait_ge(ht_out, 2 * NT)
            with pe.Fori(0, CODES // 4) as i:
                for c in range(4):
                    queries(i, c, False)
            pe.wait_ge(q_out, 2 * CODES)
            with pe.Fori(0, NT - 1) as t:
                pe.wait_ge(q_cur, t + 1)
                scores(t + 1)
                weighted_rows(t)
            weighted_rows(NT - 1)

        @block.vector
        def _(dve):
            line = Line(dve, dve_line)
            dve.sem_inc(s_free, 1)
            dve.sem_inc(dve_used, RING - pe_ring)
            dve.sem_inc(dots_done, 1)
            dve.sem_inc(v_idx_free, 1)
            dve.wait_ge(rows_in, 80)
            for g in range(2):
                line.count(dve.scalar_tensor_tensor(out=scale[:, g, :], in0=scale[:, g, :],
                                                    scalar=1.0, in1=gain, op0=ALU.add,
                                                    op1=ALU.mult))
            line.settle()
            for n, tiles in enumerate((FIRST, OTHERS)):
                dve.wait_ge(squared, (1, NT)[n])
                line.then(dve.tensor_scalar(ms[:, tiles], ms[:, tiles], 1.0 / D, EPS, ALU.mult,
                                            ALU.add))
                dve.reciprocal(ms[:, tiles], ms[:, tiles]).then_inc(ms_ready, 1)
                dve.wait_ge(rooted, n + 1)
                for t in range(NT)[tiles]:
                    g = group_of(t)
                    line.then(dve.scalar_tensor_tensor(out=H[:, t, :], in0=X[:, t, :],
                                                       scalar=root[:, t:t + 1],
                                                       in1=scale[:, g, :], op0=ALU.mult,
                                                       op1=ALU.mult))
                    dve.tensor_tensor(H[:, t, :], H[:, t, :], shift[:, g, :], ALU.add
                                      ).then_inc(h_ready, 1)
            dve.wait_ge(h_ready, NT)
            dve.wait_ge(iota_done, 1)

            def search(step, src, rest, values, places, r):
                if step == 0:
                    return dve.max(values[:, r, 0:8], src[:, r, :])
                if step == 1:
                    dve.max_index(places[:, r, 0:8], values[:, r, 0:8], src[:, r, :])
                    return dve.match_replace(rest[:, r, :], values[:, r, 0:8], src[:, r, :], LOWEST)
                if step == 2:
                    return dve.max(values[:, r, 8:16], rest[:, r, :])
                return dve.max_index(places[:, r, 8:16], values[:, r, 8:16], rest[:, r, :])

            by_code = (s, s2, top, where)
            by_head = (cand, cand2, best, at)

            def sums(h0, h1):
                n = h1 - h0
                return dve.tensor_tensor(
                    pick[:, h0:h1],
                    pair[:, h0:h1, 0, :].unsqueeze(3).to_broadcast([P, n, TOPK, TOPK]),
                    pair[:, h0:h1, 1, :].unsqueeze(2).to_broadcast([P, n, TOPK, TOPK]), ALU.add)

            def late(step, t):
                flat = at[:, :, :].rearrange("p h k -> p (h k)")
                if step == 0:
                    ins = dve.tensor_tensor(e[:], best[:], best[:, :, 0:1].to_broadcast(
                        [P, HEADS, TOPK]), ALU.subtract)
                elif step == 1:
                    dve.sem_inc(exp_in, 1)
                    dve.tensor_scalar(at_part[:, 0, :], flat, 4, None, ALU.logical_shift_right)
                    ins = dve.tensor_scalar(at_part[:, 1, :], flat, TOPK - 1, None,
                                            ALU.bitwise_and)
                elif step == 2:
                    dve.tensor_copy(where_f[:], where[:])
                    ins = dve.tensor_copy(at_f[:], at_part[:])
                elif step < 9:
                    a, part = (step - 3) // 3, (step - 3) % 3
                    if part == 0:
                        ins = dve.tensor_tensor(
                            pick.rearrange("p h k j -> p (h k) j"),
                            iota[:, :].unsqueeze(1).to_broadcast([P, SLOTS, TOPK]),
                            at_f[:, a, :].unsqueeze(2).to_broadcast([P, SLOTS, TOPK]), ALU.is_equal)
                    elif part == 1:
                        ins = dve.tensor_tensor(
                            pick, pick, half[:, :, a, :].unsqueeze(2)
                            .to_broadcast([P, HEADS, TOPK, TOPK]), ALU.mult)
                    else:
                        ins = dve.tensor_reduce(key_f[:, a, :], pick.rearrange(
                            "p h k j -> p (h k) j"), AX.X, ALU.add)
                elif step == 9:
                    dve.sem_inc(s_free, 1)
                    if not isinstance(t, int):
                        dve.wait_ge(idx_set, t)
                    ins = dve.scalar_tensor_tensor(
                        out=idx[:], in0=key_f[:, 0, :], scalar=float(P),
                        in1=key_f[:, 1, :], op0=ALU.mult, op1=ALU.add)
                elif step == 10:
                    dve.sem_inc(idx_ready, 1)
                    dve.wait_ge(exp_out, t + 1)
                    ins = dve.tensor_reduce(e_sum[:], e[:], AX.X, ALU.add)
                elif step == 11:
                    ins = dve.reciprocal(e_sum[:], e_sum[:])
                else:
                    ins = dve.tensor_tensor(
                        gate[:, :].rearrange("p (h k) -> p h k", h=HEADS), e[:],
                        e_sum[:, :].unsqueeze(2).to_broadcast([P, HEADS, TOPK]), ALU.mult)
                return ins

            def scale_and_add(t, step):
                if step == 0:
                    line.then(dve.tensor_tensor(H[:, t, :], H[:, t, :], g_row[:, group_of(t), :],
                                                ALU.mult))
                else:
                    line.then(dve.tensor_tensor(X[:, t, :], X[:, t, :], H[:, t, :], ALU.add))

            def tile(t, more):
                dve.wait_ge(h_set, t + 1)
                for n in range(SLOTS):
                    b = n % RING
                    dve.wait_ge(row_in[b], t * (16 * 2 * SLOTS // RING) + 16 * (n // RING + 1))
                    dve.tensor_tensor_reduce(rows[:, b, :], rows[:, b, :], h[:], 1.0, 0.0,
                                             ALU.mult, ALU.add, dots[:, n:n + 1]
                                             ).then_inc(dve_used, 1)
                    code, k = divmod(n - CODE_AT, CODE_GAP)
                    if more and 0 <= code < CODES and k < 4:
                        if n == CODE_AT:
                            wait_apart(dve, scored, t + 2, mark)
                        else:
                            line.settle(mark)
                        line.count(search(k, *by_code, code))
                    if not more and n % 8 == 7 and n // 8 < 2 * (NT - 1):
                        if n == 7:
                            dve.wait_ge(g_in, 32)
                        scale_and_add(n // 16, n // 8 % 2)
                credit = RING - pe_ring
                dve.wait_ge(dve_used, t * dve_tile + (credit + SLOTS))
                dve.sem_inc(dots_done, 1)
                dve.wait_ge(gelu_done, t + 1)
                line.then(dve.tensor_tensor(act_w[:], act_w[:], gate[:], ALU.mult))
                dve.sem_inc(weights_set, 1)
                mine = 0
                for n in range(SLOTS):
                    b = n % RING
                    if not on_pe(n):
                        dve.wait_ge(row_in[b], t * (16 * 2 * SLOTS // RING)
                                    + 16 * ((SLOTS + n) // RING + 1))
                        a, w = acc[:, mine % 2, :], act_w[:, n:n + 1]
                        if mine < 2:
                            ins = dve.tensor_scalar(a, rows[:, b, :], w, None, ALU.mult)
                        else:
                            dve.wait_ge(dve_used, t * dve_tile + (credit + SLOTS + mine - 1))
                            ins = dve.scalar_tensor_tensor(out=a, in0=rows[:, b, :], scalar=w,
                                                           in1=a, op0=ALU.mult, op1=ALU.add)
                        ins.then_inc(dve_used, 1)
                        mine += 1
                    if not more:
                        continue
                    head, k = divmod(n, HEAD_GAP)
                    if head < HEADS and k in (0, 2, 4, 6, 7):
                        line.settle(mark)
                        if k == 0:
                            line.count(sums(head, head + 1))
                        else:
                            line.count(search((2, 4, 6, 7).index(k), *by_head, head))
                    step, k = divmod(n - LATE_AT, LATE_GAP)
                    if 0 <= step <= 12 and k == 0:
                        line.settle(mark)
                        line.count(late(step, t + 1))
                dve.wait_ge(dve_used, t * dve_tile + (credit + dve_tile))
                dve.wait_ge(pe_used, t * pe_tile + (pe_ring + pe_tile))
                dve.sem_inc(v_idx_free, 1)
                line.then(dve.tensor_tensor(acc[:, 0, :], acc[:, 0, :], acc[:, 1, :], ALU.add))
                line.then(dve.tensor_tensor(H[:, bass.ds(t, 1), :], acc[:, 0:1, :],
                                            v_sum.unsqueeze(1), ALU.add))

            for part in range(4):
                if part < 3:
                    dve.wait_ge(code_scored, 4 * part + 4)
                else:
                    dve.wait_ge(scored, 1)
                for step in range(4):
                    for r in range(4 * part, 4 * part + 4):
                        ins = search(step, *by_code, r)
                    line.then(ins)
            line.then(sums(0, HEADS))
            for step in range(4):
                for r in range(HEADS):
                    ins = search(step, *by_head, r)
                line.then(ins)
            for step in range(13):
                line.then(late(step, 0))
            with line.loop(0, NT - 1, 4 * CODES + 5 * HEADS + 13 + 3) as t:
                tile(t, True)
            tile(NT - 1, False)
            for step in range(2):
                scale_and_add(NT - 1, step)


HYW = 512
HYF = 64
EMB = 33
DFT = P + (LAT // P) * LAT


def dft_block(m, src, dst):
    if dst == 0:
        return m[:, 0:P]
    at = P + (src - 1) * LAT + (dst - 1) * P
    return m[:, at:at + P]


def sources(tile):
    return (0,) if tile == 0 else tuple(range(1, NT))


def start(nc, T, ps, X, ident, cond_s, mod, KC, KS, spare):
    blocks = MOD_FIRST // HALF
    with stage(nc, "cond_in", "small_in", "decay_in", "ada_in0", "ada_in1", "x_in", "bias_in",
               "dft_in", "ident_set", "cond_ready", "ada_used", "rows_added", "mod_out", "x_ready",
               "layer_done", "args_ready", "sines_done", "taps_raw", "env_done", "taps_done",
               "ab_ready", "sq_done", "sums_done", "rooted", "sqrt_done", "dft_done", "dft_out",
               "dve_line", "act_line") as (
            ctx, (cond_in, small_in, decay_in, ada_in0, ada_in1, x_in, bias_in, dft_in, ident_set,
                  cond_ready, ada_used, rows_added, mod_out, x_ready, layer_done, args_ready,
                  sines_done, taps_raw, env_done, taps_done, ab_ready, sq_done, sums_done, rooted,
                  sqrt_done, dft_done, dft_out, dve_line, act_line)):
        ada_in = (ada_in0, ada_in1)
        cond = buf(ctx, nc, "cond", [P, KD, 2])
        z = buf(ctx, nc, "features", [EMB, TOK])
        w1 = buf(ctx, nc, "hy_w1", [EMB, HYF])
        w2 = buf(ctx, nc, "hy_w2", [HYF, HYF])
        w3 = buf(ctx, nc, "hy_w3", [HYF, 4 * HYW])
        col = buf(ctx, nc, "hy_cols", [HYF, 3])
        times = buf(ctx, nc, "hy_times", [P, 2, NT])
        decay = buf(ctx, nc, "decay", [P, 4 * HYW])
        arg = buf(ctx, nc, "sine_arg", [HYF, TOK])
        turn = buf(ctx, nc, "sine_turn", [HYF, TOK])
        h = buf(ctx, nc, "sine", [HYF, TOK])
        env = buf(ctx, nc, "envelope", [P, 4 * HYW])
        tmp = buf(ctx, nc, "bwd_taps", [P, 2, HYW])
        AB = buf(ctx, nc, "taps", [P, 2, NT, 2, HYW])
        ones = buf(ctx, nc, "ones", [P, P])
        root = buf(ctx, nc, "filter_norm", [P, 2, 2 * HYW])
        cf = buf(ctx, nc, "cos_fwd", [P, DFT])
        sf = buf(ctx, nc, "sin_fwd", [P, DFT])
        block = ctx.enter_context(nc.Block())
        A, B = AB[:, 0], AB[:, 1]
        four = ps[:, 0:4 * HALF]
        sq = env
        rows = buf(ctx, nc, "mod_rows", [2, MOD_FIRST])
        pos = spare[:, 0:(NT - 1) * D].rearrange("p (t d) -> p t d", d=D)
        w = [K[:, :, :, :].rearrange("p t o c -> p (t o c)")[:, 0:KD * HALF] for K in (KC, KS)]

        @block.sync
        def _(sp):
            for dst, src in ((z, "hy_z"), (w1, "hy_w1"), (w2, "hy_w2"), (col, "hy_cols"),
                             (w3, "hy_w3"), (times, "hy_times")):
                sp.dma_start(dst[:], T[src]).then_inc(small_in, 16)
            sp.dma_start(decay[:], T["hy_decay"].partition_broadcast(P)).then_inc(decay_in, 16)
            sp.dma_start(X[:], T["x"]).then_inc(x_in, 16)
            sp.dma_start(pos, T["pos"]).then_inc(x_in, 16)
            sp.dma_start(cf[:], T["cos_fwd"]).then_inc(dft_in, 16)
            sp.dma_start(sf[:], T["sin_fwd"]).then_inc(dft_in, 16)
            sp.wait_ge(rows_added, blocks)
            sp.dma_start(mod[:, 0:MOD_FIRST], rows[:]).then_inc(mod_out, 16)
            sp.wait_ge(mod_out, 16)

        @block.gpsimd
        def _(pool):
            pool.memset(ident[:], 0.0).then_inc(ident_set, 1)
            pool.dma_start(cond[:], T["cond"]).then_inc(cond_in, 16)
            for b in range(blocks):
                if b >= 2:
                    pool.wait_ge(ada_used, b - 1)
                pool.dma_start(w[b % 2], T["ada_first"][b]).then_inc(ada_in[b % 2], 16)
                if b == 0:
                    for g in range(2):
                        pool.dma_start(rows[g:g + 1, :], T["ada_b"][:, 0:MOD_FIRST]
                                       ).then_inc(bias_in, 16)
            pool.wait_ge(ident_set, 1)
            pool.affine_select(out=ident[:], in_=ident[:], compare_op=ALU.not_equal, fill=1.0,
                               base=0, pattern=[[-1, P]], channel_multiplier=1
                               ).then_inc(ident_set, 1)
            pool.wait_ge(ident_set, 2)

        @block.tensor
        def _(pe):
            def sine_layer(wl, src):
                pe.matmul(ps[0:HYF, 0:HALF], wl[:], src[:, 0:HALF], start=True, stop=True)
                pe.matmul(ps[0:HYF, HALF:TOK], wl[:], src[:, HALF:TOK],
                          start=True, stop=True).then_inc(layer_done, 1)

            def modulation(b):
                pe.wait_ge(ada_in[b % 2], 16 * (b // 2 + 1))
                at = (4 + b) * HALF
                for k in range(KD):
                    mm = pe.matmul(ps[0:2, at:at + HALF], cond_s[:, k, :],
                                   w[b % 2][:, k * HALF:(k + 1) * HALF],
                                   start=(k == 0), stop=(k == KD - 1))
                mm.then_inc(ada_used, 1)

            pe.wait_ge(small_in, 6 * 16)
            sine_layer(w1, z)
            pe.wait_ge(cond_ready, 1)
            modulation(0)
            pe.wait_ge(sines_done, 1)
            sine_layer(w2, h)
            pe.wait_ge(sines_done, 2)
            for t in range(NT):
                if t:
                    pe.wait_ge(taps_done, t)
                for j in range(4):
                    mm = pe.matmul(ps[:, j * HALF:(j + 1) * HALF], h[:, t * P:(t + 1) * P],
                                   w3[:, j * HYW:(j + 1) * HYW], start=True, stop=True)
                mm.then_inc(taps_raw, 1)
                if 0 < t < blocks:
                    modulation(t)
            pe.wait_ge(dft_in, 32)
            pe.wait_ge(taps_done, NT)
            for n in range(4 * NT):
                t, way, o = n // 4, n // 2 % 2, n % 2
                pe.wait_ge(ab_ready, NT if t else 1)
                if n >= 4:
                    pe.wait_ge(dft_out, n - 3)
                at = (n % 4) * HALF
                for k in sources(t):
                    mm = pe.matmul(ps[:, at:at + HALF], dft_block((cf, sf)[way], k, t),
                                   AB[:, way, k, o, :], start=(k == sources(t)[0]),
                                   stop=(k == sources(t)[-1]))
                mm.then_inc(dft_done, 1)
                if 3 <= n < 3 + NT:
                    ts = n - 3
                    pe.wait_ge(rows_added, blocks)
                    pe.wait_ge(sq_done, ts + 1)
                    for o in range(2):
                        at = (4 + 2 * group_of(ts) + o) * HALF
                        mm = pe.matmul(ps[:, at:at + HALF], ones[:], sq[:, o * HYW:(o + 1) * HYW],
                                       start=(ts < 2), stop=(ts in (0, NT - 1)))
                    mm.then_inc(sums_done, 1)

        @block.scalar
        def _(act):
            line = Line(act, act_line)
            act.wait_ge(cond_in, 16)
            act.activation(cond_s[:], cond[:], ACT.Silu).then_inc(cond_ready, 1)
            act.wait_ge(decay_in, 16)
            line.then(act.activation(decay[:], decay[:], ACT.Abs))
            for layer in range(2):
                act.wait_ge(args_ready, layer + 1)
                act.activation(h[:], arg[:], ACT.Sin).then_inc(sines_done, 1)
            act.wait_ge(small_in, 6 * 16)
            for t in range(NT):
                if t:
                    act.wait_ge(taps_done, t)
                act.activation(env[:], decay[:], ACT.Exp,
                               scale=times[:, 0, t:t + 1]).then_inc(env_done, 1)
            for n in range(4 * NT):
                if n == 4 * NT - 6:
                    act.wait_ge(rooted, 1)
                    act.activation(root[:], root[:], ACT.Sqrt).then_inc(sqrt_done, 1)
                act.wait_ge(dft_done, n + 1)
                at = (n % 4) * HALF
                act.activation((KC, KS)[n // 2 % 2][:, n // 4, n % 2, :], ps[:, at:at + HALF],
                               ACT.Copy).then_inc(dft_out, 1)

        @block.vector
        def _(dve):
            line = Line(dve, dve_line)
            line.then(dve.memset(ones[:], 1.0))
            dve.wait_ge(small_in, 6 * 16)

            def add_bias(b):
                dve.wait_ge(ada_used, b + 1)
                r = rows[:, b * HALF:(b + 1) * HALF]
                at = (4 + b) * HALF
                dve.tensor_tensor(r, r, ps[0:2, at:at + HALF], ALU.add).then_inc(rows_added, 1)

            for layer in range(2):
                dve.wait_ge(layer_done, layer + 1)
                line.then(dve.tensor_scalar(arg[:], ps[0:HYF, 0:TOK], col[:, layer:layer + 1],
                                            col[:, 2:3], ALU.add, ALU.mult))
                reduce_turns(dve, line, arg, turn)
                dve.sem_inc(args_ready, 1)
            for t in range(NT):
                dve.wait_ge(taps_raw, t + 1)
                dve.wait_ge(env_done, t + 1)
                raw = four.rearrange("p (o d c) -> p o d c", o=2, d=2)
                e = env[:, :].rearrange("p (o d c) -> p o d c", o=2, d=2)
                dve.tensor_tensor(A[:, t], raw[:, :, 0, :], e[:, :, 0, :], ALU.mult)
                line.then(dve.scalar_tensor_tensor(out=tmp[:], in0=raw[:, :, 1, :],
                                                   scalar=times[:, 1, t:t + 1],
                                                   in1=e[:, :, 1, :], op0=ALU.mult, op1=ALU.mult))
                dve.sem_inc(taps_done, 1)
                dve.tensor_tensor(B[:, t], A[:, t], tmp[:], ALU.subtract)
                line.then(dve.tensor_tensor(A[:, t], A[:, t], tmp[:], ALU.add))
                dve.sem_inc(ab_ready, 1)
            dve.wait_ge(bias_in, 32)
            for b in range(blocks):
                add_bias(b)
            dve.wait_ge(x_in, 32)
            dve.tensor_tensor(X[:, 1:NT, :], X[:, 1:NT, :], pos, ALU.add).then_inc(x_ready, 1)
            q = sq[:, 0:2 * HYW]
            q2 = sq[:, 2 * HYW:4 * HYW]
            for t in range(NT):
                if t:
                    dve.wait_ge(sums_done, t)
                a, b = (v[:, t].rearrange("p o c -> p (o c)") for v in (A, B))
                dve.tensor_tensor(q, a, a, ALU.mult)
                line.then(dve.tensor_tensor(q2, b, b, ALU.mult))
                dve.tensor_tensor(q, q, q2, ALU.add).then_inc(sq_done, 1)
                dve.wait_ge(sq_done, t + 1)
            dve.wait_ge(sums_done, NT)
            line.then(dve.tensor_scalar(root[:], ps[:, 4 * HALF:8 * HALF]
                                        .rearrange("p (g n) -> p g n", g=2),
                                        0.5, EPS, ALU.mult, ALU.add))
            dve.reciprocal(root[:], root[:]).then_inc(rooted, 1)
            dve.wait_ge(sqrt_done, 1)
            for t in range(NT):
                dve.wait_ge(dft_out, 4 * t + 4)
                for K in (KC, KS):
                    v = K[:, t].rearrange("p o c -> p (o c)")
                    ins = dve.tensor_tensor(v, v, root[:, group_of(t), :], ALU.mult)
                line.then(ins)


def reduce_turns(dve, line, arg, turn):
    hi = 6.28125
    line.then(dve.tensor_scalar(turn[:], arg[:], 1.0 / TWO_PI, ROUND, ALU.mult, ALU.add))
    line.then(dve.tensor_scalar(turn[:], turn[:], ROUND, None, ALU.subtract))
    line.then(dve.scalar_tensor_tensor(out=arg[:], in0=turn[:], scalar=-hi, in1=arg[:],
                                       op0=ALU.mult, op1=ALU.add))
    line.then(dve.scalar_tensor_tensor(out=arg[:], in0=turn[:], scalar=-(TWO_PI - hi),
                                       in1=arg[:], op0=ALU.mult, op1=ALU.add))
    line.then(dve.tensor_scalar(arg[:], arg[:], PI_BELOW, -PI_BELOW, ALU.min, ALU.max))


def short_conv(dve, line, out, x, taps):
    line.then(dve.tensor_scalar(out, x, taps(1), taps(3), ALU.mult, ALU.add))
    for tap, lead in ((0, 1), (2, 0)):
        for a, b in GROUPS:
            n = b - a - 1
            ins = dve.scalar_tensor_tensor(
                out=out[:, a + lead:a + lead + n], in0=x[:, a + 1 - lead:a + 1 - lead + n],
                scalar=taps(tap), in1=out[:, a + lead:a + lead + n], op0=ALU.mult, op1=ALU.add)
        line.then(ins)


def even_inputs(nc, T, ps, HT, VG, US, ident, mats, bias, mats_in):
    hyena, blocks = 3 * HYW // P, 16
    with stage(nc, "w_in0", "w_in1", "used", "x_out", "x_used", "taps_in", "conv_done", "turned",
               "vg_out", "dve_line") as (
            ctx, (w_in0, w_in1, used, x_out, x_used, taps_in, conv_done, turned, vg_out,
                  dve_line)):
        w_in = (w_in0, w_in1)
        w = buf(ctx, nc, "w_block", [P, 2, KD * P])
        taps = buf(ctx, nc, "conv_taps", [P, hyena, 4])
        cur = buf(ctx, nc, "conv_taps_cur", [P, 4])
        x = buf(ctx, nc, "conv_source", [P, 2, TOK])
        y = buf(ctx, nc, "conv_block", [P, 2, TOK])
        block = ctx.enter_context(nc.Block())

        @block.sync
        def _(sp):
            W = T["ev_w_in"]
            for b in range(2):
                sp.dma_start(w[:, b, :], W[b]).then_inc(w_in[b], 16)
            sp.dma_start(taps[:], T["hy_taps"]).then_inc(taps_in, 16)
            with sp.Fori(1, blocks // 2) as i:
                for b in range(2):
                    sp.wait_ge(used, 2 * i + (b - 1))
                    sp.dma_start(w[:, b, :], W[2 * i + b]).then_inc(w_in[b], 16)
            for dst, src in zip(mats, ("cos_fwd", "sin_fwd", "cos_inv", "sin_inv")):
                sp.dma_start(dst[:], T[src]).then_inc(mats_in, 16)
            sp.dma_start(bias[:], T["hy_bias"].partition_broadcast(P)).then_inc(mats_in, 16)

        @block.tensor
        def _(pe):
            def products(i, b):
                pe.wait_ge(w_in[b], 16 * i + 16)
                if not isinstance(i, int) or i:
                    pe.wait_ge(x_out, 2 * i + (b - 1))
                at = 2 * b * HALF
                for k in range(KD):
                    lhs = w[:, b, k * P:(k + 1) * P]
                    pe.matmul(ps[:, at:at + LAT], lhs, HT[:, k, CTX:TOK],
                              start=(k == 0), stop=(k == KD - 1))
                    mm = pe.matmul(ps[:, at + HALF:at + HALF + CTX], lhs, HT[:, k, 0:CTX],
                                   start=(k == 0), stop=(k == KD - 1))
                mm.then_inc(used, 1)

            def turn(i, b):
                pe.wait_ge(vg_out, 2 * i + (b + 1))
                pe.wait_ge(conv_done, 2 * i + (b + 1))
                for t in range(NT):
                    at = (4 + 2 * b) * HALF + t * P
                    mm = pe.transpose(ps[:, at:at + P], y[:, b, t * P:(t + 1) * P], ident[:])
                mm.then_inc(turned, 1)

            for b in range(2):
                products(0, b)
            with pe.Fori(1, hyena // 2) as i:
                for b in range(2):
                    products(i, b)
                    turn(i - 1, b)
            for b in range(2):
                products(hyena // 2, b)
                turn(hyena // 2 - 1, b)
            for b in range(2):
                products(hyena // 2 + 1, b)

        @block.scalar
        def _(act):
            def drain(i, b, OUT, n):
                act.wait_ge(used, 2 * i + (b + 1))
                act.activation(OUT[:, n, CTX:TOK], ps[:, 2 * b * HALF:2 * b * HALF + LAT],
                               ACT.Copy)
                act.activation(OUT[:, n, 0:CTX], ps[:, (2 * b + 1) * HALF:(2 * b + 1) * HALF + CTX],
                               ACT.Copy).then_inc(x_out, 1)

            def place(i, b):
                act.wait_ge(turned, 2 * i + (b + 3))
                act.activation(VG[:, :, bass.ds(i * (2 * P) + b * P, P)],
                               ps[:, (4 + 2 * b) * HALF:(4 + 2 * b) * HALF + TOK]
                               .rearrange("p (t c) -> p t c", c=P), ACT.Copy).then_inc(vg_out, 1)

            for b in range(2):
                drain(0, b, x, b)
            act.sem_inc(vg_out, 2)
            with act.Fori(1, hyena // 2) as i:
                for b in range(2):
                    act.wait_ge(x_used, 2 * i + (b - 1))
                    drain(i, b, x, b)
                    place(i - 1, b)
            for b in range(2):
                drain(hyena // 2, b, US, b)
                place(hyena // 2 - 1, b)
            for b in range(2):
                drain(hyena // 2 + 1, b, US, 2 + b)

        @block.vector
        def _(dve):
            line = Line(dve, dve_line)
            dve.wait_ge(taps_in, 16)
            dve.sem_inc(turned, 2)
            with line.loop(0, hyena // 2, 8) as i:
                for b in range(2):
                    line.then(dve.tensor_copy(cur[:, :].unsqueeze(1),
                                              taps[:, bass.ds(i * 2 + b, 1), :]))
                    dve.wait_ge(x_out, i * 2 + (b + 1))
                    dve.wait_ge(turned, i * 2 + (b + 1))
                    short_conv(dve, line, y[:, b, :], x[:, b, :], lambda k: cur[:, k:k + 1])
                    dve.sem_inc(conv_done, 1)
                    dve.sem_inc(x_used, 1)


def hyena_convolve(nc, ps, VG, KC, KS, MIXT, ident, mats, bias, mats_in):
    with stage(nc, "angles", "mixed", "lines", "z_ready", "turned", "out_done",
               "dve_line") as (
            ctx, (angles, mixed, lines, z_ready, turned, out_done, dve_line)):
        cf, sf, ci, si = mats
        R = buf(ctx, nc, "product_re", [P, NT, HYW])
        I = buf(ctx, nc, "product_im", [P, NT, HYW])
        t1 = buf(ctx, nc, "part1", [P, HYW])
        t2 = buf(ctx, nc, "part2", [P, HYW])
        t3 = buf(ctx, nc, "part3", [P, HYW])
        t4 = buf(ctx, nc, "part4", [P, HYW])
        z = VG[:, :, 0:HYW]
        block = ctx.enter_context(nc.Block())

        @block.tensor
        def _(pe):
            pe.wait_ge(mats_in, 80)
            for o in range(2):
                if o:
                    pe.wait_ge(z_ready, NT * o)
                for t in range(NT):
                    n = NT * o + t
                    if n >= 2:
                        pe.wait_ge(mixed, n - 1)
                    for j, m in enumerate((cf, sf)):
                        at = (2 * (n % 2) + j) * HALF
                        for k in sources(t):
                            mm = pe.matmul(ps[:, at:at + HALF], dft_block(m, k, t), z[:, k, :],
                                           start=(k == sources(t)[0]), stop=(k == sources(t)[-1]))
                    mm.then_inc(angles, 1)
                for t in range(NT):
                    n = NT * o + t
                    pe.wait_ge(mixed, NT * o + sources(t)[-1] + 1)
                    if n >= 2:
                        pe.wait_ge(z_ready, n - 1)
                    at = (4 + n % 2) * HALF
                    for k in sources(t):
                        pe.matmul(ps[:, at:at + HALF], dft_block(ci, k, t), R[:, k, :],
                                  start=(k == sources(t)[0]), stop=False)
                        mm = pe.matmul(ps[:, at:at + HALF], dft_block(si, k, t), I[:, k, :],
                                       start=False, stop=(k == sources(t)[-1]))
                    mm.then_inc(lines, 1)
            for t in range(NT):
                pe.wait_ge(z_ready, NT + t + 1)
                if t >= 2:
                    pe.wait_ge(out_done, t - 1)
                for m in range(4):
                    at = (6 + t % 2) * HALF + m * P
                    mm = pe.transpose(ps[:, at:at + P], z[:, t, m * P:(m + 1) * P], ident[:])
                mm.then_inc(turned, 1)

        @block.scalar
        def _(act):
            for t in range(NT):
                act.wait_ge(turned, t + 1)
                at = (6 + t % 2) * HALF
                act.activation(MIXT[:, 0:4, t * P:(t + 1) * P], ps[:, at:at + HALF]
                               .rearrange("p (m c) -> p m c", c=P), ACT.Copy).then_inc(out_done, 1)

        @block.vector
        def _(dve):
            line = Line(dve, dve_line)
            dve.wait_ge(mats_in, 80)
            for o in range(2):
                for t in range(NT):
                    n = NT * o + t
                    dve.wait_ge(angles, n + 1)
                    b = 2 * (n % 2) * HALF
                    zc, zs = ps[:, b:b + HALF], ps[:, b + HALF:b + 2 * HALF]
                    dve.tensor_tensor(t1[:], zc, KC[:, t, o, :], ALU.mult)
                    dve.tensor_tensor(t2[:], zs, KS[:, t, o, :], ALU.mult)
                    dve.tensor_tensor(t3[:], zs, KC[:, t, o, :], ALU.mult)
                    line.then(dve.tensor_tensor(t4[:], zc, KS[:, t, o, :], ALU.mult))
                    dve.tensor_tensor(R[:, t, :], t1[:], t2[:], ALU.subtract)
                    line.then(dve.tensor_tensor(I[:, t, :], t3[:], t4[:], ALU.add))
                    dve.sem_inc(mixed, 1)
                for t in range(NT):
                    n = NT * o + t
                    dve.wait_ge(lines, n + 1)
                    at = (4 + n % 2) * HALF
                    line.then(dve.tensor_tensor(t1[:], z[:, t, :], bias[:, o, :], ALU.mult))
                    line.then(dve.tensor_tensor(t1[:], t1[:], ps[:, at:at + HALF], ALU.add))
                    dve.tensor_tensor(z[:, t, :], t1[:], VG[:, t, (o + 1) * HYW:(o + 2) * HYW],
                                      ALU.mult).then_inc(z_ready, 1)
                    dve.wait_ge(z_ready, n + 1)


PAIRS = 16
S5C = 16
UNITS = 8
SEGMENTS = (((0, CTX, False), (CTX, TOK, True)), ((0, LAT, True), (LAT, TOK, False)))


def exact_exp(dve, one, out, x, n, y, bits):
    one(dve.tensor_scalar(n, x, 1.0 / math.log(2.0), ROUND, ALU.mult, ALU.add))
    one(dve.tensor_scalar(n, n, ROUND, None, ALU.subtract))
    one(dve.tensor_scalar(n, n, -126.0, 127.0, ALU.max, ALU.min))
    one(dve.scalar_tensor_tensor(out=y, in0=n, scalar=-0.693359375, in1=x, op0=ALU.mult, op1=ALU.add))
    one(dve.scalar_tensor_tensor(out=y, in0=n, scalar=0.693359375 - math.log(2.0), in1=y,
                                 op0=ALU.mult, op1=ALU.add))
    one(dve.tensor_scalar(y, y, -0.35, 0.35, ALU.max, ALU.min))
    one(dve.tensor_scalar(n, n, 127.0, None, ALU.add))
    one(dve.tensor_copy(bits, n))
    one(dve.tensor_scalar(bits, bits, 23, None, ALU.logical_shift_left))
    one(dve.tensor_scalar(out, y, 1.0 / 5040, 1.0 / 720, ALU.mult, ALU.add))
    for c in (1.0 / 120, 1.0 / 24, 1.0 / 6, 0.5, 1.0, 1.0):
        one(dve.tensor_tensor(out, out, y, ALU.mult))
        one(dve.tensor_scalar(out, out, c, None, ALU.add))
    one(dve.tensor_tensor(out, out, bits.bitcast(F32), ALU.mult))


def s5(nc, T, ps, US, G, ident, out_re, out_im, cond_s, mod):
    with stage(nc, "par_in", "d_in", "dve_line", "act_line", "pool_line", "bd_ready", "bt_raw",
               "bt_ready", "bu_done", "bu_used", "turn_set", "turn_used", "trig_set", "trig_used",
               "prod_set", "prod_used", "y_done", "y_out", "states_out", "waited",
               "ada_in0", "ada_in1", "ada_used", "ada_copied", "mod_out0", "mod_out1", "ones_set") as (
            ctx, (par_in, d_in, dve_line, act_line, pool_line, bd_ready, bt_raw, bt_ready, bu_done,
                  bu_used, turn_set, turn_used, trig_set, trig_used, prod_set, prod_used, y_done,
                  y_out, states_out, mark, ada_in0, ada_in1, ada_used, ada_copied, mod_out0,
                  mod_out1, ones_set)):
        ada_in, mod_out = (ada_in0, ada_in1), (mod_out0, mod_out1)
        assert MOD_BLOCKS == 4 * UNITS
        ada = buf(ctx, nc, "ada_block", [P, 2, KD * MOD_W])
        ada_b = buf(ctx, nc, "ada_bias", [1, 2, MOD_W])
        rows = buf(ctx, nc, "mod_rows", [2, 2, MOD_W])
        ones = buf(ctx, nc, "one_one", [1, 2])
        N2 = [P, 2, PAIRS]
        par = buf(ctx, nc, "s5_par", [P, 5, 2 * PAIRS])
        B = buf(ctx, nc, "s5_B", [P, 2, 2 * PAIRS, S5C])
        C = buf(ctx, nc, "s5_C", [P, 2, 2 * PAIRS, S5C])
        Bb = buf(ctx, nc, "s5_Bbar", [P, 2, 2 * PAIRS, S5C])
        tmpB = buf(ctx, nc, "s5_tmpB", [P, 2 * PAIRS, S5C])
        C3 = buf(ctx, nc, "s5_C3", [P, 3, 2 * PAIRS, S5C])
        dt = buf(ctx, nc, "s5_dt", [P, 2 * PAIRS])
        r = buf(ctx, nc, "s5_r", [P, 2 * PAIRS])
        hl = buf(ctx, nc, "s5_turns", [P, 3, 2 * PAIRS])
        phi = buf(ctx, nc, "s5_phi", [P, 2 * PAIRS])
        w1 = buf(ctx, nc, "s5_w1", [P, 2 * PAIRS])
        w2 = buf(ctx, nc, "s5_w2", [P, 2 * PAIRS])
        lr = buf(ctx, nc, "s5_lr", [P, 2 * PAIRS])
        li = buf(ctx, nc, "s5_li", [P, 2 * PAIRS])
        fr = buf(ctx, nc, "s5_fr", [P, 2 * PAIRS])
        fi = buf(ctx, nc, "s5_fi", [P, 2 * PAIRS])
        whole = buf(ctx, nc, "s5_exponent", [P, 2 * PAIRS], I32)
        quarter = buf(ctx, nc, "quarter_turn", [P, 1])
        steps = buf(ctx, nc, "steps", [P, 2, TOK])
        dcol = buf(ctx, nc, "s5_d", [P, 4])
        Bd = buf(ctx, nc, "s5_Bd", [P, 2, 2, 4, 2 * S5C])
        Cd = buf(ctx, nc, "s5_Cd", [P, 3, 2, 4, 2 * S5C])
        BT = buf(ctx, nc, "s5_BT", [P, 2, 2, P])
        cur = buf(ctx, nc, "s5_cur", [P, 3, 2, 4])
        turns = buf(ctx, nc, "s5_turns_cur", [P, 3, 2, 4])
        k_t = buf(ctx, nc, "s5_whole", [P, TOK])
        lo_t = buf(ctx, nc, "s5_rest", [P, TOK])
        ang = buf(ctx, nc, "s5_angle", [P, 2, TOK])
        ang_abs = buf(ctx, nc, "s5_angle_abs", [P, TOK])
        trig = buf(ctx, nc, "s5_trig", [P, 2, 2, TOK])
        g_in = buf(ctx, nc, "s5_g_in", [P, 4, TOK])
        g = buf(ctx, nc, "s5_g", [P, 2, TOK])
        prod = buf(ctx, nc, "s5_prod", [P, 2, 4, TOK])
        st = buf(ctx, nc, "s5_states", [P, 2, 2, PAIRS])
        ucur = buf(ctx, nc, "s5_u", [P, TOK])
        dnow = buf(ctx, nc, "s5_d_cur", [P, 1])
        block = ctx.enter_context(nc.Block())
        BU = (slice(0, TOK), slice(1024, 1024 + TOK))
        Y0 = 4 * HALF
        BT0 = 6 * HALF
        ADA0 = 7 * HALF
        SCALE = 6.283185

        def block_units(a, m):
            return a.rearrange("p c (d k) -> p c d k", d=2)[:, :, :, bass.ds(m * 4, 4)]

        @block.sync
        def _(sp):
            for dst, src in ((par, "s5_par"), (B, "s5_B"), (C, "s5_C"), (dcol, "s5_d")):
                sp.dma_start(dst[:], T[src]).then_inc(par_in, 16)
            sp.dma_start(steps[:], T["s5_steps"].partition_broadcast(P)).then_inc(d_in, 16)

            def ada_load(n, b):
                sp.dma_start(ada[:, b, :], T["ada_rest"][n]).then_inc(ada_in[b], 16)
                sp.dma_start(ada_b[:, b, :], T["ada_b"][:, bass.ds(n * MOD_W + MOD_FIRST, MOD_W)]
                             ).then_inc(ada_in[b], 16)

            def ada_store(n, b):
                sp.wait_ge(ada_copied, n + 2)
                sp.dma_start(mod[:, bass.ds(n * MOD_W + MOD_FIRST, MOD_W)], rows[:, b, :]
                             ).then_inc(mod_out[b], 16)

            for b in range(2):
                ada_load(b, b)
            with sp.Fori(0, MOD_BLOCKS // 2 - 1) as i:
                for b in range(2):
                    sp.wait_ge(ada_used, i * 2 + (b + 1))
                    ada_load(i * 2 + (b + 2), b)
                    ada_store(i * 2 + b, b)
            for b in range(2):
                ada_store(MOD_BLOCKS - 2 + b, b)
                sp.wait_ge(mod_out[b], 16 * MOD_BLOCKS // 2 + 16)
            sp.wait_ge(y_done, 8)
            for part, out in ((0, out_re), (1, out_im)):
                sp.dma_start(out.rearrange("d (k g) s -> (g s) d k", g=2), st[:, part],
                             allow_slow_non_contiguous=True).then_inc(states_out, 16)
            sp.wait_ge(states_out, 32)

        @block.gpsimd
        def _(pool):
            line = Line(pool, pool_line)
            pool.wait_ge(d_in, 16)
            pool.wait_ge(bd_ready, 1)
            with line.loop(0, 4, 1 + UNITS * 7) as m:
                line.then(pool.tensor_copy(turns[:], block_units(hl, m)), mark)
                for u in range(UNITS):
                    q, d = u // 2, u % 2
                    b = u % 2
                    both, hi, lo = (turns[:, c, d, q:q + 1] for c in range(3))
                    s, a = steps[:, d, :], ang[:, b, :]
                    line.then(pool.tensor_scalar(k_t[:], s, both, ROUND, ALU.mult, ALU.add), mark)
                    wait_apart(pool, turn_used, m * UNITS + (u + 1), mark)
                    line.then(pool.tensor_scalar(k_t[:], k_t[:], 1.0, -ROUND, ALU.mult, ALU.add), mark)
                    line.then(pool.tensor_scalar(a, s, hi, 0.0, ALU.mult, ALU.add), mark)
                    line.then(pool.tensor_scalar(lo_t[:], s, lo, 0.0, ALU.mult, ALU.add))
                    line.then(pool.tensor_tensor(a, a, k_t[:], ALU.subtract))
                    line.then(pool.tensor_tensor(a, a, lo_t[:], ALU.add), mark)
                    line.then(pool.tensor_scalar(a, a, 0.5, -0.5, ALU.min, ALU.max))
                    pool.sem_inc(turn_set, 1)

        @block.scalar
        def _(act):
            line = Line(act, act_line)
            act.wait_ge(bd_ready, 1)
            line.then(act.activation(w1[:], phi[:], ACT.Sin, scale=SCALE))
            line.then(act.activation(w2[:], phi[:], ACT.Abs))
            line.then(act.activation(w2[:], w2[:], ACT.Sin, bias=quarter[:], scale=-SCALE))
            act.sem_inc(turn_used, 2)
            act.sem_inc(ada_copied, 1)
            for b in range(2):
                act.sem_inc(mod_out[b], 16)

            def ada_copy(m, u):
                b = u % 2
                act.wait_ge(ada_used, m * UNITS + (u + 1))
                act.wait_ge(mod_out[b], m * (16 * UNITS // 2) + 16 * (u // 2 + 1))
                act.activation(rows[:, b, :], ps[0:2, ADA0:ADA0 + MOD_W], ACT.Copy
                               ).then_inc(ada_copied, 1)
            with line.loop(0, 4, UNITS + 1) as m:
                for u in range(UNITS):
                    b = u % 2
                    act.wait_ge(turn_set, m * UNITS + (u + 1))
                    act.wait_ge(trig_used, m * UNITS + (u + 1))
                    line.then(act.activation(ang_abs[:], ang[:, b, :], ACT.Abs))
                    act.activation(trig[:, b, 1, :], ang[:, b, :], ACT.Sin, scale=SCALE
                                   ).then_inc(trig_set, 1)
                    act.activation(trig[:, b, 0, :], ang_abs[:], ACT.Sin, bias=quarter[:],
                                   scale=-SCALE).then_inc(trig_set, 1)
                    act.wait_ge(trig_set, m * (2 * UNITS) + (2 * u + 2))
                    act.sem_inc(turn_used, 1)
                    if u == 0:
                        act.wait_ge(bt_raw, m + 1)
                        line.then(act.activation(BT[:, :, :, :].rearrange("p a b n -> p (a b n)"),
                                                 ps[:, BT0:BT0 + 4 * P], ACT.Copy))
                        act.sem_inc(bt_ready, 1)
                    ada_copy(m, u)
            act.wait_ge(y_done, 8)
            act.activation(G[:], G[:], ACT.Gelu_apprx_tanh).then_inc(y_out, 1)
            act.wait_ge(y_out, 1)

        @block.tensor
        def _(pe):
            def bu(m, u):
                q, d = u // 2, u % 2
                pe.wait_ge(bu_used, m * UNITS + (u + 1))
                rows = slice(32 * q, 32 * q + 32)
                for part in range(2):
                    at = BU[part].start
                    for c0, c1 in ((0, HALF), (HALF, TOK)):
                        mm = pe.matmul(ps[:, at + c0:at + c1], BT[rows, d, part, :],
                                       ucur[rows, c0:c1], start=True, stop=True)
                mm.then_inc(bu_done, 1)

            def readout(m, u):
                q, d = u // 2, u % 2
                pe.wait_ge(prod_set, m * UNITS + (u + 1))
                for j, c in enumerate((0, 1, 2, 2)):
                    for c0, c1 in ((0, HALF), (HALF, TOK)):
                        mm = pe.matmul(ps[32 * q:32 * q + 32, Y0 + c0:Y0 + c1],
                                       Cd[:, c, d, q, :], prod[:, u % 2, j, c0:c1],
                                       start=(d == 0 and j == 0), stop=(d == 1 and j == 3))
                mm.then_inc(prod_used, 1)

            def ada_rows(m, u):
                b = u % 2
                pe.wait_ge(ada_in[b], m * (32 * UNITS // 2) + 32 * (u // 2 + 1))
                pe.wait_ge(ada_copied, m * UNITS + (u + 1))
                for k in range(KD):
                    pe.matmul(ps[0:2, ADA0:ADA0 + MOD_W], cond_s[:, k, :],
                              ada[:, b, k * MOD_W:(k + 1) * MOD_W], start=(k == 0), stop=False)
                pe.matmul(ps[0:2, ADA0:ADA0 + MOD_W], ones[:], ada_b[:, b, :],
                          start=False, stop=True).then_inc(ada_used, 1)

            pe.wait_ge(ones_set, 1)
            with pe.Fori(0, 4) as m:
                pe.wait_ge(bd_ready, m + 2)
                for d in range(2):
                    for part in range(2):
                        at = BT0 + (2 * d + part) * P
                        mm = pe.transpose(ps[:, at:at + P],
                                          Bd[:, d, part].rearrange("p q c -> p (q c)"), ident[:])
                mm.then_inc(bt_raw, 1)
                pe.wait_ge(bt_ready, m + 1)
                for u in range(UNITS):
                    bu(m, u)
                    ada_rows(m, u)
                    if u:
                        readout(m, u - 1)
                readout(m, UNITS - 1)

        @block.vector
        def _(dve):
            line = Line(dve, dve_line)
            one = line.then
            tt, ts = dve.tensor_tensor, dve.tensor_scalar
            dve.memset(ones[:], 1.0).then_inc(ones_set, 1)
            dve.memset(Bd[:], 0.0)
            dve.memset(Cd[:], 0.0)
            one(dve.memset(quarter[:], math.pi / 2))
            dve.wait_ge(par_in, 64)
            exact_exp(dve, one, dt[:], par[:, 2, :], w1[:], w2[:], whole[:])
            one(tt(lr[:], par[:, 0, :], dt[:], ALU.mult))
            exact_exp(dve, one, r[:], lr[:], w1[:], w2[:], whole[:])
            one(tt(phi[:], par[:, 1, :], dt[:], ALU.mult))
            one(ts(phi[:], phi[:], 1.0 / TWO_PI, None, ALU.mult))
            one(ts(w1[:], phi[:], ROUND, None, ALU.add))
            one(ts(w1[:], w1[:], ROUND, None, ALU.subtract))
            one(tt(phi[:], phi[:], w1[:], ALU.subtract))
            one(ts(w2[:], phi[:], 1536.0, None, ALU.add))
            one(ts(hl[:, 1, :], w2[:], 1536.0, None, ALU.subtract))
            one(tt(hl[:, 2, :], phi[:], hl[:, 1, :], ALU.subtract))
            one(dve.tensor_copy(hl[:, 0, :], phi[:]))
            dve.sem_inc(bd_ready, 1)
            dve.wait_ge(act_line, 3)
            one(tt(lr[:], r[:], w2[:], ALU.mult))
            one(tt(li[:], r[:], w1[:], ALU.mult))
            one(ts(lr[:], lr[:], -1.0, None, ALU.add))
            one(tt(w1[:], par[:, 0, :], par[:, 0, :], ALU.mult))
            one(tt(w2[:], par[:, 1, :], par[:, 1, :], ALU.mult))
            one(tt(w1[:], w1[:], w2[:], ALU.add))
            one(dve.reciprocal(w1[:], w1[:]))
            one(tt(fr[:], lr[:], par[:, 0, :], ALU.mult))
            one(tt(w2[:], li[:], par[:, 1, :], ALU.mult))
            one(tt(fr[:], fr[:], w2[:], ALU.add))
            one(tt(fr[:], fr[:], w1[:], ALU.mult))
            one(tt(fi[:], li[:], par[:, 0, :], ALU.mult))
            one(tt(w2[:], lr[:], par[:, 1, :], ALU.mult))
            one(tt(fi[:], fi[:], w2[:], ALU.subtract))
            one(tt(fi[:], fi[:], w1[:], ALU.mult))
            wide = [P, 2 * PAIRS, S5C]
            fr_w, fi_w = (f[:, :].unsqueeze(2).to_broadcast(wide) for f in (fr, fi))
            one(tt(Bb[:, 0], B[:, 0], fr_w, ALU.mult))
            one(tt(tmpB[:], B[:, 1], fi_w, ALU.mult))
            one(tt(Bb[:, 0], Bb[:, 0], tmpB[:], ALU.subtract))
            one(tt(Bb[:, 1], B[:, 1], fr_w, ALU.mult))
            one(tt(tmpB[:], B[:, 0], fi_w, ALU.mult))
            one(tt(Bb[:, 1], Bb[:, 1], tmpB[:], ALU.add))
            one(dve.tensor_copy(C3[:, 0], C[:, 0]))
            one(ts(C3[:, 1], C[:, 0], -1.0, None, ALU.mult))
            one(ts(C3[:, 2], C[:, 1], -1.0, None, ALU.mult))
            dve.sem_inc(trig_used, 2)
            dve.sem_inc(bu_used, 1)
            dve.wait_ge(d_in, 16)
            with line.loop(0, 4, 10 * UNITS + 2) as m:
                for n, (src, dst) in enumerate(((Bb, Bd), (C3, Cd))):
                    for part in range(2 + n):
                        for gr in range(2):
                            half = slice(64 * gr, 64 * gr + 64)
                            view = src[half, part].rearrange("p (d k) j -> p d k j", d=2)
                            to = dst[half, :, part] if n == 0 else dst[half, part]
                            dve.tensor_copy(to[:, :, :, S5C * gr:S5C * gr + S5C],
                                            view[:, :, bass.ds(m * 4, 4), :])
                dve.tensor_copy(ucur[:, :].unsqueeze(1), US[:, bass.ds(m, 1), :])
                dve.tensor_copy(cur[:, 0:1], block_units(r[:, :].unsqueeze(1), m))
                one(dve.tensor_copy(cur[:, 1:3], block_units(par[:, 3:5, :], m)))
                dve.sem_inc(bd_ready, 1)
                for u in range(UNITS):
                    q, d, b = u // 2, u % 2, u % 2
                    cos, sin = trig[:, b, 0, :], trig[:, b, 1, :]
                    way = (lambda a: a) if d == 0 else (lambda a: a[:, ::-1])
                    bre, bim = way(ps[:, BU[0]]), way(ps[:, BU[1]])
                    dve.wait_ge(bu_done, m * UNITS + (u + 1))
                    dve.wait_ge(trig_set, m * (2 * UNITS) + (2 * u + 2))
                    line.count(tt(g_in[:, 0], bre, cos, ALU.mult))
                    first_pair = line.count(tt(g_in[:, 1], bim, sin, ALU.mult))
                    line.count(tt(g_in[:, 2], bim, cos, ALU.mult))
                    second_pair = line.count(tt(g_in[:, 3], bre, sin, ALU.mult))
                    line.settle(upto=first_pair)
                    re_in = line.count(tt(g_in[:, 0], g_in[:, 0], g_in[:, 1], ALU.add))
                    line.settle(upto=second_pair)
                    dve.sem_inc(bu_used, 1)
                    im_in = line.count(tt(g_in[:, 2], g_in[:, 2], g_in[:, 3], ALU.subtract))
                    scanned = []
                    for part, ready in ((0, re_in), (1, im_in)):
                        line.settle(upto=ready)
                        for a, z, cached in SEGMENTS[d]:
                            first = cur[:, 1 + part, d, q:q + 1] if cached else 0.0
                            ins = dve.tensor_tensor_scan(
                                g[:, part, a:z], cur[:, 0, d, q:q + 1].to_broadcast([P, z - a]),
                                g_in[:, 2 * part, a:z], first, ALU.mult, ALU.add)
                        scanned.append(line.count(ins))
                    if u >= 2:
                        dve.wait_ge(prod_used, m * UNITS + (u - 1))
                    for part in range(2):
                        line.settle(upto=scanned[part])
                        for j, f in ((0, cos), (2, sin)) if part == 0 else ((1, sin), (3, cos)):
                            ins = tt(way(prod[:, b, j, :]), g[:, part, :], f, ALU.mult)
                    one(ins)
                    dve.sem_inc(prod_set, 1)
                    dve.sem_inc(trig_used, 1)
                    last = CTX - 1 if d == 0 else 0
                    one_st = [prod[:, b, j, last:last + 1].unsqueeze(1) for j in range(4)]
                    at = bass.ds(m * 4 + q, 1)
                    tt(st[:, 0, d:d + 1, at], one_st[0], one_st[1], ALU.subtract)
                    one(tt(st[:, 1, d:d + 1, at], one_st[2], one_st[3], ALU.add))
                dve.wait_ge(prod_used, m * UNITS + UNITS)
                dve.tensor_copy(dnow[:], dcol[:, bass.ds(m, 1)]).then_inc(y_done, 1)
                dve.wait_ge(y_done, m * 2 + 1)
                one(dve.scalar_tensor_tensor(out=G[:, bass.ds(m, 1), :], in0=ucur[:, :].unsqueeze(1),
                                             scalar=dnow[:], in1=ps[:, Y0:Y0 + TOK].unsqueeze(1),
                                             op0=ALU.mult, op1=ALU.add))
                dve.sem_inc(y_done, 1)


def s5_gate(nc, T, ps, G, MIXT, w_out, w_out_in):
    with stage(nc, "w_in", "mm_done", "sig_done", "bank_free") as (
            ctx, (w_in, mm_done, sig_done, bank_free)):
        w = buf(ctx, nc, "glu_w", [P, 4, 4 * P])
        bcol = buf(ctx, nc, "glu_b", [P, 4])
        sig = buf(ctx, nc, "glu_gate", [P, 4, TOK])
        block = ctx.enter_context(nc.Block())

        @block.sync
        def _(sp):
            sp.dma_start(w[:], T["glu_w"]).then_inc(w_in, 16)
            sp.dma_start(bcol[:], T["glu_b"]).then_inc(w_in, 16)
            sp.dma_start(w_out[:], T["ev_w_out"]).then_inc(w_out_in, 16)
            sp.wait_ge(w_in, 32)

        @block.tensor
        def _(pe):
            pe.wait_ge(w_in, 32)
            for m in range(4):
                at = 2 * m * HALF
                for k in range(4):
                    lhs = w[:, k, m * P:(m + 1) * P]
                    pe.matmul(ps[:, at:at + HALF], lhs, G[:, k, 0:HALF], start=(k == 0), stop=(k == 3))
                    mm = pe.matmul(ps[:, at + HALF:at + TOK], lhs, G[:, k, HALF:TOK],
                                   start=(k == 0), stop=(k == 3))
                mm.then_inc(mm_done, 1)

        @block.scalar
        def _(act):
            for m in range(4):
                act.wait_ge(mm_done, m + 1)
                act.activation(sig[:, m, :], ps[:, 2 * m * HALF:2 * m * HALF + TOK], ACT.Sigmoid,
                               bias=bcol[:, m:m + 1]).then_inc(sig_done, 1)

        @block.vector
        def _(dve):
            for m in range(4):
                dve.wait_ge(sig_done, m + 1)
                dve.tensor_tensor(MIXT[:, 4 + m, :], sig[:, m, :], G[:, m, :],
                                  ALU.mult).then_inc(bank_free, 1)
            dve.wait_ge(bank_free, 4)


def project_out(nc, ps, MIXT, w, w_in, X, mod, layer, g_chunk):
    with stage(nc, "g_in", "mm_done", "bank_free", "dve_line") as (
            ctx, (g_in, mm_done, bank_free, dve_line)):
        g_row = buf(ctx, nc, "gate_row", [P, 2, D])
        tmp = buf(ctx, nc, "gated", [P, 2, HALF])
        block = ctx.enter_context(nc.Block())

        @block.sync
        def _(sp):
            for g in range(2):
                sp.dma_start(g_row[:, g, :], mod_row(mod, layer, g, g_chunk)).then_inc(g_in, 16)

        @block.tensor
        def _(pe):
            pe.wait_ge(w_in, 16)
            for n in range(2 * NT):
                t, c = n // 2, n % 2
                if n >= 4:
                    pe.wait_ge(bank_free, n - 3)
                at = (n % 4) * HALF
                for k in range(KD):
                    mm = pe.matmul(ps[:, at:at + HALF], MIXT[:, k, t * P:(t + 1) * P],
                                   w[:, k, c * HALF:(c + 1) * HALF], start=(k == 0), stop=(k == KD - 1))
                mm.then_inc(mm_done, 1)

        @block.vector
        def _(dve):
            dve.wait_ge(g_in, 32)
            for n in range(2 * NT):
                t, c = n // 2, n % 2
                dve.wait_ge(mm_done, n + 1)
                at = (n % 4) * HALF
                col = slice(c * HALF, (c + 1) * HALF)
                dve.tensor_tensor(tmp[:, c, :], ps[:, at:at + HALF], g_row[:, group_of(t), col],
                                  ALU.mult).then_inc(bank_free, 1)
                dve.wait_ge(bank_free, n + 1)
                dve.tensor_tensor(X[:, t, col], X[:, t, col], tmp[:, c, :], ALU.add
                                  ).then_inc(dve_line, 1)
            dve.wait_ge(dve_line, 2 * NT)


MLH = 8
VN = P + 1
KINDS = 4


def mlstm_inputs(nc, T, ps, HT, ident, QK, VX, O, negM, COLS, KEEP, out_m):
    R = 2 * TOK
    blocks = 2 * MLH
    W2 = 2 * P
    FIRST = 6
    with stage(nc, "in_done", "mm_done", "raw_ready", "abs_done", "e_ready", "ln_done", "x_ready",
               "exp_done", "rows_ready", "dve_line", "turned", "m_out", "w_in0", "w_in1", "used",
               "qk_out", "taps_in", "conv_done", "silu_done", "tok_done", "tok_out") as (
            ctx, (in_done, mm_done, raw_ready, abs_done, e_ready, ln_done, x_ready, exp_done,
                  rows_ready, dve_line, turned, m_out, w_in0, w_in1, used, qk_out, taps_in,
                  conv_done, silu_done, tok_done, tok_out)):
        w_in = (w_in0, w_in1)
        wblk = buf(ctx, nc, "w_block", [P, 2, KD * W2])
        taps = buf(ctx, nc, "conv_taps", [P, blocks, 4])
        cur = buf(ctx, nc, "conv_taps_cur", [P, 4])
        src = buf(ctx, nc, "conv_source", [P, TOK])
        y = buf(ctx, nc, "conv_block", [P, 2, TOK])
        wg = buf(ctx, nc, "gate_w", [P, KD, P])
        gb = buf(ctx, nc, "gate_b", [MLH, 4])
        m0 = buf(ctx, nc, "m_cached", [MLH, 2])
        nat = buf(ctx, nc, "gate_rows", [MLH, KINDS, 2, TOK])
        flat4 = nat[:, :, :, :].rearrange("h k d s -> h (k d s)")
        raw = flat4[:, 0:4 * TOK].rearrange("h (j s) -> h j s", j=4)
        e = flat4[:, 4 * TOK:6 * TOK].rearrange("h (d s) -> h d s", d=2)
        ig = flat4[:, 6 * TOK:8 * TOK].rearrange("h (d s) -> h d s", d=2)
        lf = buf(ctx, nc, "gate_logf", [MLH, 2, TOK])
        b = buf(ctx, nc, "gate_b_sum", [MLH, R])
        w = buf(ctx, nc, "gate_w_row", [MLH, R])
        M = lf[:, :, :].rearrange("h d s -> h (d s)")
        mp = buf(ctx, nc, "m_before", [MLH, 2, NT])
        ML = buf(ctx, nc, "M_last", [MLH, 2, NT])
        mn = buf(ctx, nc, "m_after", [MLH, 2, NT])
        kp = buf(ctx, nc, "state_keep", [MLH, 2 * NT])
        X4 = buf(ctx, nc, "gate_args", [MLH, 3, R])
        keeper = X4[:, 0, :]
        drop = X4[:, 1, :]
        diag = buf(ctx, nc, "keep_diag", [MLH, 2 * NT, MLH])
        ones8 = buf(ctx, nc, "ones8", [MLH, P])
        block = ctx.enter_context(nc.Block())
        chunks = lambda a: a.rearrange("h (c s) -> h c s", s=P)
        LATB, CTXB = (2 * HALF, 4 * HALF), (3 * HALF, 5 * HALF)
        TOKB = (6 * HALF, 7 * HALF)

        @block.sync
        def _(sp):
            for dst, src_ in ((wg, "gate_w"), (gb, "gate_b"), (m0, "ml_m0")):
                sp.dma_start(dst[:], T[src_]).then_inc(in_done, 16)
            for c in range(2):
                sp.dma_start(wblk[:, c, 0:KD * P], T["od_w_qk"][c]).then_inc(w_in[c], 16)
            sp.dma_start(taps[:], T["ml_taps"]).then_inc(taps_in, 16)
            with sp.Fori(1, blocks // 2) as i:
                for c in range(2):
                    sp.wait_ge(used, 2 * i + (c - 1))
                    sp.dma_start(wblk[:, c, 0:KD * P], T["od_w_qk"][2 * i + c]
                                 ).then_inc(w_in[c], 16)
            for n in range(8):
                c = n % 2
                if n < 2:
                    sp.wait_ge(used, blocks - 1 + n)
                else:
                    sp.wait_ge(tok_done, NT * (n - 1))
                sp.dma_start(wblk[:, c, :], T["od_w_vo"][n]).then_inc(w_in[c], 16)
            sp.wait_ge(x_ready, 1)
            sp.dma_start(out_m[0].unsqueeze(1), mn[:, 0, 0:1],
                         allow_slow_non_contiguous=True).then_inc(m_out, 16)
            sp.dma_start(out_m[1].unsqueeze(1), mn[:, 1, NT - 1:NT],
                         allow_slow_non_contiguous=True).then_inc(m_out, 16)
            sp.wait_ge(m_out, 32)

        @block.tensor
        def _(pe):
            pe.wait_ge(in_done, 48)
            for k in range(KD):
                pe.matmul(ps[:, 0:HALF], wg[:, k, :], HT[:, k, 0:HALF],
                          start=(k == 0), stop=(k == KD - 1))
                mm = pe.matmul(ps[:, HALF:TOK], wg[:, k, :], HT[:, k, HALF:TOK],
                               start=(k == 0), stop=(k == KD - 1))
            mm.then_inc(mm_done, 1)

            def channels(c):
                for k in range(KD):
                    lhs = wblk[:, c, k * P:(k + 1) * P]
                    pe.matmul(ps[:, LATB[c]:LATB[c] + LAT], lhs, HT[:, k, CTX:TOK],
                              start=(k == 0), stop=(k == KD - 1))
                    mm = pe.matmul(ps[:, CTXB[c]:CTXB[c] + CTX], lhs, HT[:, k, 0:CTX],
                                   start=(k == 0), stop=(k == KD - 1))
                mm.then_inc(used, 1)

            for c in range(2):
                pe.wait_ge(w_in[c], 16)
                channels(c)
            with pe.Fori(1, blocks // 2) as i:
                for c in range(2):
                    pe.wait_ge(w_in[c], 16 * i + 16)
                    pe.wait_ge(qk_out, 2 * i + (c - 1))
                    channels(c)
            with pe.Fori(0, 4) as i:
                for c in range(2):
                    pe.wait_ge(w_in[c], 16 * i + (16 * blocks // 2 + 16))
                    for t in range(NT):
                        g = c * NT + t
                        pe.wait_ge(tok_out, i * (2 * NT) + (g + 1))
                        at = TOKB[g % 2]
                        for k in range(KD):
                            mm = pe.matmul(ps[:, at:at + W2], HT[:, k, t * P:(t + 1) * P],
                                           wblk[:, c, k * W2:(k + 1) * W2],
                                           start=(k == 0), stop=(k == KD - 1))
                        mm.then_inc(tok_done, 1)
            pe.wait_ge(rows_ready, 1)
            for kind in range(KINDS):
                for d in range(2):
                    for t in range(NT):
                        at = ((kind * 2 + d) * NT + t) * MLH
                        mm = pe.transpose(ps[:, at:at + MLH], nat[:, kind, d, t * P:(t + 1) * P],
                                          ident[0:MLH, 0:MLH])
            mm.then_inc(turned, 1)
            pe.matmul(ps[:, HALF:HALF + 2 * NT * MLH], ones8[:],
                      diag[:, :, :].rearrange("h c g -> h (c g)"), start=True, stop=True
                      ).then_inc(turned, 1)

        @block.scalar
        def _(act):
            act.wait_ge(raw_ready, 1)
            act.sem_inc(tok_out, 2)
            act.activation(e[:], raw[:, 2:4, :], ACT.Abs).then_inc(abs_done, 1)
            act.wait_ge(abs_done, 1)
            act.activation(e[:], e[:], ACT.Exp, scale=-1.0).then_inc(abs_done, 1)
            act.wait_ge(e_ready, 1)
            act.activation(e[:], e[:], ACT.Ln).then_inc(ln_done, 1)

            def drain(i, c):
                act.wait_ge(used, 2 * i + (c + 1))
                act.activation(QK[:, bass.ds(2 * i + c, 1), CTX:TOK],
                               ps[:, LATB[c]:LATB[c] + LAT].unsqueeze(1), ACT.Copy)
                act.activation(QK[:, bass.ds(2 * i + c, 1), 0:CTX],
                               ps[:, CTXB[c]:CTXB[c] + CTX].unsqueeze(1), ACT.Copy
                               ).then_inc(qk_out, 1)

            def silu(n, c):
                act.wait_ge(conv_done, n + 1)
                act.activation(QK[:, bass.ds(n, 1), :], y[:, c, :].unsqueeze(1),
                               ACT.Silu).then_inc(silu_done, 1)

            def values(i, place, silus):
                for g in range(2 * NT):
                    act.wait_ge(tok_done, i * (2 * NT) + (g + 1))
                    act.activation(place(i, g // NT, g % NT),
                                   ps[:, TOKB[g % 2]:TOKB[g % 2] + W2]
                                   .rearrange("p (h v) -> p h v", v=P), ACT.Copy
                                   ).then_inc(tok_out, 1)
                    if silus and g % 3 == 2:
                        n = blocks - FIRST + i * 3 + g // 3
                        silu(n, n % 2)

            with act.Fori(0, FIRST // 2) as i:
                for c in range(2):
                    drain(i, c)
            act.wait_ge(x_ready, 1)
            act.activation(X4[:], X4[:], ACT.Exp).then_inc(exp_done, 1)
            act.activation(kp[:], kp[:], ACT.Exp).then_inc(exp_done, 1)
            with act.Fori(FIRST // 2, blocks // 2) as i:
                for c in range(2):
                    drain(i, c)
                    silu(i * 2 + (c - FIRST), c)
            for i in range(2):
                values(i, lambda i, c, t: VX[:, t, bass.ds(i * 4 + 2 * c, 2), 0:P], True)
            with act.Fori(2, 4) as i:
                values(i, lambda i, c, t: O[:, t, bass.ds(i * (2 * W2) + (c * W2 - 4 * W2), W2)]
                       .rearrange("p (h v) -> p h v", v=P), False)

        @block.vector
        def _(dve):
            line = Line(dve, dve_line)
            one, tt, ts = line.then, dve.tensor_tensor, dve.tensor_scalar
            dve.memset(keeper, 1.0)
            dve.memset(drop, 0.0)
            one(dve.memset(ones8[:], 1.0))
            dve.memset(chunks(keeper)[:, :, 0:1], 0.0)
            one(dve.memset(chunks(drop)[:, :, 0:1], LOWEST))
            dve.wait_ge(in_done, 48)
            dve.wait_ge(mm_done, 1)
            for j in (2, 3, 0, 1):
                ins = ts(raw[:, j, :], ps[32 * j:32 * j + MLH, 0:TOK], gb[:, j:j + 1], None, ALU.add)
            one(ins)
            dve.sem_inc(raw_ready, 1)
            dve.wait_ge(abs_done, 2)
            one(ts(e[:], e[:], 1.0, None, ALU.add))
            dve.sem_inc(e_ready, 1)
            dve.wait_ge(ln_done, 1)
            for d in range(2):
                way = (lambda a: a) if d == 0 else (lambda a: a[:, ::-1])
                dve.scalar_tensor_tensor(out=lf[:, d, :], in0=way(raw[:, 2 + d, :]), scalar=0.0,
                                         in1=way(e[:, d, :]), op0=ALU.min, op1=ALU.subtract)
                ins = dve.tensor_copy(ig[:, d, :], way(raw[:, d, :]))
            one(ins)
            flat = lambda a: a.rearrange("h d s -> h (d s)")
            wide = [MLH, 2 * NT, P]
            one(dve.tensor_tensor_scan(b[:], keeper, flat(lf[:, :, :]), 0.0, ALU.mult, ALU.add))
            one(tt(w[:], flat(ig), b[:], ALU.subtract))
            one(dve.tensor_tensor_scan(M, drop, w[:], LOWEST, ALU.add, ALU.max))
            last = lambda a, c: chunks(a)[:, c, P - 1:P]
            one(dve.memset(mp[:], 0.0))
            dve.tensor_copy(mp[:, 0, 1:2], m0[:, 0:1])
            one(dve.tensor_copy(mp[:, 1, 0:1], m0[:, 1:2]))
            for step in range(NT):
                both = [((0, None), (1, 2), (2, 3), (3, 4), (4, None))[step],
                        ((4, None), (0, 1), (1, 2), (2, 3), (3, None))[step]]
                for d, (c, after) in enumerate(both):
                    ins = tt(ML[:, d, c:c + 1], mp[:, d, c:c + 1], last(M, d * NT + c), ALU.max)
                one(ins)
                for d, (c, after) in enumerate(both):
                    ins = tt(mn[:, d, c:c + 1], ML[:, d, c:c + 1], last(b[:, :], d * NT + c),
                             ALU.add)
                one(ins)
                if both[0][1] is not None:
                    for d, (c, after) in enumerate(both):
                        ins = dve.tensor_copy(mp[:, d, after:after + 1], mn[:, d, c:c + 1])
                    one(ins)
            mpw = flat(mp[:, :, :]).unsqueeze(2).to_broadcast(wide)
            mlw = flat(ML[:, :, :]).unsqueeze(2).to_broadcast(wide)
            tt(chunks(X4[:, 0, :]), chunks(w[:, :]), mlw, ALU.subtract)
            one(tt(chunks(M), chunks(M), mpw, ALU.max))
            tt(chunks(X4[:, 1, :]), mpw, chunks(M), ALU.subtract)
            dve.scalar_tensor_tensor(out=X4[:, 2, :], in0=b[:], scalar=-1.0, in1=M,
                                     op0=ALU.mult, op1=ALU.subtract)
            one(tt(kp[:], flat(mp[:, :, :]), flat(ML[:, :, :]), ALU.subtract))
            dve.sem_inc(x_ready, 1)
            one(ts(M, M, -1.0, None, ALU.mult))
            dve.wait_ge(exp_done, 2)
            rows = [w[:, :]] + [X4[:, j, :] for j in range(3)]
            for d in range(2):
                way = (lambda a: a) if d == 0 else (lambda a: a[:, ::-1])
                for kind, row in enumerate(rows):
                    dve.tensor_copy(nat[:, kind, d, :], way(row[:, d * TOK:(d + 1) * TOK]))
                dve.tensor_copy(negM[:, d, :], way(M[:, d * TOK:(d + 1) * TOK]))
            w8 = [MLH, 2 * NT, MLH]
            one(tt(diag[:], ident[0:MLH, 0:MLH].unsqueeze(1).to_broadcast(w8),
                   kp[:, :].unsqueeze(2).to_broadcast(w8), ALU.mult))
            dve.sem_inc(rows_ready, 1)
            dve.wait_ge(taps_in, 16)
            dve.sem_inc(silu_done, 2)
            with line.loop(0, blocks // 2, 8) as i:
                for c in range(2):
                    dve.wait_ge(qk_out, i * 2 + (c + 1))
                    dve.tensor_copy(src[:, :].unsqueeze(1), QK[:, bass.ds(i * 2 + c, 1), :])
                    line.then(dve.tensor_copy(cur[:, :].unsqueeze(1),
                                              taps[:, bass.ds(i * 2 + c, 1), :]))
                    dve.wait_ge(silu_done, i * 2 + (c + 1))
                    short_conv(dve, line, y[:, c, :], src[:, :], lambda k: cur[:, k:k + 1])
                    dve.sem_inc(conv_done, 1)
            dve.wait_ge(turned, 2)
            one(dve.tensor_copy(COLS[:, :, :].rearrange("p c h -> p (c h)"),
                                ps[:, 0:KINDS * 2 * NT * MLH]))
            one(dve.tensor_copy(KEEP[:, :, :].rearrange("p c h -> p (c h)"),
                                ps[:, HALF:HALF + 2 * NT * MLH]))


def turn_keys(nc, ps, QK, KT, ident):
    with stage(nc, "turned", "out_done") as (ctx, (turned, out_done)):
        block = ctx.enter_context(nc.Block())

        @block.tensor
        def _(pe):
            for n in range(2 * NT):
                t, q = n // 2, n % 2
                if n >= 4:
                    pe.wait_ge(out_done, n - 3)
                for h in range(4):
                    at = (n % 4) * HALF + h * P
                    mm = pe.transpose(ps[:, at:at + P], QK[:, MLH + 4 * q + h, t * P:(t + 1) * P],
                                      ident[:])
                mm.then_inc(turned, 1)

        @block.scalar
        def _(act):
            for n in range(2 * NT):
                t, q = n // 2, n % 2
                act.wait_ge(turned, n + 1)
                at = (n % 4) * HALF
                act.activation(KT[:, t, 4 * q:4 * q + 4, :], ps[:, at:at + HALF]
                               .rearrange("p (h v) -> p h v", v=P), ACT.Copy).then_inc(out_done, 1)


def mlstm_cells(nc, T, ps, QK, KT, VX, HM, negM, COLS, KEEP, ident, out_C, out_n):
    with stage(nc, "cn_in", "v_ones", "mask_line", "mask_done", "pair_set", "pair_copied",
               "scores_done", "exp_done", "kw_set", "added_done", "share_done", "share_out",
               "st_done", "chunk_done", "state_set", "tail_done", "dve_line", "state_out") as (
            ctx, (cn_in, v_ones, mask_line, mask_done, pair_set, pair_copied, scores_done,
                  exp_done, kw_set, added_done, share_done, share_out, st_done, chunk_done,
                  state_set, tail_done,
                  dve_line, state_out)):
        CN0 = buf(ctx, nc, "state_cached", [P, 2, MLH, VN])
        CNo = buf(ctx, nc, "state_ctx", [P, 2, MLH, VN])
        CN = buf(ctx, nc, "state", [P, 2, 2, VN])
        CNk = buf(ctx, nc, "state_kept", [P, 2, 2, VN])
        mask = buf(ctx, nc, "mask", [P, 2, P])
        pick = buf(ctx, nc, "head_pick", [MLH, 2, P])
        q = buf(ctx, nc, "q_heads", [P, 2, TOK])
        k = buf(ctx, nc, "k_heads", [P, 2, TOK])
        cols = buf(ctx, nc, "cols_heads", [P, KINDS * 2 * NT, 2])
        keep = buf(ctx, nc, "keep_heads", [P, 2 * NT, 2])
        E = buf(ctx, nc, "weights", [P, 2, 2, P])
        ST = buf(ctx, nc, "scores_T", [P, 2, 2, P])
        kw = buf(ctx, nc, "k_weighted", [P, 2, 2, P])
        share = buf(ctx, nc, "state_share", [P, 2, 2, 2, VN])
        nd = buf(ctx, nc, "num_den", [P, 2, 2, VN])
        den = buf(ctx, nc, "den", [P, 2, 2, 1])
        block = ctx.enter_context(nc.Block())
        pairs = MLH // 2
        es = ps[:, 0:2 * HALF].rearrange("p (d h e n) -> p d h e n", d=2, h=2, e=2)

        def units(bank):
            return (ps[:, bank * HALF:(bank + 2) * HALF].rearrange("p (d n) -> p d n", d=2)
                    [:, :, 0:2 * VN].rearrange("p d (h n) -> p d h n", h=2))
        shared, added, chunk = units(2), units(4), units(6)

        def tiles(i):
            return i, (NT - i) % NT

        def col(kind, i):
            a, z = (kind * 2 * NT + d * NT + t for d, t in enumerate(tiles(i)))
            return cols[:, a:z + 1:z - a, :]

        @block.sync
        def _(sp):
            sp.dma_start(CN0[:], T["ml_CN0"]).then_inc(cn_in, 16)
            sp.wait_ge(tail_done, pairs * NT + 1)
            for d in range(2):
                sp.dma_start(out_C[d].rearrange("h k v -> k h v"), CNo[:, d, :, 0:P]
                             ).then_inc(state_out, 16)
                sp.dma_start(out_n[d].rearrange("h k -> k h").unsqueeze(2), CNo[:, d, :, P:VN],
                             allow_slow_non_contiguous=True).then_inc(state_out, 16)
            sp.wait_ge(state_out, 64)

        @block.gpsimd
        def _(pool):
            pool.memset(VX[:, :, :, P:VN], 1.0).then_inc(v_ones, 1)
            pool.memset(mask[:], 0.0).then_inc(mask_line, 1)
            pool.wait_ge(mask_line, 1)
            for d, way in ((0, 1), (1, -1)):
                pool.affine_select(out=mask[:, d, :], in_=mask[:, d, :], compare_op=ALU.is_ge,
                                   fill=-1.0e30, base=0, pattern=[[way, P]],
                                   channel_multiplier=-way).then_inc(mask_done, 1)
            pool.wait_ge(mask_done, 2)
            pool.wait_ge(v_ones, 1)

        @block.scalar
        def _(act):
            with act.Fori(0, pairs) as p:
                act.wait_ge(chunk_done, p * NT + 1)
                act.activation(q[:], QK[:, bass.ds(p * 2, 2), :], ACT.Copy, scale=float(P) ** -0.5)
                act.activation(k[:], QK[:, bass.ds(p * 2 + MLH, 2), :], ACT.Copy
                               ).then_inc(pair_copied, 1)
                act.wait_ge(pair_set, p + 1)
                for i in range(NT):
                    act.wait_ge(scores_done, p * NT + (i + 1))
                    for d in range(2):
                        for h in range(2):
                            ins = act.activation(E[:, d, h, :], es[:, d, h, 0, :], ACT.Exp,
                                                 bias=col(0, i)[:, d, h:h + 1])
                    ins.then_inc(exp_done, 1)
                    act.wait_ge(share_done, p * NT + (i + 1))
                    act.wait_ge(tail_done, p * NT + max(i, 1))
                    for d in range(2):
                        for h in range(2):
                            ins = act.activation(share[:, i % 2, d, h, :], shared[:, d, h, :],
                                                 ACT.Copy, scale=col(2, i)[:, d, h:h + 1])
                    ins.then_inc(share_out, 1)

        @block.tensor
        def _(pe):
            pe.wait_ge(mask_done, 2)
            pe.wait_ge(v_ones, 1)

            def scores(i):
                for d, t in enumerate(tiles(i)):
                    tile = slice(t * P, (t + 1) * P)
                    for h in range(2):
                        pe.matmul(es[:, d, h, 0, :], ident[:], mask[:, d, :],
                                  start=True, stop=False)
                        pe.matmul(es[:, d, h, 0, :], pick[:, h, :], negM[:, d, tile],
                                  start=False, stop=True)
                        mm = pe.matmul(es[:, d, h, 1, :], k[:, h, tile], q[:, h, tile],
                                       start=True, stop=True)
                mm.then_inc(scores_done, 1)

            with pe.Fori(0, pairs) as p:
                pe.wait_ge(pair_set, p + 1)
                pe.wait_ge(pair_copied, p + 1)
                scores(0)
                for i in range(NT):
                    for out, lhs in ((added, kw), (chunk, ST)):
                        if out is added:
                            pe.wait_ge(kw_set, p * NT + (i + 1))
                            pe.wait_ge(state_set, p * (NT + 1) + (i + 1))
                        else:
                            pe.wait_ge(st_done, p * NT + (i + 1))
                        for d, t in enumerate(tiles(i)):
                            for h in range(2):
                                v = VX[:, t, bass.ds(p * 2 + h, 1), :].rearrange("p h n -> p (h n)")
                                mm = pe.matmul(out[:, d, h, :], lhs[:, d, h, :], v,
                                               start=True, stop=True)
                        if out is added:
                            mm.then_inc(added_done, 1)
                            pe.wait_ge(share_out, p * NT + (i + 1))
                            for d, t in enumerate(tiles(i)):
                                for h in range(2):
                                    mm = pe.matmul(shared[:, d, h, :], q[:, h, t * P:(t + 1) * P],
                                                   CN[:, d, h, :], start=True, stop=True)
                            mm.then_inc(share_done, 1)
                    mm.then_inc(chunk_done, 1)
                    if i < NT - 1:
                        scores(i + 1)

        @block.vector
        def _(dve):
            line = Line(dve, dve_line)
            one, tt, ts = line.then, dve.tensor_tensor, dve.tensor_scalar
            full = [P, 2, 2, VN]
            dve.wait_ge(cn_in, 16)
            for free in (chunk_done, share_out, tail_done):
                dve.sem_inc(free, 1)

            def weigh_keys(p, i):
                for d, t in enumerate(tiles(i)):
                    ins = tt(kw[:, d], KT[:, t, bass.ds(p * 2, 2), :],
                             col(1, i)[:, d, :].unsqueeze(2).to_broadcast([P, 2, P]), ALU.mult)
                ins.then_inc(kw_set, 1)

            with line.loop(0, pairs, 7 * NT + 1) as p:
                dve.tensor_copy(pick[:], ident[0:MLH, bass.ds(p * 2, 2)].unsqueeze(2)
                                .to_broadcast([MLH, 2, P]))
                dve.tensor_copy(cols[:], COLS[:, :, bass.ds(p * 2, 2)])
                dve.tensor_copy(keep[:], KEEP[:, :, bass.ds(p * 2, 2)])
                one(dve.memset(CN[:], 0.0))
                dve.sem_inc(pair_set, 1)
                dve.sem_inc(state_set, 1)
                weigh_keys(p, 0)
                for i in range(NT):
                    a, z = i, NT + (NT - 1 - tiles(i)[1])
                    kept = keep[:, a:z + 1:z - a, :].unsqueeze(3).to_broadcast(full)
                    dve.wait_ge(state_set, p * (NT + 1) + (i + 1))
                    line.count(tt(CNk[:], CN[:], kept, ALU.mult))
                    dve.wait_ge(exp_done, p * NT + (i + 1))
                    tt(ST[:], es[:, :, :, 1, :], E[:], ALU.mult).then_inc(st_done, 1)
                    line.settle()
                    dve.wait_ge(added_done, p * NT + (i + 1))
                    dve.wait_ge(share_done, p * NT + (i + 1))
                    if i == 0:
                        tt(CNo[:, :, bass.ds(p * 2, 2), :], CNk[:], added, ALU.add)
                        ins = dve.tensor_copy(CN[:], CN0[:, :, bass.ds(p * 2, 2), :])
                    else:
                        ins = tt(CN[:], CNk[:], added, ALU.add)
                    ins.then_inc(state_set, 1)
                    if i < NT - 1:
                        weigh_keys(p, i + 1)
                    dve.wait_ge(chunk_done, p * NT + (i + 2))
                    dve.wait_ge(share_out, p * NT + (i + 2))
                    one(tt(nd[:], share[:, i % 2], chunk, ALU.add))
                    n_dot = nd[:, :, :, P:VN]
                    one(dve.scalar_tensor_tensor(out=den[:], in0=n_dot, scalar=-1.0, in1=n_dot,
                                                 op0=ALU.mult, op1=ALU.max))
                    one(tt(den[:], den[:], col(3, i).unsqueeze(3), ALU.max))
                    one(dve.reciprocal(den[:], den[:]))
                    for d, t in enumerate(tiles(i)):
                        out = HM[:, t, bass.ds(p * 2, 2), :]
                        row = nd[:, d, :, 0:P]
                        by = den[:, d].to_broadcast([P, 2, P])
                        if (d, t) in ((0, 0), (0, 1), (0, 2), (1, 4), (1, 3)):
                            ins = tt(out, row, by, ALU.mult)
                        else:
                            one(tt(row, row, by, ALU.mult))
                            ins = tt(out, row, out, ALU.add)
                    one(ins)
                    dve.sem_inc(tail_done, 1)


def mlstm_finish(nc, T, ps, HM, O, MIXT, ident, w_out, w_out_in):
    with stage(nc, "g_in", "silu_done", "ms_ready", "rooted", "dve_line", "h_ready", "turned",
               "out_done") as (ctx, (g_in, silu_done, ms_ready, rooted, dve_line, h_ready, turned,
                                     out_done)):
        g = buf(ctx, nc, "norm_row", [P, D])
        sq = buf(ctx, nc, "squares", [P, MLH, P])
        ms = buf(ctx, nc, "mean_square", [P, NT, MLH])
        block = ctx.enter_context(nc.Block())

        @block.sync
        def _(sp):
            sp.dma_start(g[:], T["ml_norm_g"].partition_broadcast(P)).then_inc(g_in, 16)
            sp.dma_start(w_out[:], T["od_w_out"]).then_inc(w_out_in, 16)

        @block.scalar
        def _(act):
            for t in range(NT):
                act.activation(O[:, t, :], O[:, t, :], ACT.Silu).then_inc(silu_done, 1)
            act.wait_ge(ms_ready, 1)
            act.activation(ms[:], ms[:], ACT.Sqrt).then_inc(rooted, 1)
            for n in range(2 * NT):
                t, q = n // 2, n % 2
                act.wait_ge(turned, n + 1)
                at = (n % 4) * HALF
                act.activation(MIXT[:, 4 * q:4 * q + 4, t * P:(t + 1) * P], ps[:, at:at + HALF]
                               .rearrange("p (k c) -> p k c", k=4), ACT.Copy).then_inc(out_done, 1)

        @block.vector
        def _(dve):
            line = Line(dve, dve_line)
            one, tt = line.then, dve.tensor_tensor
            for t in range(NT):
                one(tt(sq[:], HM[:, t], HM[:, t], ALU.mult))
                one(dve.tensor_reduce(ms[:, t, :], sq[:], AX.X, ALU.add))
            one(dve.tensor_scalar(ms[:], ms[:], 1.0 / P, EPS, ALU.mult, ALU.add))
            dve.reciprocal(ms[:], ms[:]).then_inc(ms_ready, 1)
            dve.wait_ge(rooted, 1)
            dve.wait_ge(g_in, 16)
            dve.wait_ge(silu_done, NT)
            for t in range(NT):
                flat = HM[:, t].rearrange("p h v -> p (h v)")
                one(tt(HM[:, t], HM[:, t], ms[:, t, :].unsqueeze(2).to_broadcast([P, MLH, P]),
                       ALU.mult))
                one(tt(flat, flat, g[:], ALU.mult))
                tt(flat, flat, O[:, t, :], ALU.mult).then_inc(h_ready, 1)

        @block.tensor
        def _(pe):
            for n in range(2 * NT):
                t, q = n // 2, n % 2
                pe.wait_ge(h_ready, t + 1)
                if n >= 4:
                    pe.wait_ge(out_done, n - 3)
                for k in range(4):
                    at = (n % 4) * HALF + k * P
                    mm = pe.transpose(ps[:, at:at + P], HM[:, t, 4 * q + k, :], ident[:])
                mm.then_inc(turned, 1)


def finish(nc, T, X, out):
    with stage(nc, "g_in", "squared", "ms_ready", "rooted", "y_ready", "dve_line", "y_out") as (
            ctx, (g_in, squared, ms_ready, rooted, y_ready, dve_line, y_out)):
        g = buf(ctx, nc, "final_row", [P, D])
        junk = buf(ctx, nc, "squares", [P, D])
        ms = buf(ctx, nc, "mean_square", [P, NT])
        block = ctx.enter_context(nc.Block())

        @block.sync
        def _(sp):
            sp.dma_start(g[:], T["final_g"].partition_broadcast(P)).then_inc(g_in, 16)
            for t in range(NT):
                sp.wait_ge(y_ready, t + 1)
                sp.dma_start(out[t * P:(t + 1) * P, :], X[:, t, :]).then_inc(y_out, 16)
            sp.wait_ge(y_out, 16 * NT)

        @block.scalar
        def _(act):
            for t in range(NT):
                act.activation(junk[:], X[:, t, :], ACT.Square,
                               accum_out=ms[:, t:t + 1]).then_inc(squared, 1)
                act.wait_ge(squared, t + 1)
            act.wait_ge(ms_ready, 1)
            act.activation(ms[:], ms[:], ACT.Sqrt).then_inc(rooted, 1)

        @block.vector
        def _(dve):
            line = Line(dve, dve_line)
            dve.wait_ge(squared, NT)
            line.then(dve.tensor_scalar(ms[:], ms[:], 1.0 / D, EPS, ALU.mult, ALU.add))
            dve.reciprocal(ms[:], ms[:]).then_inc(ms_ready, 1)
            dve.wait_ge(rooted, 1)
            dve.wait_ge(g_in, 16)
            for t in range(NT):
                dve.scalar_tensor_tensor(out=X[:, t, :], in0=X[:, t, :], scalar=ms[:, t:t + 1],
                                         in1=g[:], op0=ALU.mult, op1=ALU.mult).then_inc(y_ready, 1)




def trunk(nc, T, O):
    mod = nc.dram_tensor("mod_rows_dram", [2, MOD], F32, kind="Internal").ap()
    with ExitStack() as ctx:
        ps = ctx.enter_context(nc.psum_tensor("banks", [P, 8 * HALF], F32))
        X = buf(ctx, nc, "X", [P, NT, D])
        ident = buf(ctx, nc, "ident", [P, P])
        cond_s = buf(ctx, nc, "cond_s", [P, KD, 2])

        def peer(layer):
            with ExitStack() as c1:
                H = buf(c1, nc, "H", [P, NT, D])
                HT = buf(c1, nc, "HT", [P, KD, TOK])
                experts(nc, T, ps, HT, H, X, mod, ident, layer)

        with ExitStack() as c1:
            MIXT = buf(c1, nc, "MIXT", [P, KD, TOK])
            US = buf(c1, nc, "US", [P, 4, TOK])
            with ExitStack() as c0:
                KC = buf(c0, nc, "KC", [P, NT, 2, HYW])
                KS = buf(c0, nc, "KS", [P, NT, 2, HYW])
                start(nc, T, ps, X, ident, cond_s, mod, KC, KS,
                      MIXT[:, :, :].rearrange("p k t -> p (k t)"))
                VG = buf(c0, nc, "VG", [P, NT, 3 * HYW])
                mats = [buf(c0, nc, n, [P, DFT]) for n in ("cos_fwd", "sin_fwd", "cos_inv", "sin_inv")]
                bias = buf(c0, nc, "hy_bias", [P, 2, HYW])
                mats_in = c0.enter_context(carried(nc, "mats_in"))
                with ExitStack() as c2:
                    HT = buf(c2, nc, "HT", [P, KD, TOK])
                    H = MIXT[:, :, :].rearrange("p k t -> p (k t)").rearrange("p (t d) -> p t d", d=D)
                    norm_modulate(nc, ps, X, H, HT, ident, mod, T["norm_g"][0, 0], 0, 0, 1)
                    even_inputs(nc, T, ps, HT, VG, US, ident, mats, bias, mats_in)
                hyena_convolve(nc, ps, VG, KC, KS, MIXT, ident, mats, bias, mats_in)
            G = buf(c1, nc, "G", [P, 4, TOK])
            s5(nc, T, ps, US, G, ident, O["s5_re"], O["s5_im"], cond_s, mod)
            w_out = buf(c1, nc, "w_out", [P, KD, D])
            with carried(nc, "w_out_in") as w_out_in:
                s5_gate(nc, T, ps, G, MIXT, w_out, w_out_in)
                project_out(nc, ps, MIXT, w_out, w_out_in, X, mod, 0, 2)
        peer(0)
        with ExitStack() as c1:
            negM = buf(c1, nc, "negM", [MLH, 2, TOK])
            COLS = buf(c1, nc, "COLS", [P, KINDS * 2 * NT, MLH])
            KEEP = buf(c1, nc, "KEEP", [P, 2 * NT, MLH])
            with ExitStack() as c2:
                HT = c2.enter_context(nc.sbuf_tensor(numbered("HT"), [P, KD, TOK], F32,
                                                     side="right"))
                with ExitStack() as c3:
                    H = buf(c3, nc, "H", [P, NT, D])
                    norm_modulate(nc, ps, X, H, HT, ident, mod, T["norm_g"][1, 0], 1, 0, 1)
                QK = buf(c1, nc, "QK", [P, 2 * MLH, TOK])
                VX = buf(c1, nc, "VX", [P, NT, MLH, VN])
                O_ = buf(c1, nc, "Ogate", [P, NT, D])
                mlstm_inputs(nc, T, ps, HT, ident, QK, VX, O_, negM, COLS, KEEP, O["ml_m"])
            with ExitStack() as c2:
                HM = buf(c2, nc, "HM", [P, NT, MLH, P])
                with ExitStack() as c3:
                    KT = buf(c3, nc, "KT", [P, NT, MLH, P])
                    turn_keys(nc, ps, QK, KT, ident)
                    mlstm_cells(nc, T, ps, QK, KT, VX, HM, negM, COLS, KEEP, ident, O["ml_C"],
                                O["ml_n"])
                MIXT = buf(c2, nc, "MIXT", [P, KD, TOK])
                w_out = buf(c2, nc, "w_out", [P, KD, D])
                with carried(nc, "w_out_in") as w_out_in:
                    mlstm_finish(nc, T, ps, HM, O_, MIXT, ident, w_out, w_out_in)
                    project_out(nc, ps, MIXT, w_out, w_out_in, X, mod, 1, 2)
        peer(1)
        finish(nc, T, X, O["y"])


OUTS = {"y": [TOK, D], "s5_re": [2, 32, 64], "s5_im": [2, 32, 64], "ml_C": [2, 8, P, P],
        "ml_n": [2, 8, P], "ml_m": [2, 8]}


def host_arrays(inp):
    f = np.float32

    def slices(w, width):
        n = w.shape[1] // width
        return np.ascontiguousarray(w.reshape(KD, P, n, width).transpose(2, 1, 0, 3)).reshape(n, P, KD * width)

    a = {}
    a["cond"] = np.stack([inp["c_ctx"], inp["c"][0]], -1).reshape(KD, P, 2).transpose(1, 0, 2)
    ada = np.concatenate(list(inp["ada_w"]), 1)
    a["ada_first"], a["ada_rest"] = slices(ada[:, :MOD_FIRST], HALF), slices(ada[:, MOD_FIRST:], MOD_W)
    a["ada_b"] = inp["ada_b"].reshape(1, -1)
    a["x"] = np.concatenate([inp["x_prompt"][0], inp["x_sample"][0]]).reshape(NT, P, D).transpose(1, 0, 2)
    a["norm_g"] = inp["norm_g"]
    a["ev_w_in"] = slices(inp["ev_w_in"][0], P)
    quarter = D // 4
    omega = (1.0 / (f(10000.0) ** (np.arange(quarter, dtype=f) / f(quarter)))).astype(f)

    def emb(n):
        ang = np.arange(n, dtype=f)[:, None] * omega[None]
        return np.concatenate([np.sin(ang), np.cos(ang)], -1)
    er, ec = emb(LAT // 64), emb(64)
    pe = np.concatenate([np.repeat(er, 64, 0), np.tile(ec, (LAT // 64, 1))], -1)
    a["pos"] = pe.reshape(NT - 1, P, D).transpose(1, 0, 2)
    feats, times = [], np.ones((2, NT, P), f)
    for g, n in ((0, CTX), (1, LAT)):
        t = np.arange(n, dtype=f) / f(n)
        bands = np.linspace(1e-4, 15, 16, dtype=f)
        ang = f(2.0 * math.pi) * t[:, None] * bands[None]
        feats.append(np.concatenate([t[:, None], np.cos(ang), np.sin(ang)], -1))
        times[0, g:g + 1 + 3 * g] = -t.reshape(-1, P)
        times[1, g, 0] = 0.0
        w = (2 * np.arange(n)[None] + 1) * np.arange(n)[:, None] % (4 * n) * (math.pi / (2 * n))
        for name, m in (("cos", np.cos(w)), ("sin", np.sin(w))):
            for way, mat in (("fwd", m), ("inv", m.T / n)):
                part = mat.reshape(n // P, P, n).transpose(1, 0, 2).reshape(P, -1).astype(f)
                a[f"{name}_{way}"] = np.concatenate([a[f"{name}_{way}"], part], 1) if g else part
    a["hy_z"] = np.concatenate(feats).T
    a["hy_times"] = times.transpose(2, 0, 1)
    a["hy_w1"], a["hy_w2"], a["hy_w3"] = inp["hy_w1"][0], inp["hy_w2"][0], inp["hy_w3"][0]
    a["hy_cols"] = np.stack([inp["hy_b1"][0], inp["hy_b2"][0], inp["hy_freq"][0]], -1)
    a["hy_decay"], a["hy_bias"] = inp["hy_decay"][0], inp["hy_bias"][0]

    def taps(w, b):
        return np.concatenate([w, b[None]]).reshape(4, -1, P).transpose(2, 1, 0)
    a["hy_taps"] = taps(inp["hy_conv_w"][0], inp["hy_conv_b"][0])
    def states(v):
        v = v.reshape(2, PAIRS, 2, 64, *v.shape[3:])
        return np.moveaxis(v, (2, 3), (0, 1)).reshape(P, 2 * PAIRS, *v.shape[4:])
    step = np.broadcast_to(inp["s5_log_step"][0][:, :, None], (2, 32, 64))
    a["s5_par"] = np.stack([states(v) for v in (
        inp["s5_a_re"][0], inp["s5_a_im"][0], step, inp["state_s5_re"][0, 0],
        inp["state_s5_im"][0, 0])], 1)
    a["s5_B"] = np.stack([states(inp["s5_b_re"][0]), states(inp["s5_b_im"][0])], 1)
    a["s5_C"] = np.stack([states(inp[n][0].transpose(0, 1, 3, 2)) for n in ("s5_c_re", "s5_c_im")], 1)
    a["s5_d"] = inp["s5_d"][0].reshape(4, P).T
    ctx_steps, lat_steps = np.arange(1, CTX + 1, dtype=f), np.arange(1, LAT + 1, dtype=f)
    a["s5_steps"] = np.stack([np.concatenate([ctx_steps, lat_steps]),
                              np.concatenate([lat_steps, ctx_steps])])
    a["glu_w"] = inp["s5_glu_w"][0].reshape(4, P, 512).transpose(1, 0, 2)
    a["glu_b"] = inp["s5_glu_b"][0].reshape(4, P).T
    a["ev_w_out"] = inp["ev_w_out"][0].reshape(KD, P, D).transpose(1, 0, 2)
    w = inp["od_w_in"][0]
    a["od_w_qk"], a["od_w_vo"] = slices(w[:, 0:2 * D], P), slices(w[:, 2 * D:4 * D], 2 * P)
    a["gate_w"] = np.zeros((P, KD, 4, 32), f)
    a["gate_w"][:, :, :, 0:MLH] = w[:, 4 * D:].reshape(KD, P, 4, MLH).transpose(1, 0, 2, 3)
    a["gate_w"] = a["gate_w"].reshape(P, KD, P)
    a["gate_b"], a["ml_m0"] = inp["od_gate_b"][0].T, inp["state_mlstm_m"][0, 0].T
    a["ml_taps"] = taps(inp["ml_conv_w"][0], inp["ml_conv_b"][0])
    a["ml_CN0"] = np.concatenate([inp["state_mlstm_C"][0, 0], inp["state_mlstm_n"][0, 0][..., None]],
                                 -1).transpose(2, 0, 1, 3)
    a["ml_norm_g"], a["final_g"] = inp["ml_norm_g"][0], inp["final_g"]
    a["od_w_out"] = inp["od_w_out"][0].reshape(KD, P, D).transpose(1, 0, 2)
    for l in range(2):
        a[f"pk_w_q{l}"] = slices(inp["pk_w_q"][l], P)
        a[f"pk_u{l}"], a[f"pk_v{l}"] = inp["pk_u"][l], inp["pk_v"][l]
    a["pk_keys"] = inp["pk_keys"].transpose(0, 4, 1, 2, 3).reshape(2, P, CODES, P)
    return {k: np.ascontiguousarray(v, dtype=v.dtype) for k, v in a.items()}


def kernel(**inputs):
    import concourse.bacc as bacc
    from concourse.bass_utils import run_bass_kernel_spmd as run

    USED.clear()
    arrays = {f"in_{n}_dram": a for n, a in host_arrays(inputs).items()}
    nc = bacc.Bacc("TRN2", target_bir_lowering=False, num_devices=1)
    T = {n[3:-5]: nc.dram_tensor(n, a.shape, mybir.dt.from_np(a.dtype), kind="ExternalInput").ap()
         for n, a in arrays.items()}
    O = {n: nc.dram_tensor(f"out_{n}_dram", shape, F32, kind="ExternalOutput").ap()
         for n, shape in OUTS.items()}
    trunk(nc, T, O)
    r = run(nc, [arrays], core_ids=[0]).results[0]
    y, re, im, C, n, m = (r[f"out_{k}_dram"] for k in OUTS)
    return (y[None, :CTX], y[None, CTX:], re[None, None], im[None, None], C[None, None],
            n[None, None], m[None, None])
```
